# Optimizing a Trainium2 kernel written in Bass

```python
import jax, jax.numpy as jnp
from jax import lax
import numpy as np

D_MODEL = 1024
BATCH = 1
SEQ = 256
DEPTH = 2

GRID_W = 64
CTX_LEN = 256
CONV_DIM = 512
MLSTM_DIM = D_MODEL - CONV_DIM
MLSTM_HEADS = 4
MLSTM_HEAD_DIM = MLSTM_DIM // MLSTM_HEADS
CHUNK = 128
D_FF = 2816
N_EXPERTS = 8
TOP_K = 2
ROUTE_BLOCK = 256
N_DENSE = (DEPTH + 1) // 2
N_MOE = DEPTH // 2
EPS = 1e-6
Q0 = 3 * CONV_DIM
O0 = Q0 + 3 * MLSTM_DIM + 4 * MLSTM_HEADS
P_IN = O0 + MLSTM_DIM

kernel_name = "hybrid_conv_mlstm_prefix_dit"

def rmsnorm(x, g):
    xf = x.astype(jnp.float32)
    y = xf * lax.rsqrt(jnp.mean(xf * xf, axis=-1, keepdims=True) + EPS)
    return (y * g.astype(jnp.float32)).astype(x.dtype)

def modulate(u, shift, scale):
    return u * (1 + scale) + shift

def conv3(z, w):
    L = z.shape[-2]
    zp = jnp.pad(z, [(0, 0)] * (z.ndim - 2) + [(1, 1), (0, 0)])
    return zp[..., :L, :] * w[0] + zp[..., 1:L + 1, :] * w[1] + zp[..., 2:, :] * w[2]

def short_conv_mixer(u, w_cols, cw, rows):
    b, t, _ = u.shape
    gb, gc, hh = jnp.split(u @ w_cols, 3, axis=-1)
    y = gc * hh
    if rows is None:
        y = conv3(y, cw)
    else:
        y = conv3(y.reshape(b, rows, GRID_W, CONV_DIM), cw).reshape(b, t, CONV_DIM)
    return gb * y

def to_heads(z):
    b, t, _ = z.shape
    return z.reshape(b, t, MLSTM_HEADS, MLSTM_HEAD_DIM).transpose(0, 2, 1, 3).astype(jnp.float32)

def mlstm_inputs(u, w_cols, bg):
    b, t, _ = u.shape
    q, k, v, g = jnp.split(u @ w_cols, [MLSTM_DIM, 2 * MLSTM_DIM, 3 * MLSTM_DIM], axis=-1)
    g = (g.reshape(b, t, 4, MLSTM_HEADS) + bg).astype(jnp.float32).transpose(0, 2, 3, 1)
    return to_heads(q), to_heads(k) * (MLSTM_HEAD_DIM ** -0.5), to_heads(v), g

def mlstm_scan(q, k, v, log_i, log_f, state, return_h):
    b, h, t, d = q.shape
    nc = t // CHUNK
    lower = jnp.tril(jnp.ones((CHUNK, CHUNK), dtype=bool))

    def blocks(a):
        return jnp.moveaxis(a.reshape((b, h, nc, CHUNK) + a.shape[3:]), 2, 0)

    def step(carry, xs):
        C, n, m = carry
        qc, kc, vc, ic, fc = xs
        bcum = jnp.cumsum(fc, axis=-1)
        bL = bcum[..., -1]
        w_end = bL[..., None] - bcum + ic
        m_new = jnp.maximum(bL + m, jnp.max(w_end, axis=-1))
        dec = jnp.exp(bL + m - m_new)
        wk = jnp.exp(w_end - m_new[..., None])
        C_new = dec[..., None, None] * C + jnp.einsum('bhl,bhld,bhle->bhde', wk, kc, vc)
        n_new = dec[..., None] * n + jnp.einsum('bhl,bhld->bhd', wk, kc)
        if not return_h:
            return (C_new, n_new, m_new), None
        dmat = bcum[..., :, None] - bcum[..., None, :] + ic[..., None, :]
        dmat = jnp.where(lower, dmat, -jnp.inf)
        inter = bcum + m[..., None]
        m_t = jnp.maximum(inter, jnp.max(dmat, axis=-1))
        s = jnp.einsum('bhtd,bhsd->bhts', qc, kc) * jnp.exp(dmat - m_t[..., None])
        w_int = jnp.exp(inter - m_t)
        num = jnp.einsum('bhts,bhsd->bhtd', s, vc) + w_int[..., None] * jnp.einsum('bhtd,bhde->bhte', qc, C)
        den = jnp.sum(s, axis=-1) + w_int * jnp.einsum('bhtd,bhd->bht', qc, n)
        hout = num / jnp.maximum(jnp.abs(den), jnp.exp(-m_t))[..., None]
        return (C_new, n_new, m_new), hout

    state, hs = lax.scan(step, state, (blocks(q), blocks(k), blocks(v), blocks(log_i), blocks(log_f)))
    if return_h:
        hs = jnp.moveaxis(hs, 0, 2).reshape(b, h, t, d)
    return state, hs

def mlstm_bidirectional(lat, ctxs, need_ctx):
    q, k, v, g = lat
    qc, kc, vc, gc = ctxs
    b, h, _, d = q.shape
    out_lat, out_ctx = None, None
    for direction in range(2):
        rev = direction == 1
        orient = (lambda a: jnp.flip(a, axis=2)) if rev else (lambda a: a)
        state0 = (jnp.zeros((b, h, d, d), jnp.float32), jnp.zeros((b, h, d), jnp.float32),
                  jnp.zeros((b, h), jnp.float32))
        st, hc = mlstm_scan(orient(qc), orient(kc), orient(vc), orient(gc[:, 2 * direction]),
                            orient(jax.nn.log_sigmoid(gc[:, 2 * direction + 1])), state0, need_ctx)
        _, hl = mlstm_scan(orient(q), orient(k), orient(v), orient(g[:, 2 * direction]),
                           orient(jax.nn.log_sigmoid(g[:, 2 * direction + 1])), st, True)
        out_lat = orient(hl) if out_lat is None else out_lat + orient(hl)
        if need_ctx:
            out_ctx = orient(hc) if out_ctx is None else out_ctx + orient(hc)
    return out_lat, out_ctx

def mlstm_merge(hh, g_norm, o):
    hn = hh * lax.rsqrt(jnp.mean(hh * hh, axis=-1, keepdims=True) + EPS)
    b, _, t, _ = hn.shape
    hn = hn.transpose(0, 2, 1, 3).reshape(b, t, MLSTM_DIM) * g_norm.astype(jnp.float32)
    return hn.astype(o.dtype) * o

def swiglu(u, w1, w3, w2):
    return (jax.nn.silu(u @ w1) * (u @ w3)) @ w2

def moe_swiglu(xf, router, w1, w3, w2):
    n, dm = xf.shape
    logits = xf.astype(jnp.float32) @ router.astype(jnp.float32)
    top_v, top_i = lax.top_k(logits, TOP_K)
    gates = jax.nn.softmax(top_v, axis=-1).astype(xf.dtype)
    a = n * TOP_K
    flat_e = top_i.reshape(-1)
    flat_t = jnp.repeat(jnp.arange(n, dtype=jnp.int32), TOP_K)
    flat_g = gates.reshape(-1)
    order = jnp.argsort(flat_e)
    se = flat_e[order]
    counts = jnp.bincount(flat_e, length=N_EXPERTS)
    padded = (counts + ROUTE_BLOCK - 1) // ROUTE_BLOCK * ROUTE_BLOCK
    start = jnp.cumsum(counts) - counts
    pend = jnp.cumsum(padded)
    pstart = pend - padded
    dest = pstart[se] + (jnp.arange(a, dtype=jnp.int32) - start[se])
    cap = -(-a // ROUTE_BLOCK) * ROUTE_BLOCK + N_EXPERTS * ROUTE_BLOCK
    tok_buf = jnp.zeros((cap,), jnp.int32).at[dest].set(flat_t[order])
    gate_buf = jnp.zeros((cap,), xf.dtype).at[dest].set(flat_g[order])
    nblk = cap // ROUTE_BLOCK
    blk_e = jnp.minimum(jnp.searchsorted(pend, jnp.arange(nblk) * ROUTE_BLOCK, side='right'), N_EXPERTS - 1)
    xb = xf[tok_buf].reshape(nblk, ROUTE_BLOCK, dm)

    def expert_block(args):
        xblk, e = args
        return swiglu(xblk, w1[e], w3[e], w2[e])

    yb = lax.map(expert_block, (xb, blk_e)).reshape(cap, dm)
    return jnp.zeros_like(xf).at[tok_buf].add(yb * gate_buf[:, None])

def channel_mixer(layer, u, ffn_w1, ffn_w3, ffn_w2, moe_router, moe_w1, moe_w3, moe_w2):
    j = layer // 2
    if layer % 2 == 0:
        return swiglu(u, ffn_w1[j], ffn_w3[j], ffn_w2[j])
    b, t, dm = u.shape
    return moe_swiglu(u.reshape(b * t, dm), moe_router[j], moe_w1[j], moe_w3[j], moe_w2[j]).reshape(b, t, dm)

def setup_inputs(seed: int = 0) -> dict:
    key = jax.random.key(seed)
    ks = jax.random.split(key, 24)
    nrm = lambda k, s, sc: jax.random.normal(k, s, jnp.float32) * sc
    D, H = D_MODEL, MLSTM_HEADS
    ib = nrm(ks[10], (DEPTH, 2, H), 0.1)
    fb = jnp.linspace(3.0, 6.0, H, dtype=jnp.float32)[None, None] + nrm(ks[11], (DEPTH, 2, H), 0.1)
    b_gates = jnp.stack([ib[:, 0], fb[:, 0], ib[:, 1], fb[:, 1]], axis=1)
    return {
        "x": nrm(ks[0], (BATCH, SEQ, D), 1.0),
        "c": nrm(ks[1], (BATCH, D), 1.0),
        "ctx": nrm(ks[2], (BATCH, CTX_LEN, D), 1.0),
        "c_ctx": nrm(ks[3], (D,), 1.0),
        "norm1_g": 1.0 + nrm(ks[4], (DEPTH, D), 0.05),
        "norm2_g": 1.0 + nrm(ks[5], (DEPTH, D), 0.05),
        "w_ada": nrm(ks[6], (DEPTH, D, 6 * D), 0.5 * D ** -0.5),
        "b_ada": nrm(ks[7], (DEPTH, 6 * D), 0.02),
        "w_in": nrm(ks[8], (DEPTH, D, P_IN), D ** -0.5),
        "conv_w": nrm(ks[9], (DEPTH, 3, CONV_DIM), 0.5),
        "b_gates": b_gates,
        "mlstm_norm_g": 1.0 + nrm(ks[12], (DEPTH, MLSTM_DIM), 0.05),
        "w_out": nrm(ks[13], (DEPTH, D, D), D ** -0.5),
        "ffn_w1": nrm(ks[14], (N_DENSE, D, D_FF), D ** -0.5),
        "ffn_w3": nrm(ks[15], (N_DENSE, D, D_FF), D ** -0.5),
        "ffn_w2": nrm(ks[16], (N_DENSE, D_FF, D), D_FF ** -0.5),
        "moe_router": nrm(ks[17], (N_MOE, D, N_EXPERTS), D ** -0.5),
        "moe_w1": nrm(ks[18], (N_MOE, N_EXPERTS, D, D_FF), D ** -0.5),
        "moe_w3": nrm(ks[19], (N_MOE, N_EXPERTS, D, D_FF), D ** -0.5),
        "moe_w2": nrm(ks[20], (N_MOE, N_EXPERTS, D_FF, D), D_FF ** -0.5),
        "final_norm_g": 1.0 + nrm(ks[21], (D,), 0.05),
    }

def reference(x, c, ctx, c_ctx, norm1_g, norm2_g, w_ada, b_ada, w_in, conv_w, b_gates,
              mlstm_norm_g, w_out, ffn_w1, ffn_w3, ffn_w2, moe_router, moe_w1, moe_w3, moe_w2,
              final_norm_g):
    rows = x.shape[1] // GRID_W
    s_lat = jax.nn.silu(c)
    s_ctx = jax.nn.silu(c_ctx)
    h, hc = x, ctx
    for layer in range(DEPTH):
        last = layer == DEPTH - 1
        mod = s_lat @ w_ada[layer] + b_ada[layer]
        mod_c = s_ctx @ w_ada[layer] + b_ada[layer]
        sh1, sc1, g1, sh2, sc2, g2 = jnp.split(mod[:, None, :], 6, axis=-1)
        csh1, csc1, cg1, csh2, csc2, cg2 = jnp.split(mod_c, 6, axis=-1)
        w = w_in[layer]

        u = modulate(rmsnorm(h, norm1_g[layer]), sh1, sc1)
        uc = modulate(rmsnorm(hc, norm1_g[layer]), csh1, csc1)
        lat_in = mlstm_inputs(u, w[:, Q0:O0], b_gates[layer])
        ctx_in = mlstm_inputs(uc, w[:, Q0:O0], b_gates[layer])
        m_lat, m_ctx = mlstm_bidirectional(lat_in, ctx_in, not last)
        y_conv = short_conv_mixer(u, w[:, :Q0], conv_w[layer], rows)
        y_mlstm = mlstm_merge(m_lat, mlstm_norm_g[layer], jax.nn.sigmoid(u @ w[:, O0:]))
        h = h + g1 * (jnp.concatenate([y_conv, y_mlstm], axis=-1) @ w_out[layer])

        u2 = modulate(rmsnorm(h, norm2_g[layer]), sh2, sc2)
        h = h + g2 * channel_mixer(layer, u2, ffn_w1, ffn_w3, ffn_w2, moe_router, moe_w1, moe_w3, moe_w2)

        if not last:
            yc_conv = short_conv_mixer(uc, w[:, :Q0], conv_w[layer], None)
            yc_mlstm = mlstm_merge(m_ctx, mlstm_norm_g[layer], jax.nn.sigmoid(uc @ w[:, O0:]))
            hc = hc + cg1 * (jnp.concatenate([yc_conv, yc_mlstm], axis=-1) @ w_out[layer])
            uc2 = modulate(rmsnorm(hc, norm2_g[layer]), csh2, csc2)
            hc = hc + cg2 * channel_mixer(layer, uc2, ffn_w1, ffn_w3, ffn_w2, moe_router, moe_w1, moe_w3, moe_w2)
    return rmsnorm(h, final_norm_g)


_drawn_inputs = setup_inputs


def setup_inputs(seed=0):
    import zlib

    import numpy as np

    out = dict(_drawn_inputs(seed))
    spreads = {}
    factors = {'mlstm_norm_g': 3.881}
    for name, (base, spread) in spreads.items():
        noise = np.random.default_rng([zlib.crc32(name.encode()), seed]).standard_normal(out[name].shape)
        drawn = base * np.exp(spread * noise) if base else spread * noise
        out[name] = __import__('jax').numpy.asarray(drawn.astype(out[name].dtype))
    for name, factor in factors.items():
        out[name] = (out[name] * factor).astype(out[name].dtype)
    return out
```

```python
from contextlib import ExitStack, contextmanager

import numpy as np
import concourse.bass as bass
from concourse import mybir

P = 128
D = 1024
KT = D // P
SEQ, CTX = 256, 256
NT = SEQ + CTX
TT = NT // P
GRID_W = 64
CONV = 512
CT = CONV // P
HEADS, HD = 4, 128
DFF = 2816
FT = DFF // P
NE = 8
DEPTH = 2
EPS = 1e-6
NEG = -1e30
UNIT = 2048
SLOTS = 3
HE = HD + 1
GROUPS = [8, 8, 6]
CHUNKS = [512] * 5 + [256]
UPE = 33
ADA_UNITS = DEPTH * 6 * D // 256
LAT_STEPS = {0: [2, 3, 0, 1], 1: [3, 2, 1, 0]}

PARAMS = [("ident", P), ("ones", P), ("mask_low", P), ("mask_up", P), ("up01", P), ("low01", P), ("iota", P),
          ("rank", NE), ("eps", 1), ("cond", KT * 2), ("final_g", KT), ("router", KT * NE), ("b_ada", DEPTH * 48)]
for _l in range(DEPTH):
    PARAMS += [(f"norm1_{_l}", KT), (f"norm2_{_l}", KT), (f"conv_{_l}", CT * 3), (f"mnorm_{_l}", CT),
               (f"bgates_{_l}", 16), (f"wgates_{_l}", KT * 16)]
COL, _n = {}, 0
for _name, _w in PARAMS:
    COL[_name] = (_n, _n + _w)
    _n += _w
NPAR = _n


def expert_units():
    out = []
    for c, w in enumerate(CHUNKS):
        parts = 2 if w == 512 else 1
        out += [("w1", c, h) for h in range(parts)] + [("w3", c, h) for h in range(parts)]
        if c:
            out += [("w2", c - 1, h) for h in range(2)]
    return out + [("w2", len(CHUNKS) - 1, 0)]


EXPERT_UNITS = expert_units()
assert len(EXPERT_UNITS) == UPE


def first_units():
    at, n = {}, 0
    for name, k in ([("ada", ADA_UNITS), ("conv0", 6), ("qkvo0", 8), ("out0", 4)]
                    + [(f"ffn{g}", f + 4) for g, f in enumerate(GROUPS)]
                    + [("conv1", 6), ("qkvo1", 8), ("out1", 4), ("moe", NE * UPE)]):
        at[name] = n
        n += k
    return at, n


UNIT_AT, N_UNITS = first_units()
assert (N_UNITS + 2) % SLOTS == 0 and NE * UPE % SLOTS == 0


class Fills:

    def __init__(self):
        self.n, self.at = [0] * 16, {}

    def add(self, name, bank, unit=None):
        self.n[bank] += 1
        if unit is None:
            self.n[8 + bank] += 1
        self.at[name] = (bank, self.n[bank], unit, self.n[8 + bank])

    def repeat(self, before, trips):
        per = [b - a for a, b in zip(before, self.n)]
        self.n = [b + (trips - 1) * p for b, p in zip(self.n, per)]
        return per


def plan_fills():
    f, per = Fills(), {}
    f.add("ada", 7, ADA_UNITS - 1)

    def norm(tag):
        f.add(f"norm {tag}", 0)

    for l in range(DEPTH):
        norm(f"1 {l}")
        u = UNIT_AT[f"conv{l}"]
        for k in range(6):
            for j in range(2):
                f.add(f"conv {l} {k} {j}", 2 * (k % 4) + j, u + k)
        u = UNIT_AT[f"qkvo{l}"]
        for c, name in enumerate("qkvo"):
            for t in range(TT if l == 0 or name in "kv" else 2):
                f.add(f"{name} {l} {t}", 4 * (c % 2) + t, u + 2 * c + 1)
        f.add(f"gates {l}", 0)
        for t in range(TT):
            if l == 0 or t < 2:
                f.add(f"qT {l} {t}", 4 + t)
                f.add(f"kT {l} {t}", t)
        f.add(f"cum {l}", 0)
        for a in range(2 * TT):
            f.add(f"G {l} {a}", a % 2)
        for t, d, k in scan_steps():
            if l == 0 or t < 2:
                f.add(f"M {l} {t} {d}", 0)
                f.add(f"S {l} {t} {d}", 1)
                f.add(f"num {l} {t} {d} 0", 2)
                f.add(f"num {l} {t} {d} 1", 3)
                if k:
                    f.add(f"int {l} {t} {d} 0", 4)
                    f.add(f"int {l} {t} {d} 1", 5)
            if k < 3:
                f.add(f"upd {l} {t} {d} 0", 6)
                f.add(f"upd {l} {t} {d} 1", 7)
        for t in range(TT if l == 0 else 2):
            f.add(f"yT {l} {t}", t)
        for k in range(4):
            for j in range(2):
                f.add(f"out {l} {k} {j}", 2 * (k % 4) + j, UNIT_AT[f"out{l}"] + k)
        norm(f"2 {l}")
        if l == 0:
            def group(g):
                u, nf = UNIT_AT[f"ffn{g}"], GROUPS[g]
                for k in range(nf + 4):
                    for j in range(2):
                        f.add(f"ffn {g} {k} {j}", 2 * (k % 4) + j, u + k)
            before = list(f.n)
            group(0)
            per["ffn"] = f.repeat(before, 2)
            group(2)
    f.add("logits", 0)
    f.add("count", 1)
    for i in range(8):
        f.add(f"utok {i}", 2 + i % 4)
    before_pass = list(f.n)
    for i in range(4):
        f.add(f"PT {i}", i)
    f.add("gslot", 6)
    for i in range(4):
        f.add(f"gather {i}", 4 + i % 2)
    before, u = list(f.n), UNIT_AT["moe"]
    aux = 0
    for j, (m, c, h) in enumerate(EXPERT_UNITS):
        last = j + 1 == UPE or EXPERT_UNITS[j + 1][:2] != (m, c)
        if m != "w2" and last:
            f.add(f"{m} {c}", 2 * (c % 2) + (m == "w3"), u + j)
        if j == UPE - 1:
            f.add("y 0", 6, u + j)
            f.add("y 1", 7, u + j)
        if (m == "w1" and last and c) or j == UPE - 2:
            f.add(f"T {c - 1 if m == 'w1' else len(CHUNKS) - 1}", 4 + aux % 2)
            aux += 1
        if j == UPE - 2:
            for i in range(4):
                f.add(f"next {i}", 4 + aux % 2)
                aux += 1
        if j == UPE - 1:
            for i in range(4):
                f.add(f"back {i}", 4 + aux % 2)
                aux += 1
    per["expert"] = f.repeat(before, NE)
    per["pass"] = [b - a for a, b in zip(before_pass, f.n)]
    f.add("norm f", 0)
    return f, per


def scan_steps():
    return [(LAT_STEPS[d][k], d, k) for k in range(4) for d in range(2)]


FILLS, FILLS_PER = plan_fills()


def backbone(nc, stream, tokens, params, out):
    f32, f32r, i32 = mybir.dt.float32, mybir.dt.float32r, mybir.dt.int32
    ACT, ALU, AX = mybir.ActivationFunctionType, mybir.AluOpType, mybir.AxisListType
    ds = bass.ds

    ctx = ExitStack()
    with ctx:
        def tensors(stack):
            def sb(name, shape, dt=f32):
                return stack.enter_context(nc.sbuf_tensor(name, shape, dt))
            return sb

        sb = tensors(ctx)
        raw = [sb(f"raw{i}", [P, UNIT]) for i in range(SLOTS)]
        whi = [sb(f"whi{i}", [P, UNIT], f32r) for i in range(SLOTS)]
        wlo = [sb(f"wlo{i}", [P, UNIT], f32r) for i in range(SLOTS)]
        h = sb("h", [P, KT, NT])
        u_hi = sb("u_hi", [P, KT, NT], f32r)
        u_lo = sb("u_lo", [P, KT, NT], f32r)
        par = sb("par", [P, NPAR])
        cond4 = sb("cond4", [P, KT, 4], f32r)
        condf = sb("condf", [P, KT, 2])
        wg_hi = sb("wg_hi", [P, DEPTH, KT, 16], f32r)
        wg_lo = sb("wg_lo", [P, DEPTH, KT, 16], f32r)
        ro_hi = sb("ro_hi", [P, KT, NE], f32r)
        ro_lo = sb("ro_lo", [P, KT, NE], f32r)
        mod = sb("mod", [P, DEPTH * 48, 2])
        gain = sb("gain", [P, DEPTH, 2, KT, 2])
        npass = sb("npass", [1, 1], i32)
        with ExitStack() as stack:
            sb = tensors(stack)
            square = sb("square", [P, 2, NT])
            std = sb("std", [P, NT])
            rstd = sb("rstd", [P, NT])
            scaled = sb("scaled", [P, 2, NT])
            modded = sb("modded", [P, 2, NT])
            result = sb("result", [P, KT, SEQ])
        with ExitStack() as stack:
            sb = tensors(stack)
            q = sb("q", [P, TT, 512])
            k = sb("k", [P, TT, 512])
            v = sb("v", [P, TT, HEADS, HE])
            o = sb("o", [P, TT, 512])
            qT = sb("qT", [P, HEADS, NT])
            kT = sb("kT", [P, HEADS, NT])
            conv = sb("conv", [P, CT, NT])
            hacc = q
            diag = sb("diag", [P, 2, 512])
            t512 = sb("t512", [P, 512])
            decay = sb("decay", [P, 512])
            prob = sb("prob", [P, 512])
            inter = sb("inter", [P, HEADS, HE])
            u_sum = inter
            kw = sb("kw", [P, 512])
            state = sb("state", [P, 2, HEADS, HE])
            hh, yprod = diag, t512
            gts = sb("gts", [P, TT * 2, 2, HEADS])
            lf = sb("lf", [P, TT * 2, HEADS])
            g_tmp = sb("g_tmp", [P, 2, TT * 2, HEADS])
            cum = sb("cum", [P, 2, TT * 2, HEADS])
            gg = sb("gg", [P, TT * 2, HEADS])
            gmax = sb("gmax", [P, TT * 2, HEADS])
            pmax = sb("pmax", [P, TT * 2, HEADS])
            mprev = sb("mprev", [P, TT * 2, HEADS])
            m_t = sb("m_t", [P, TT * 2, HEADS])
            m_l = sb("m_l", [P, TT * 2, HEADS])
            e_in = sb("e_in", [P, 4, TT * 2, HEADS])
            e_out = sb("e_out", [P, 4, TT * 2, HEADS])
            small = sb("small", [P, 4, HEADS])
        with ExitStack() as stack:
            sb = tensors(stack)
            hid_hi = sb("hid_hi", [P, 8, NT], f32r)
            hid_lo = sb("hid_lo", [P, 8, NT], f32r)
            sil0 = sb("sil0", [P, 2, NT])
            hid0 = sb("hid0", [P, 2, NT])
        with ExitStack() as stack:
            sb = tensors(stack)
            pick = sb("pick", [P, 2, NE + 1, P], f32r)
            pickT = sb("pickT", [P, NE, SEQ], f32r)
            utok_hi = sb("utok_hi", [P, 2, D], f32r)
            utok_lo = sb("utok_lo", [P, 2, D], f32r)
            xe_hi = sb("xe_hi", [P, KT, P], f32r)
            xe_lo = sb("xe_lo", [P, KT, P], f32r)
            sil = sb("sil", [P, 2, 512])
            hid = sb("hid", [P, 2, 512])
            hT_hi = sb("hT_hi", [P, 2, 4, P], f32r)
            hT_lo = sb("hT_lo", [P, 2, 4, P], f32r)
            y_hi = sb("y_hi", [P, D], f32r)
            y_lo = sb("y_lo", [P, D], f32r)
            gslot = sb("gslot", [P, NE])
            gcol = sb("gcol", [P, 1])
            lg = sb("lg", [P, 2, NE])
            sc8 = sb("sc8", [P, 6, 2, NE])
            one1 = sb("one1", [P, 2, NE])
            one2 = sb("one2", [P, 2, NE])
            gate = sb("gate", [P, 2, NE])
            sel = sb("sel", [P, 2, NE])
            slot_of = sb("slot_of", [P, 2, NE])
            s2 = sb("s2", [P, 8, 2])
        bank = [ctx.enter_context(nc.psum_tensor(f"bank{i}", [P, 512], f32)) for i in range(8)]

        def sem(name):
            return ctx.enter_context(nc.semaphore(name))

        raw_loaded = [sem(f"raw_loaded{i}") for i in range(SLOTS)]
        hi_ready, lo_ready, unit_used = sem("hi_ready"), sem("lo_ready"), sem("unit_used")
        bank_full = [sem(f"bank_full{i}") for i in range(8)]
        bank_read = [sem(f"bank_read{i}") for i in range(8)]
        params_loaded, tokens_loaded, out_stored = sem("params_loaded"), sem("tokens_loaded"), sem("out_stored")
        small_hi, small_lo = sem("small_hi"), sem("small_lo")
        cond_silu, mod_ready = sem("cond_silu"), sem("mod_ready")
        square_ready, square_used = sem("square_ready"), sem("square_used")
        scaled_ready, modded_ready, u_hi_ready, u_lo_ready = (sem("scaled_ready"), sem("modded_ready"),
                                                              sem("u_hi_ready"), sem("u_lo_ready"))
        conv_ready, conv_hi, conv_lo = sem("conv_ready"), sem("conv_hi"), sem("conv_lo")
        v_ones = sem("v_ones")
        gate_arg, gate_log, logf_ready = sem("gate_arg"), sem("gate_log"), sem("logf_ready")
        diag_ready, exp_arg, exp_done = sem("diag_ready"), sem("exp_arg"), sem("exp_done")
        decay_arg, decay_ready, kw_ready = sem("decay_arg"), sem("decay_ready"), sem("kw_ready")
        sumsq_ready, root_ready, merged, y_hi_done = (sem("sumsq_ready"), sem("root_ready"), sem("merged"),
                                                      sem("y_hi_done"))
        hid_hi_ready, hid_lo_ready = sem("hid_hi_ready"), sem("hid_lo_ready")
        route_arg, route_exp, sel_ready, pick_ready, npass_ready = (
            sem("route_arg"), sem("route_exp"), sem("sel_ready"), sem("pick_ready"), sem("npass_ready"))
        silu_ready, hidden_ready, hT_hi_ready, y_hi_ready = (sem("silu_ready"), sem("hidden_ready"),
                                                             sem("hT_hi_ready"), sem("y_hi_ready"))
        result_ready = sem("result_ready")
        dve_chain, act_chain = sem("dve_chain"), sem("act_chain")

        class Counts:

            def __init__(self, eng):
                self.eng, self.n, self.loops = eng, {}, []

            def at(self, s, base):
                value = base
                for i, per in self.loops:
                    if per.get(s, 0):
                        assert base > 0, "a wait that may be for zero"
                        value = i * per[s] + value
                return value

            def next(self, s, k=1):
                self.n[s] = self.n.get(s, 0) + k
                return s, self.at(s, self.n[s])

            @contextmanager
            def loop(self, trips, per, count=None):
                before = dict(self.n)
                with self.eng.Fori(0, trips) as i:
                    self.loops.append((i, per))
                    yield i
                    self.loops.pop()
                for s, n in self.n.items():
                    step = n - before.get(s, 0)
                    assert step == per.get(s, 0), (s, step, per.get(s, 0))
                    self.n[s] += (count - 1) * step

            def full(self, name):
                b, _, unit, n = FILLS.at[name]
                s, n = (bank_full[b], n) if unit is None else (unit_used, unit + 1)
                return s, self.at(s, n)

            def read(self, name, later_turns=0):
                b, n = FILLS.at[name][:2]
                return bank_read[b], self.at(bank_read[b], n + later_turns * FILLS_PER["expert"][b])

            def free(self, name):
                b, n = FILLS.at[name][:2]
                return bank_read[b], self.at(bank_read[b], n - 1)

        def bank_of(name):
            return bank[FILLS.at[name][0]]

        def fill_loops(kind):
            out = {bank_read[b]: FILLS_PER[kind][b] for b in range(8)}
            out.update({bank_full[b]: FILLS_PER[kind][8 + b] for b in range(8)})
            return out

        def read_of(name):
            return bank_read[FILLS.at[name][0]]

        def full_of(name):
            return bank_full[FILLS.at[name][0]]

        def cols(name):
            a, b = COL[name]
            return par[:, a:b]

        ident, ones = cols("ident"), cols("ones")
        masks = {("A", 0): cols("mask_low"), ("A", 1): cols("mask_up"),
                 ("D", 0): cols("mask_up"), ("D", 1): cols("mask_low")}
        tri = [cols("up01"), cols("low01")]

        def mod_col(l, j, kt, s):
            return mod[:, 48 * l + 8 * j + kt, s:s + 1]

        def sets(width):
            return [(s, slice(256 * s, 256 * s + 256)) for s in range(width // 256)]

        UNIT_LOOP = {"ada": 3, "ffn": 12, "expert": UPE, "pass": NE * UPE}

        def unit_loops(kind, extra=None):
            n = UNIT_LOOP[kind]
            out = {unit_used: n, hi_ready: n, lo_ready: n, **{s: 16 * n // SLOTS for s in raw_loaded}}
            out.update(extra or {})
            return out

        block = ctx.enter_context(nc.Block())

        @block.sync
        def _(sp):
            sp.dma_start(par[:, :], params).then_inc(params_loaded, 16)

            for n in range(SLOTS):
                sp.dma_start(raw[n][:, :], stream[n]).then_inc(raw_loaded[n], 16)
            sp.dma_start(h[:, :, :], tokens).then_inc(tokens_loaded, 16)

            def load_rest(first, turns, back):
                with sp.Fori(0, turns) as i:
                    for j in range(SLOTS):
                        slot = (first + j) % SLOTS
                        sp.wait_ge(lo_ready, i * SLOTS + (first + j - SLOTS + 1))
                        sp.dma_start(raw[slot][:, :],
                                     stream[ds(i * SLOTS + (first + j - back), 1)].rearrange("a p n -> p (a n)")
                                     ).then_inc(raw_loaded[slot], 16)

            load_rest(SLOTS, (N_UNITS + 2 - SLOTS) // SLOTS, 0)
            sp.wait_ge(npass_ready, 1)
            passes = sp.value_load(npass[0:1, 0:1], min_val=1, max_val=2)
            with sp.If(passes > 1):
                load_rest(N_UNITS + 2, NE * UPE // SLOTS, NE * UPE)
            with sp.Else():
                sp.nop()
            sp.wait_ge(result_ready, 1)
            sp.dma_start(out, result[:, :, :]).then_inc(out_stored, 16)
            sp.wait_ge(out_stored, 16)

        @block.scalar
        def _(act):
            t = Counts(act)

            def chain(ins):
                ins.then_inc(act_chain, 1)
                act.wait_ge(*t.next(act_chain))

            def split(n):
                act.wait_ge(raw_loaded[n % SLOTS], t.at(raw_loaded[n % SLOTS], 16 * (n // SLOTS + 1)))
                if n >= SLOTS:
                    act.wait_ge(unit_used, t.at(unit_used, n - SLOTS + 1))
                nc.scalar.activation(whi[n % SLOTS][:, :], raw[n % SLOTS][:, :], ACT.Copy).then_inc(hi_ready, 1)

            ahead = [0]

            def split_to(n):
                while ahead[0] <= min(n, N_UNITS - 1):
                    split(ahead[0])
                    ahead[0] += 1

            def copy(dst, src, **kw_):
                return nc.scalar.activation(dst, src, ACT.Copy, **kw_)

            act.wait_ge(params_loaded, 16)
            cd = cols("cond").rearrange("p (k s) -> p k s", s=2)
            chain(nc.scalar.activation(condf[:, :, :], cd, ACT.Silu))
            copy(cond4[:, :, 0:2], condf[:, :, :]).then_inc(small_hi, 1)
            for l in range(DEPTH):
                copy(wg_hi[:, l, :, :], cols(f"wgates_{l}").rearrange("p (k c) -> p k c", c=16)).then_inc(small_hi, 1)
            copy(ro_hi[:, :, :], cols("router").rearrange("p (k c) -> p k c", c=NE)).then_inc(small_hi, 1)

            def norm(tag, width, final=False):
                for kt in range(KT):
                    if kt >= 2:
                        act.wait_ge(*t.next(square_used))
                    nc.scalar.activation(square[:, kt % 2, 0:width], h[:, kt, 0:width],
                                         ACT.Square).then_inc(square_ready, 1)
                act.wait_ge(*t.next(square_used))
                act.wait_ge(*t.full(f"norm {tag}"))
                ps = bank_of(f"norm {tag}")
                nc.scalar.activation(std[:, 0:width], ps[:, 0:width], ACT.Sqrt, bias=cols("eps"),
                                     scale=1.0 / D).then_inc(read_of(f"norm {tag}"), 1)
                if final:
                    return
                which, l = tag.split()
                which, l = int(which) - 1, int(l)
                for kt in range(KT):
                    act.wait_ge(*t.next(scaled_ready))
                    if kt >= 2:
                        act.wait_ge(*t.next(u_lo_ready))
                    for s, c in sets(width):
                        last = nc.scalar.activation(modded[:, kt % 2, c], scaled[:, kt % 2, c], ACT.Identity,
                                                    bias=mod_col(l, 3 * which, kt, s), scale=gain[:, l, which, kt, s:s + 1])
                    last.then_inc(modded_ready, 1)
                    act.wait_ge(*t.next(modded_ready))
                    copy(u_hi[:, kt, 0:width], modded[:, kt % 2, 0:width]).then_inc(u_hi_ready, 1)
                act.wait_ge(*t.next(u_lo_ready, 2))

            split_to(1)
            split_to(4)
            loop_at = ahead[0]
            with t.loop(ADA_UNITS // 3 - 1, unit_loops("ada"), 15) as i:
                for j in range(3):
                    split(loop_at + j)
            ahead[0] = loop_at + 3 * 15

            act.wait_ge(tokens_loaded, 16)
            act.wait_ge(mod_ready, 1)
            for l in range(DEPTH):
                W = NT if l == 0 else SEQ
                norm(f"1 {l}", NT)
                u = UNIT_AT[f"conv{l}"]
                for c in range(6):
                    split_to(u + c + 2)
                    if c < CT:
                        act.wait_ge(*t.full(f"conv {l} {c} 1"))
                        ps = bank_of(f"conv {l} {c} 1")
                        if c >= 2:
                            act.wait_ge(*t.read(f"conv {l} {c - 2} 0"))
                        copy(hh[:, c % 2, 0:W], ps[:, 0:W]).then_inc(read_of(f"conv {l} {c} 1"), 1)
                u = UNIT_AT[f"qkvo{l}"]
                for c, name in enumerate("qkvo"):
                    split_to(u + 2 * c + 2)
                    split_to(u + 2 * c + 3)
                    for tt in range(TT if l == 0 or name in "kv" else 2):
                        if name == "k":
                            continue
                        act.wait_ge(*t.full(f"{name} {l} {tt}"))
                        ps = bank_of(f"{name} {l} {tt}")
                        if name == "q":
                            ins = copy(q[:, tt, :], ps[:, :])
                        elif name == "v":
                            ins = copy(v[:, tt, :, 0:HD], ps[:, :].rearrange("p (h d) -> p h d", h=HEADS))
                        else:
                            ins = nc.scalar.activation(o[:, tt, :], ps[:, :], ACT.Sigmoid)
                        ins.then_inc(read_of(f"{name} {l} {tt}"), 1)
                for c in (4, 5):
                    for j in range(2):
                        act.wait_ge(*t.read(f"conv {l} {c} {j}"))
                act.wait_ge(unit_used, t.at(unit_used, u + 8))
                act.wait_ge(*t.full(f"gates {l}"))
                copy(u_hi[:, 0:CT, 0:W], conv[:, :, 0:W]).then_inc(conv_hi, 1)
                act.wait_ge(*t.next(gate_arg))
                chain(nc.scalar.activation(g_tmp[:, 1], g_tmp[:, 0], ACT.Exp))
                nc.scalar.activation(g_tmp[:, 0], g_tmp[:, 1], ACT.Ln, bias=1.0).then_inc(gate_log, 1)
                for tt in range(TT if l == 0 else 2):
                    act.wait_ge(*t.full(f"qT {l} {tt}"))
                    ps = bank_of(f"qT {l} {tt}")
                    copy(qT[:, :, tt * P:tt * P + P], ps[:, :].rearrange("p (h s) -> p h s", h=HEADS)
                         ).then_inc(read_of(f"qT {l} {tt}"), 1)
                act.wait_ge(*t.next(exp_arg))
                nc.scalar.activation(e_out[:, :, :, :], e_in[:, :, :, :], ACT.Exp).then_inc(exp_done, 1)
                act.wait_ge(*t.next(exp_done))
                for tt, d, kk in scan_steps():
                    if l and tt >= 2:
                        continue
                    a = 2 * tt + d
                    act.wait_ge(*t.read(f"M {l} {tt} {d}"))
                    for hd in range(HEADS):
                        last = nc.scalar.activation(decay[:, hd * P:hd * P + P], t512[:, hd * P:hd * P + P], ACT.Exp,
                                                    bias=gg[:, a, hd:hd + 1])
                    last.then_inc(decay_ready, 1)
                    if kk:
                        for part in range(2):
                            act.wait_ge(*t.full(f"int {l} {tt} {d} {part}"))
                            ps = bank_of(f"int {l} {tt} {d} {part}")
                            for j in range(2):
                                hd = 2 * part + j
                                last = copy(inter[:, hd, :], ps[:, 256 * j:256 * j + HE],
                                            scale=e_out[:, 0, a, hd:hd + 1])
                            last.then_inc(read_of(f"int {l} {tt} {d} {part}"), 1)
                for tt in range(TT if l == 0 else 2):
                    act.wait_ge(*t.next(sumsq_ready))
                    nc.scalar.activation(small[:, 1, :], small[:, 0, :], ACT.Sqrt, bias=cols("eps"),
                                         scale=1.0 / HD).then_inc(root_ready, 1)
                for tt in range(TT if l == 0 else 2):
                    act.wait_ge(*t.full(f"yT {l} {tt}"))
                    ps = bank_of(f"yT {l} {tt}")
                    for hd in range(HEADS):
                        last = copy(u_hi[:, CT + hd, tt * P:tt * P + P], ps[:, hd * P:hd * P + P],
                                    scale=cols(f"mnorm_{l}")[:, hd:hd + 1])
                    last.then_inc(y_hi_done, 1)
                u = UNIT_AT[f"out{l}"]
                for c in range(4):
                    split_to(u + c + 2)
                act.wait_ge(*t.read(f"out {l} 3 1"))
                norm(f"2 {l}", W)
                if l == 0:
                    def group(g, base):
                        u, nf = UNIT_AT[f"ffn{g}"], GROUPS[g]
                        for c in range(nf + 4):
                            split(base + c)
                            if c < nf and c % 2:
                                for j in range(2):
                                    act.wait_ge(*t.full(f"ffn {g} {c - 1} {j}"))
                                    ps = bank_of(f"ffn {g} {c - 1} {j}")
                                    nc.scalar.activation(sil0[:, j, :], ps[:, :], ACT.Silu
                                                         ).then_inc(read_of(f"ffn {g} {c - 1} {j}"), 1)
                                for j in range(2):
                                    act.wait_ge(*t.read(f"ffn {g} {c} {j}"))
                                    copy(hid_hi[:, c - 1 + j, :], hid0[:, j, :]).then_inc(hid_hi_ready, 1)
                    assert ahead[0] == UNIT_AT["ffn0"] + 2
                    with t.loop(2, unit_loops("ffn", fill_loops("ffn")), 2):
                        group(0, ahead[0])
                    ahead[0] += 24
                    group(2, ahead[0])
                    ahead[0] += 10
                    act.wait_ge(*t.read("ffn 2 9 1"))
            act.wait_ge(*t.next(route_arg))
            nc.scalar.activation(s2[:, 3, :], s2[:, 2, :], ACT.Exp).then_inc(route_exp, 1)
            for i in range(0, 8, 2):
                act.wait_ge(*t.full(f"utok {i}"))
                ps = bank_of(f"utok {i}")
                tt, half = i // 4, i // 2 % 2
                copy(utok_hi[:, tt, 512 * half:512 * half + 512], ps[:, :]).then_inc(read_of(f"utok {i}"), 1)
            act.wait_ge(npass_ready, 1)
            passes = act.value_load(npass[0:1, 0:1], min_val=1, max_val=2)
            assert ahead[0] == UNIT_AT["moe"] + 2

            def gathered(name, i):
                act.wait_ge(*t.full(name))
                ps = bank_of(name)
                copy(xe_hi[:, 2 * i:2 * i + 4, :], ps[:, :].rearrange("p (k s) -> p k s", k=4)
                     ).then_inc(read_of(name), 1)

            with t.loop(passes, {**unit_loops("pass", fill_loops("pass")), y_hi_ready: NE}, 1) as i_pass:
                for i in range(4):
                    act.wait_ge(*t.full(f"PT {i}"))
                    ps = bank_of(f"PT {i}")
                    copy(pickT[:, 2 * i:2 * i + 2, :], ps[:, :].rearrange("p (e n) -> p e n", e=2)
                         ).then_inc(read_of(f"PT {i}"), 1)
                for i in (0, 2):
                    gathered(f"gather {i}", i)
                with t.loop(NE, {**unit_loops("expert", fill_loops("expert")), y_hi_ready: 1}, NE) as e:
                    for j, (m, c, part) in enumerate(EXPERT_UNITS):
                        split(ahead[0] + j)
                        last = j + 1 == UPE or EXPERT_UNITS[j + 1][:2] != (m, c)
                        if m == "w1" and last:
                            act.wait_ge(*t.full(f"w1 {c}"))
                            ps, w = bank_of(f"w1 {c}"), CHUNKS[c]
                            if c >= 2:
                                act.wait_ge(*t.read(f"w3 {c - 2}"))
                            nc.scalar.activation(sil[:, c % 2, 0:w], ps[:, 0:w], ACT.Silu
                                                 ).then_inc(read_of(f"w1 {c}"), 1)
                        if (m == "w1" and last and c) or j == UPE - 2:
                            c_t = c - 1 if m == "w1" else len(CHUNKS) - 1
                            n_t = CHUNKS[c_t] // P
                            act.wait_ge(*t.full(f"T {c_t}"))
                            ps = bank_of(f"T {c_t}")
                            copy(hT_hi[:, c_t % 2, 0:n_t, :], ps[:, 0:n_t * P].rearrange("p (k s) -> p k s", k=n_t)
                                 ).then_inc(hT_hi_ready, 1)
                        if j == UPE - 2:
                            for i in (0, 2):
                                gathered(f"next {i}", i)
                        if j == UPE - 1:
                            for half in range(2):
                                act.wait_ge(*t.full(f"y {half}"))
                                ps = bank_of(f"y {half}")
                                last_ins = copy(y_hi[:, 512 * half:512 * half + 512], ps[:, :], scale=gcol[:, :])
                            last_ins.then_inc(y_hi_ready, 1)
            t.loops.append((passes - 1, fill_loops("pass")))
            act.wait_ge(*t.read("back 3", later_turns=NE - 1))
            norm("f", SEQ, final=True)

        @block.vector
        def _(dve):
            t = Counts(dve)
            TTn, STT = nc.vector.tensor_tensor, nc.vector.scalar_tensor_tensor

            def chain(ins):
                ins.then_inc(dve_chain, 1)
                dve.wait_ge(*t.next(dve_chain))

            def split(n):
                dve.wait_ge(hi_ready, t.at(hi_ready, n + 1))
                TTn(wlo[n % SLOTS][:, :], raw[n % SLOTS][:, :], whi[n % SLOTS][:, :].bitcast(f32),
                    ALU.subtract).then_inc(lo_ready, 1)

            ahead = [0]

            def split_to(n):
                while ahead[0] <= min(n, N_UNITS - 1):
                    split(ahead[0])
                    ahead[0] += 1

            def wide(x, n, shape):
                return x.unsqueeze(len(shape) - 1).broadcast_to(shape)

            dve.wait_ge(params_loaded, 16)
            dve.wait_ge(*t.next(small_hi))
            TTn(cond4[:, :, 2:4], condf[:, :, :], cond4[:, :, 0:2].bitcast(f32), ALU.subtract).then_inc(small_lo, 1)
            for l in range(DEPTH):
                dve.wait_ge(*t.next(small_hi))
                TTn(wg_lo[:, l, :, :], cols(f"wgates_{l}").rearrange("p (k c) -> p k c", c=16),
                    wg_hi[:, l, :, :].bitcast(f32), ALU.subtract).then_inc(small_lo, 1)
            dve.wait_ge(*t.next(small_hi))
            TTn(ro_lo[:, :, :], cols("router").rearrange("p (k c) -> p k c", c=NE), ro_hi[:, :, :].bitcast(f32),
                ALU.subtract).then_inc(small_lo, 1)

            split_to(4)
            loop_at = ahead[0]
            with t.loop(15, unit_loops("ada"), 15) as i:
                for j in range(3):
                    split(loop_at + j)
            ahead[0] = loop_at + 45
            dve.wait_ge(*t.full("ada"))
            ps = bank_of("ada")[:, 0:DEPTH * 48 * 4].rearrange("p (n c) -> p n c", c=4)
            chain(TTn(mod[:, :, :], ps[:, :, 0:2], wide(cols("b_ada"), 2, [P, DEPTH * 48, 2]), ALU.add))
            TTn(mod[:, :, :], mod[:, :, :], ps[:, :, 2:4], ALU.add).then_inc(read_of("ada"), 1)
            dve.wait_ge(*t.read("ada"))
            for l in range(DEPTH):
                for w in range(2):
                    s0 = 48 * l + 8 * (3 * w + 1)
                    last = STT(gain[:, l, w, :, :], mod[:, s0:s0 + 8, :], 1.0,
                               wide(cols(f"norm{w + 1}_{l}"), 2, [P, KT, 2]), ALU.add, ALU.mult)
            last.then_inc(mod_ready, 1)
            dve.wait_ge(*t.next(mod_ready))
            dve.wait_ge(tokens_loaded, 16)

            def norm(tag, width, final=False):
                dve.wait_ge(*t.read(f"norm {tag}"))
                chain(nc.vector.reciprocal(rstd[:, 0:width], std[:, 0:width]))
                if final:
                    for kt in range(KT):
                        last = STT(result[:, kt, :], h[:, kt, 0:width], cols("final_g")[:, kt:kt + 1],
                                   rstd[:, 0:width], ALU.mult, ALU.mult)
                    last.then_inc(result_ready, 1)
                    return

                def scale(kt):
                    TTn(scaled[:, kt % 2, 0:width], h[:, kt, 0:width], rstd[:, 0:width],
                        ALU.mult).then_inc(scaled_ready, 1)
                scale(0)
                scale(1)
                for kt in range(KT):
                    dve.wait_ge(*t.next(u_hi_ready))
                    TTn(u_lo[:, kt, 0:width], modded[:, kt % 2, 0:width], u_hi[:, kt, 0:width].bitcast(f32),
                        ALU.subtract).then_inc(u_lo_ready, 1)
                    if kt + 2 < KT:
                        scale(kt + 2)

            def residual(name, kt, width, l, j):
                dve.wait_ge(*t.full(name))
                ps = bank_of(name)
                for s, c in sets(width):
                    last = STT(h[:, kt, c], ps[:, c], mod_col(l, j, kt, s), h[:, kt, c], ALU.mult, ALU.add)
                last.then_inc(read_of(name), 1)

            for l in range(DEPTH):
                W = NT if l == 0 else SEQ
                norm(f"1 {l}", NT)
                nc.vector.memset(v[:, :, :, HD:HE], 1.0).then_inc(v_ones, 1)
                u = UNIT_AT[f"conv{l}"]
                cw = cols(f"conv_{l}").rearrange("p (c j) -> p c j", j=3)
                for c in range(6):
                    split_to(u + c + 2)
                    if c < CT:
                        dve.wait_ge(*t.full(f"conv {l} {c} 0"))
                        ps = bank_of(f"conv {l} {c} 0")
                        dve.wait_ge(*t.read(f"conv {l} {c} 1"))
                        TTn(yprod[:, 0:W], ps[:, 0:W], hh[:, c % 2, 0:W], ALU.mult).then_inc(
                            read_of(f"conv {l} {c} 0"), 1)
                        dve.wait_ge(*t.read(f"conv {l} {c} 0"))
                        chain(nc.vector.tensor_scalar(conv[:, c, 0:W], yprod[:, 0:W], cw[:, c, 1:2], None, ALU.mult))
                        rows = [(0, SEQ, GRID_W)] + ([(SEQ, NT, CTX)] if l == 0 else [])
                        for side in range(2):
                            for a, b, w in rows:
                                z = conv[:, c, a:b].rearrange("p (r w) -> p r w", w=w)
                                y = yprod[:, a:b].rearrange("p (r w) -> p r w", w=w)
                                to, of = (slice(1, w), slice(0, w - 1)) if side == 0 else (slice(0, w - 1), slice(1, w))
                                last = STT(z[:, :, to], y[:, :, of], cw[:, c, 2 * side:2 * side + 1], z[:, :, to],
                                           ALU.mult, ALU.add)
                            chain(last)
                    else:
                        for j in range(2):
                            ch = 2 * (c - CT) + j
                            name = f"conv {l} {c} {j}"
                            dve.wait_ge(*t.full(name))
                            ps = bank_of(name)
                            TTn(conv[:, ch, 0:W], conv[:, ch, 0:W], ps[:, 0:W], ALU.mult).then_inc(read_of(name), 1)
                u = UNIT_AT[f"qkvo{l}"]
                for c, name in enumerate("qkvo"):
                    split_to(u + 2 * c + 3)
                    if name == "k":
                        for tt in range(TT):
                            dve.wait_ge(*t.full(f"k {l} {tt}"))
                            ps = bank_of(f"k {l} {tt}")
                            nc.vector.tensor_scalar(k[:, tt, :], ps[:, :], HD ** -0.5, None,
                                                    ALU.mult).then_inc(read_of(f"k {l} {tt}"), 1)
                dve.wait_ge(*t.full(f"gates {l}"))
                ps = bank_of(f"gates {l}")
                TTn(gts[:, :, :, :].rearrange("p (t d) k h -> p t (d k h)", d=2),
                    ps[:, 0:TT * 16].rearrange("p (t c) -> p t c", c=16),
                    cols(f"bgates_{l}").unsqueeze(1).broadcast_to([P, TT, 16]), ALU.add
                    ).then_inc(read_of(f"gates {l}"), 1)
                dve.wait_ge(*t.read(f"gates {l}"))
                forget, inputg = gts[:, :, 1, :], gts[:, :, 0, :]
                STT(g_tmp[:, 0], forget, -1.0, forget, ALU.mult, ALU.min).then_inc(gate_arg, 1)
                dve.wait_ge(*t.next(conv_hi))
                TTn(u_lo[:, 0:CT, 0:W], conv[:, :, 0:W], u_hi[:, 0:CT, 0:W].bitcast(f32),
                    ALU.subtract).then_inc(conv_lo, 1)
                dve.wait_ge(*t.next(gate_log))
                STT(lf[:, :, :], forget, 0.0, g_tmp[:, 0], ALU.min, ALU.subtract).then_inc(logf_ready, 1)
                for tt in range(TT if l == 0 else 2):
                    dve.wait_ge(*t.full(f"kT {l} {tt}"))
                    ps = bank_of(f"kT {l} {tt}")
                    nc.vector.tensor_copy(kT[:, :, tt * P:tt * P + P], ps[:, :].rearrange("p (h s) -> p h s", h=HEADS)
                                          ).then_inc(read_of(f"kT {l} {tt}"), 1)
                dve.wait_ge(*t.full(f"cum {l}"))
                ps = bank_of(f"cum {l}")
                nc.vector.tensor_copy(cum[:, :, :, :].rearrange("p a b c -> p (a b c)"), ps[:, 0:64]
                                      ).then_inc(read_of(f"cum {l}"), 1)
                dve.wait_ge(*t.read(f"cum {l}"))
                chain(TTn(gg[:, :, :], inputg, cum[:, 0], ALU.subtract))

                def diagonal(src, a, slot):
                    return TTn(diag[:, slot, :].rearrange("p (h s) -> p h s", h=HEADS),
                               ident.unsqueeze(1).broadcast_to([P, HEADS, P]),
                               wide(src[:, a, :], P, [P, HEADS, P]), ALU.mult)

                for a in range(2):
                    diagonal(gg, a, a).then_inc(diag_ready, 1)
                for a in range(2 * TT):
                    dve.wait_ge(*t.full(f"G {l} {a}"))
                    ps = bank_of(f"G {l} {a}")[:, :].rearrange("p (h s) -> p h s", h=HEADS)
                    nc.vector.tensor_reduce(gmax[:, a, :], ps, AX.X, ALU.max)
                    TTn(t512[:, :].rearrange("p (h s) -> p h s", h=HEADS), ps,
                        masks["A", a % 2].unsqueeze(1).broadcast_to([P, HEADS, P]), ALU.add
                        ).then_inc(read_of(f"G {l} {a}"), 1)
                    if a + 2 < 2 * TT:
                        diagonal(gg, a + 2, a % 2).then_inc(diag_ready, 1)
                    dve.wait_ge(*t.read(f"G {l} {a}"))
                    chain(nc.vector.tensor_reduce(pmax[:, a, :], t512[:, :].rearrange("p (h s) -> p h s", h=HEADS),
                                                  AX.X, ALU.max))
                for kk in range(4):
                    for d in range(2):
                        a = 2 * LAT_STEPS[d][kk] + d
                        if kk == 0:
                            chain(nc.vector.memset(mprev[:, a, :], 0.0))
                        TTn(m_t[:, a, :], pmax[:, a, :], mprev[:, a, :], ALU.max)
                        chain(TTn(m_l[:, a, :], gmax[:, a, :], mprev[:, a, :], ALU.max))
                        if kk < 3:
                            nxt = 2 * LAT_STEPS[d][kk + 1] + d
                            chain(TTn(mprev[:, nxt, :], cum[:, 1, a, :], m_l[:, a, :], ALU.add))
                TTn(e_in[:, 0], mprev[:, :, :], m_t[:, :, :], ALU.subtract)
                TTn(e_in[:, 1], gg[:, :, :], m_l[:, :, :], ALU.subtract)
                TTn(e_in[:, 2], mprev[:, :, :], m_l[:, :, :], ALU.subtract)
                STT(e_in[:, 3], cum[:, 0], -1.0, m_t[:, :, :], ALU.mult, ALU.subtract).then_inc(exp_arg, 1)
                dve.wait_ge(*t.next(exp_arg))
                dve.wait_ge(*t.next(exp_done))

                for tt in range(TT):
                    dve.wait_ge(*t.read(f"k {l} {tt}"))
                for tt, d, kk in scan_steps():
                    a = 2 * tt + d
                    if l == 0 or tt < 2:
                        diagonal(m_t, a, 0).then_inc(diag_ready, 1)
                    if kk < 3:
                        TTn(kw[:, :].rearrange("p (h s) -> p h s", h=HEADS),
                            k[:, tt, :].rearrange("p (h s) -> p h s", h=HEADS),
                            wide(e_out[:, 1, a, :], P, [P, HEADS, P]), ALU.mult).then_inc(kw_ready, 1)
                    if l == 0 or tt < 2:
                        name = f"M {l} {tt} {d}"
                        dve.wait_ge(*t.full(name))
                        ps = bank_of(name)
                        STT(t512[:, :].rearrange("p (h s) -> p h s", h=HEADS),
                            ps[:, :].rearrange("p (h s) -> p h s", h=HEADS), -1.0,
                            masks["D", d].unsqueeze(1).broadcast_to([P, HEADS, P]), ALU.mult, ALU.add
                            ).then_inc(read_of(name), 1)
                        dve.wait_ge(*t.next(decay_ready))
                        name = f"S {l} {tt} {d}"
                        dve.wait_ge(*t.full(name))
                        ps = bank_of(name)
                        TTn(prob[:, :], ps[:, :], decay[:, :], ALU.mult).then_inc(read_of(name), 1)
                        for part in range(2):
                            name = f"num {l} {tt} {d} {part}"
                            dve.wait_ge(*t.full(name))
                            ps = bank_of(name)[:, :].rearrange("p (h s) -> p h s", h=2)[:, :, 0:HE]
                            dst = u_sum[:, 2 * part:2 * part + 2, :]
                            if kk:
                                dve.wait_ge(*t.read(f"int {l} {tt} {d} {part}"))
                                ins = TTn(dst, ps, inter[:, 2 * part:2 * part + 2, :], ALU.add)
                            else:
                                ins = nc.vector.tensor_copy(dst, ps)
                            ins.then_inc(read_of(name), 1)
                            dve.wait_ge(*t.read(name))
                        den = u_sum[:, :, HD]
                        chain(STT(small[:, 0, :], den, -1.0, den, ALU.mult, ALU.max))
                        chain(TTn(small[:, 1, :], small[:, 0, :], e_out[:, 3, a, :], ALU.max))
                        chain(nc.vector.reciprocal(small[:, 2, :], small[:, 1, :]))
                        later = 2 * LAT_STEPS[1 - d].index(tt) + 1 - d < 2 * kk + d
                        for hd in range(HEADS):
                            dst = hacc[:, tt, hd * P:hd * P + P]
                            if later:
                                last = STT(dst, u_sum[:, hd, 0:HD], small[:, 2, hd:hd + 1], dst, ALU.mult, ALU.add)
                            else:
                                last = nc.vector.tensor_scalar(dst, u_sum[:, hd, 0:HD], small[:, 2, hd:hd + 1], None,
                                                               ALU.mult)
                        chain(last)
                    if kk < 3:
                        for part in range(2):
                            name = f"upd {l} {tt} {d} {part}"
                            dve.wait_ge(*t.full(name))
                            ps = bank_of(name)
                            for j in range(2):
                                hd = 2 * part + j
                                src = ps[:, 256 * j:256 * j + HE]
                                if kk:
                                    last = STT(state[:, d, hd, :], state[:, d, hd, :], e_out[:, 2, a, hd:hd + 1], src,
                                               ALU.mult, ALU.add)
                                else:
                                    last = nc.vector.tensor_copy(state[:, d, hd, :], src)
                            last.then_inc(read_of(name), 1)
                            dve.wait_ge(*t.read(name))
                for tt in range(TT if l == 0 else 2):
                    dve.wait_ge(*t.read(f"o {l} {tt}"))
                    hv = hacc[:, tt, :].rearrange("p (h s) -> p h s", h=HEADS)
                    chain(TTn(t512[:, :], hacc[:, tt, :], hacc[:, tt, :], ALU.mult))
                    nc.vector.tensor_reduce(small[:, 0, :], t512[:, :].rearrange("p (h s) -> p h s", h=HEADS), AX.X,
                                            ALU.add).then_inc(sumsq_ready, 1)
                    dve.wait_ge(*t.next(root_ready))
                    chain(nc.vector.reciprocal(small[:, 2, :], small[:, 1, :]))
                    chain(TTn(hv, hv, wide(small[:, 2, :], P, [P, HEADS, P]), ALU.mult))
                    TTn(hacc[:, tt, :], hacc[:, tt, :], o[:, tt, :], ALU.mult).then_inc(merged, 1)
                for tt in range(TT if l == 0 else 2):
                    name = f"yT {l} {tt}"
                    dve.wait_ge(*t.full(name))
                    ps = bank_of(name)
                    dve.wait_ge(*t.next(y_hi_done))
                    for hd in range(HEADS):
                        c = slice(tt * P, tt * P + P)
                        last = STT(u_lo[:, CT + hd, c], ps[:, hd * P:hd * P + P], cols(f"mnorm_{l}")[:, hd:hd + 1],
                                   u_hi[:, CT + hd, c].bitcast(f32), ALU.mult, ALU.subtract)
                    last.then_inc(read_of(name), 1)
                u = UNIT_AT[f"out{l}"]
                for c in range(4):
                    split_to(u + c + 2)
                    for j in range(2):
                        residual(f"out {l} {c} {j}", 2 * c + j, W, l, 2)
                norm(f"2 {l}", W)
                if l == 0:
                    def group(g, base):
                        nf = GROUPS[g]
                        for c in range(nf + 4):
                            split(base + c)
                            if c and c % 2 == 0 and c <= nf:
                                dve.wait_ge(*t.next(hid_lo_ready, 2))
                            if c < nf and c % 2:
                                for j in range(2):
                                    dve.wait_ge(*t.full(f"ffn {g} {c} {j}"))
                                    ps = bank_of(f"ffn {g} {c} {j}")
                                    dve.wait_ge(*t.read(f"ffn {g} {c - 1} {j}"))
                                    TTn(hid0[:, j, :], ps[:, :], sil0[:, j, :], ALU.mult
                                        ).then_inc(read_of(f"ffn {g} {c} {j}"), 1)
                                for j in range(2):
                                    dve.wait_ge(*t.next(hid_hi_ready))
                                    TTn(hid_lo[:, c - 1 + j, :], hid0[:, j, :], hid_hi[:, c - 1 + j, :].bitcast(f32),
                                        ALU.subtract).then_inc(hid_lo_ready, 1)
                            if c >= nf:
                                for j in range(2):
                                    residual(f"ffn {g} {c} {j}", 2 * (c - nf) + j, NT, 0, 5)
                    with t.loop(2, unit_loops("ffn", {**fill_loops("ffn"), hid_hi_ready: 8, hid_lo_ready: 8}), 2):
                        group(0, ahead[0])
                    ahead[0] += 24
                    group(2, ahead[0])
                    ahead[0] += 10

            dve.wait_ge(*t.full("logits"))
            ps = bank_of("logits")
            nc.vector.tensor_copy(lg[:, :, :].rearrange("p t e -> p (t e)"), ps[:, 0:2 * NE]
                                  ).then_inc(read_of("logits"), 1)
            dve.wait_ge(*t.read("logits"))
            shape = [P, 2, NE]
            rank = cols("rank").unsqueeze(1).broadcast_to(shape)
            for i, one in enumerate((one1, one2)):
                chain(nc.vector.tensor_reduce(s2[:, i, :], lg[:, :, :], AX.X, ALU.max))
                chain(TTn(sc8[:, 0], lg[:, :, :], wide(s2[:, i, :], NE, shape), ALU.is_equal))
                chain(TTn(sc8[:, 1], sc8[:, 0], rank, ALU.mult))
                chain(nc.vector.tensor_reduce(s2[:, 7, :], sc8[:, 1], AX.X, ALU.max))
                chain(TTn(one[:, :, :], sc8[:, 1], wide(s2[:, 7, :], NE, shape), ALU.is_equal))
                if i == 0:
                    chain(STT(lg[:, :, :], one[:, :, :], NEG, lg[:, :, :], ALU.mult, ALU.add))
            TTn(sel[:, :, :], one1[:, :, :], one2[:, :, :], ALU.add).then_inc(sel_ready, 1)
            TTn(s2[:, 2, :], s2[:, 1, :], s2[:, 0, :], ALU.subtract).then_inc(route_arg, 1)
            dve.wait_ge(*t.next(route_exp))
            chain(nc.vector.tensor_scalar(s2[:, 4, :], s2[:, 3, :], 1.0, None, ALU.add))
            chain(nc.vector.reciprocal(s2[:, 5, :], s2[:, 4, :]))
            chain(TTn(s2[:, 6, :], s2[:, 5, :], s2[:, 3, :], ALU.mult))
            TTn(sc8[:, 2], one1[:, :, :], wide(s2[:, 5, :], NE, shape), ALU.mult)
            chain(TTn(sc8[:, 3], one2[:, :, :], wide(s2[:, 6, :], NE, shape), ALU.mult))
            chain(TTn(gate[:, :, :], sc8[:, 2], sc8[:, 3], ALU.add))
            dve.wait_ge(*t.full("count"))
            ps = bank_of("count")
            chain(nc.vector.tensor_reduce(s2[:, 7, 0:1], ps[:, 16:24], AX.X, ALU.max))
            nc.vector.tensor_scalar(npass[0:1, 0:1], s2[0:1, 7, 0:1], float(P), 1.0, ALU.is_gt, ALU.add
                                    ).then_inc(npass_ready, 1)
            dve.wait_ge(*t.next(npass_ready))
            dve.wait_ge(*t.next(sel_ready))
            TTn(sc8[:, 4], ps[:, 0:16].rearrange("p (t e) -> p t e", t=2), sel[:, :, :], ALU.mult
                ).then_inc(read_of("count"), 1)
            dve.wait_ge(*t.read("count"))
            chain(nc.vector.tensor_scalar(slot_of[:, :, :], sc8[:, 4], -1.0, None, ALU.add))
            for i in range(1, 8, 2):
                dve.wait_ge(*t.full(f"utok {i}"))
                ps = bank_of(f"utok {i}")
                tt, half = i // 4, i // 2 % 2
                nc.vector.tensor_copy(utok_lo[:, tt, 512 * half:512 * half + 512], ps[:, :]
                                      ).then_inc(read_of(f"utok {i}"), 1)
            passes = dve.value_load(npass[0:1, 0:1], min_val=1, max_val=2)

            def gathered(name, i):
                dve.wait_ge(*t.full(name))
                ps = bank_of(name)
                nc.vector.tensor_copy(xe_lo[:, 2 * i - 2:2 * i + 2, :], ps[:, :].rearrange("p (k s) -> p k s", k=4)
                                      ).then_inc(read_of(name), 1)

            chain(nc.vector.memset(pick[:, :, NE, :].bitcast(f32), 0.0))
            per_expert = {dve_chain: 1, y_hi_ready: 1, hT_hi_ready: len(CHUNKS)}
            per_pass = {y_hi_ready: NE, hT_hi_ready: NE * len(CHUNKS), dve_chain: 1 + NE, pick_ready: 1}
            with t.loop(passes, {**unit_loops("pass", fill_loops("pass")), **per_pass}, 1):
                for tt in range(2):
                    last = TTn(pick[:, tt, 0:NE, :], cols("iota").unsqueeze(1).broadcast_to([P, NE, P]),
                               wide(slot_of[:, tt, :], P, [P, NE, P]), ALU.is_equal)
                last.then_inc(pick_ready, 1)
                dve.wait_ge(*t.next(pick_ready))
                chain(nc.vector.tensor_scalar(slot_of[:, :, :], slot_of[:, :, :], -float(P), None, ALU.add))
                for i in (1, 3):
                    gathered(f"gather {i}", i)
                dve.wait_ge(*t.full("gslot"))
                ps = bank_of("gslot")
                nc.vector.tensor_copy(gslot[:, :], ps[:, 0:NE]).then_inc(read_of("gslot"), 1)
                with t.loop(NE, {**unit_loops("expert", fill_loops("expert")), **per_expert}, NE) as e:
                    for j, (m, c, part) in enumerate(EXPERT_UNITS):
                        split(ahead[0] + j)
                        if j == 0:
                            dve.wait_ge(*t.read("gslot"))
                            chain(nc.vector.tensor_copy(gcol[:, :], gslot[:, ds(e, 1)]))
                        last_part = j + 1 == UPE or EXPERT_UNITS[j + 1][:2] != (m, c)
                        if m == "w3" and last_part:
                            dve.wait_ge(*t.full(f"w3 {c}"))
                            ps, w = bank_of(f"w3 {c}"), CHUNKS[c]
                            dve.wait_ge(*t.read(f"w1 {c}"))
                            TTn(hid[:, c % 2, 0:w], ps[:, 0:w], sil[:, c % 2, 0:w], ALU.mult
                                ).then_inc(read_of(f"w3 {c}"), 1)
                        if (m == "w1" and last_part and c) or j == UPE - 2:
                            c_t = c - 1 if m == "w1" else len(CHUNKS) - 1
                            n_t = CHUNKS[c_t] // P
                            dve.wait_ge(*t.full(f"T {c_t}"))
                            ps = bank_of(f"T {c_t}")
                            dve.wait_ge(*t.next(hT_hi_ready))
                            TTn(hT_lo[:, c_t % 2, 0:n_t, :], ps[:, 0:n_t * P].rearrange("p (k s) -> p k s", k=n_t),
                                hT_hi[:, c_t % 2, 0:n_t, :].bitcast(f32), ALU.subtract
                                ).then_inc(read_of(f"T {c_t}"), 1)
                        if j == UPE - 2:
                            for i in (1, 3):
                                gathered(f"next {i}", i)
                        if j == UPE - 1:
                            dve.wait_ge(*t.next(y_hi_ready))
                            for half in range(2):
                                c_ = slice(512 * half, 512 * half + 512)
                                dve.wait_ge(*t.full(f"y {half}"))
                                ps = bank_of(f"y {half}")
                                STT(y_lo[:, c_], ps[:, :], gcol[:, :], y_hi[:, c_].bitcast(f32),
                                    ALU.mult, ALU.subtract).then_inc(read_of(f"y {half}"), 1)
                            for i in range(4):
                                dve.wait_ge(*t.full(f"back {i}"))
                                ps = bank_of(f"back {i}")
                                for s in range(2):
                                    kt = 2 * i + s
                                    last = STT(h[:, kt, 0:SEQ], ps[:, 256 * s:256 * s + 256],
                                               mod_col(1, 5, kt, 0), h[:, kt, 0:SEQ], ALU.mult, ALU.add)
                                last.then_inc(read_of(f"back {i}"), 1)
                                dve.wait_ge(*t.read(f"back {i}"))
            t.loops.append((passes - 1, {**fill_loops("pass"), dve_chain: per_pass[dve_chain]}))
            norm("f", SEQ, final=True)

        @block.tensor
        def _(pe):
            t = Counts(pe)
            mm = nc.tensor.matmul

            def mm3(dst, a_hi, a_lo, b_hi, b_lo, start, stop):
                mm(dst, a_hi, b_hi, start=start, stop=False)
                mm(dst, a_hi, b_lo, start=False, stop=False)
                return mm(dst, a_lo, b_hi, start=False, stop=stop)

            def arrived(n):
                pe.wait_ge(lo_ready, t.at(lo_ready, n + 1))
                return n % SLOTS

            pe.wait_ge(*t.next(small_lo, DEPTH + 2))
            psum = bank[7]

            def ada(n, i):
                sl = arrived(n)
                for j in range(2):
                    tile = i * 6 + (2 * (n % 3) + j)
                    for kt in range(KT):
                        for part, w in enumerate((whi, wlo)):
                            last = mm(psum[:, ds(tile * 4, 4)], w[sl][:, kt * 256 + j * P:kt * 256 + j * P + P],
                                      cond4[:, kt, :], start=kt == 0 and part == 0, stop=kt == KT - 1 and part == 1)
                last.then_inc(unit_used, 1)

            with t.loop(ADA_UNITS // 3, unit_loops("ada"), 16) as i:
                for n in range(3):
                    ada(n, i)

            def norm(tag, width, final=False):
                pe.wait_ge(*t.free(f"norm {tag}"))
                ps = bank_of(f"norm {tag}")
                for kt in range(KT):
                    pe.wait_ge(*t.next(square_ready))
                    last = mm(ps[:, 0:width], ones, square[:, kt % 2, 0:width], start=kt == 0, stop=kt == KT - 1)
                    if kt < KT - 1:
                        last.then_inc(square_used, 1)
                last.then_inc(full_of(f"norm {tag}"), 1)

            def columns(u, width, n_k, names, hi, lo, before=None):
                sl = arrived(u)
                for j in range(2):
                    pe.wait_ge(*t.free(names[j]))
                    ps = bank_of(names[j])
                    for kt in range(n_k):
                        if before:
                            before(kt)
                        w = slice(kt * 256 + j * P, kt * 256 + j * P + P)
                        last = mm3(ps[:, 0:width], whi[sl][:, w], wlo[sl][:, w], hi[:, kt, 0:width],
                                   lo[:, kt, 0:width], kt == 0, kt == n_k - 1)
                last.then_inc(unit_used, 1)

            for l in range(DEPTH):
                W = NT if l == 0 else SEQ
                norm(f"1 {l}", NT)
                done = [0]

                def u_part(kt):
                    if done[0] <= kt:
                        pe.wait_ge(*t.next(u_lo_ready))
                        done[0] += 1

                u = UNIT_AT[f"conv{l}"]
                for c in range(6):
                    columns(u + c, W, KT, [f"conv {l} {c} {j}" for j in range(2)], u_hi, u_lo, u_part)
                u = UNIT_AT[f"qkvo{l}"]
                for c, name in enumerate("qkvo"):
                    for part in range(2):
                        sl = arrived(u + 2 * c + part)
                        for tt in range(TT if l == 0 or name in "kv" else 2):
                            if part == 0:
                                pe.wait_ge(*t.free(f"{name} {l} {tt}"))
                            ps = bank_of(f"{name} {l} {tt}")
                            for kk in range(4):
                                kt = 4 * part + kk
                                w = slice(kk * 512, kk * 512 + 512)
                                last = mm3(ps[:, :], u_hi[:, kt, tt * P:tt * P + P], u_lo[:, kt, tt * P:tt * P + P],
                                           whi[sl][:, w], wlo[sl][:, w], kt == 0, kt == KT - 1)
                        last.then_inc(unit_used, 1)
                pe.wait_ge(*t.free(f"gates {l}"))
                ps = bank_of(f"gates {l}")
                for tt in range(TT):
                    for kt in range(KT):
                        last = mm3(ps[:, tt * 16:tt * 16 + 16], u_hi[:, kt, tt * P:tt * P + P],
                                   u_lo[:, kt, tt * P:tt * P + P], wg_hi[:, l, kt, :], wg_lo[:, l, kt, :],
                                   kt == 0, kt == KT - 1)
                last.then_inc(full_of(f"gates {l}"), 1)
                for tt in range(TT if l == 0 else 2):
                    pe.wait_ge(*t.read(f"q {l} {tt}"))
                    pe.wait_ge(*t.read(f"k {l} {tt}"))
                    for name, src in ((f"qT {l} {tt}", q), (f"kT {l} {tt}", k)):
                        pe.wait_ge(*t.free(name))
                        ps = bank_of(name)
                        for hd in range(HEADS):
                            last = nc.tensor.transpose(ps[:, hd * P:hd * P + P], src[:, tt, hd * P:hd * P + P], ident)
                        last.then_inc(full_of(name), 1)
                pe.wait_ge(*t.free(f"cum {l}"))
                ps = bank_of(f"cum {l}")
                pe.wait_ge(*t.next(logf_ready))
                for d in range(2):
                    dst = ps[:, 0:32].rearrange("p (t d h) -> p t d h", d=2, h=HEADS)[:, :, d, :]
                    mm(dst, tri[d], lf[:, :, :].rearrange("p (t d) h -> p t d h", d=2)[:, :, d, :], start=True, stop=True)
                mm(ps[:, 32:64], ones, lf[:, :, :].rearrange("p a h -> p (a h)"), start=True, stop=True
                   ).then_inc(full_of(f"cum {l}"), 1)
                for a in range(2 * TT):
                    pe.wait_ge(*t.free(f"G {l} {a}"))
                    ps = bank_of(f"G {l} {a}")
                    pe.wait_ge(*t.next(diag_ready))
                    mm(ps[:, :], ones, diag[:, a % 2, :], start=True, stop=True).then_inc(full_of(f"G {l} {a}"), 1)
                for tt in range(TT if l == 0 else 2):
                    pe.wait_ge(*t.read(f"qT {l} {tt}"))
                    pe.wait_ge(*t.read(f"kT {l} {tt}"))
                for tt in range(TT):
                    pe.wait_ge(*t.read(f"v {l} {tt}"))
                pe.wait_ge(v_ones, t.at(v_ones, l + 1))
                previous = {}
                for tt, d, kk in scan_steps():
                    full = l == 0 or tt < 2
                    c = slice(tt * P, tt * P + P)
                    if full:
                        name = f"M {l} {tt} {d}"
                        pe.wait_ge(*t.free(name))
                        ps = bank_of(name)
                        pe.wait_ge(*t.next(diag_ready))
                        mm(ps[:, :], ones, diag[:, 0, :], start=True, stop=True).then_inc(full_of(name), 1)
                        name = f"S {l} {tt} {d}"
                        pe.wait_ge(*t.free(name))
                        ps = bank_of(name)
                        for hd in range(HEADS):
                            last = mm(ps[:, hd * P:hd * P + P], kT[:, hd, c], qT[:, hd, c], start=True, stop=True)
                        last.then_inc(full_of(name), 1)
                        if kk:
                            for part in range(2):
                                pe.wait_ge(*t.read(previous[d][part]))
                                name = f"int {l} {tt} {d} {part}"
                                pe.wait_ge(*t.free(name))
                                ps = bank_of(name)
                                for j in range(2):
                                    last = mm(ps[:, 256 * j:256 * j + HE], qT[:, 2 * part + j, c],
                                              state[:, d, 2 * part + j, :], start=True, stop=True)
                                last.then_inc(full_of(name), 1)
                    if kk < 3:
                        pe.wait_ge(*t.next(kw_ready))
                        for part in range(2):
                            name = f"upd {l} {tt} {d} {part}"
                            pe.wait_ge(*t.free(name))
                            ps = bank_of(name)
                            for j in range(2):
                                hd = 2 * part + j
                                last = mm(ps[:, 256 * j:256 * j + HE], kw[:, hd * P:hd * P + P], v[:, tt, hd, :],
                                          start=True, stop=True)
                            last.then_inc(full_of(name), 1)
                        previous[d] = [f"upd {l} {tt} {d} {part}" for part in range(2)]
                    if full:
                        pe.wait_ge(*t.read(f"S {l} {tt} {d}"))
                        for part in range(2):
                            name = f"num {l} {tt} {d} {part}"
                            pe.wait_ge(*t.free(name))
                            ps = bank_of(name)
                            for j in range(2):
                                hd = 2 * part + j
                                last = mm(ps[:, 256 * j:256 * j + HE], prob[:, hd * P:hd * P + P], v[:, tt, hd, :],
                                          start=True, stop=True)
                            last.then_inc(full_of(name), 1)
                for tt in range(TT if l == 0 else 2):
                    name = f"yT {l} {tt}"
                    pe.wait_ge(*t.free(name))
                    ps = bank_of(name)
                    pe.wait_ge(*t.next(merged))
                    for hd in range(HEADS):
                        last = nc.tensor.transpose(ps[:, hd * P:hd * P + P], hacc[:, tt, hd * P:hd * P + P], ident)
                    last.then_inc(full_of(name), 1)
                pe.wait_ge(*t.next(conv_lo))
                for tt in range(TT if l == 0 else 2):
                    pe.wait_ge(*t.read(f"yT {l} {tt}"))
                u = UNIT_AT[f"out{l}"]
                for c in range(4):
                    columns(u + c, W, KT, [f"out {l} {c} {j}" for j in range(2)], u_hi, u_lo)
                norm(f"2 {l}", W)
                pe.wait_ge(*t.next(u_lo_ready, KT))
                if l == 0:
                    def group(g):
                        u, nf = UNIT_AT[f"ffn{g}"], GROUPS[g]
                        for c in range(nf + 4):
                            names = [f"ffn {g} {c} {j}" for j in range(2)]
                            if c < nf:
                                columns(u + c, NT, KT, names, u_hi, u_lo)
                            else:
                                if c == nf:
                                    pe.wait_ge(*t.next(hid_lo_ready, nf))
                                columns(u + c, NT, nf, names, hid_hi, hid_lo)
                    with t.loop(2, unit_loops("ffn", {**fill_loops("ffn"), hid_lo_ready: 8}), 2):
                        group(0)
                    group(2)

            pe.wait_ge(*t.free("logits"))
            ps = bank_of("logits")
            for tt in range(2):
                for kt in range(KT):
                    c = slice(tt * P, tt * P + P)
                    last = mm3(ps[:, tt * NE:tt * NE + NE], u_hi[:, kt, c], u_lo[:, kt, c], ro_hi[:, kt, :],
                               ro_lo[:, kt, :], kt == 0, kt == KT - 1)
            last.then_inc(full_of("logits"), 1)

            def token_major(i):
                pe.wait_ge(*t.free(f"utok {i}"))
                ps = bank_of(f"utok {i}")
                tt, half, src = i // 4, i // 2 % 2, (u_hi, u_lo)[i % 2]
                for j in range(4):
                    last = nc.tensor.transpose(ps[:, j * P:j * P + P],
                                               src[:, 4 * half + j, tt * P:tt * P + P].bitcast(f32), ident)
                last.then_inc(full_of(f"utok {i}"), 1)

            for i in range(4):
                token_major(i)
            pe.wait_ge(*t.free("count"))
            ps = bank_of("count")
            pe.wait_ge(*t.next(sel_ready))
            mm(ps[:, 0:8], tri[0], sel[:, 0, :], start=True, stop=True)
            mm(ps[:, 8:16], ones, sel[:, 0, :], start=True, stop=False)
            mm(ps[:, 8:16], tri[0], sel[:, 1, :], start=False, stop=True)
            mm(ps[:, 16:24], ones, sel[:, 0, :], start=True, stop=False)
            mm(ps[:, 16:24], ones, sel[:, 1, :], start=False, stop=True).then_inc(full_of("count"), 1)
            for i in range(4, 8):
                token_major(i)
            pe.wait_ge(npass_ready, 1)
            passes = pe.value_load(npass[0:1, 0:1], min_val=1, max_val=2)
            for i in range(8):
                pe.wait_ge(*t.read(f"utok {i}"))

            def gather(names, e):
                for i in range(4):
                    src = (utok_hi, utok_lo)[i % 2]
                    pe.wait_ge(*t.free(names[i]))
                    ps = bank_of(names[i])
                    for j in range(4):
                        kt = 4 * (i // 2) + j
                        for tt in range(2):
                            last = mm(ps[:, j * P:j * P + P], src[:, tt, kt * P:kt * P + P],
                                      pick[:, tt, ds(e, 1), :].rearrange("p a s -> p (a s)") if not isinstance(e, int)
                                      else pick[:, tt, e, :], start=tt == 0, stop=tt == 1)
                    last.then_inc(full_of(names[i]), 1)

            u = UNIT_AT["moe"]
            with t.loop(passes, {**unit_loops("pass", fill_loops("pass")), pick_ready: 1,
                                 hidden_ready: 0}, 1):
                pe.wait_ge(*t.next(pick_ready))
                for i in range(4):
                    pe.wait_ge(*t.free(f"PT {i}"))
                    ps = bank_of(f"PT {i}")
                    for ee in range(2):
                        for tt in range(2):
                            c = ee * SEQ + tt * P
                            last = nc.tensor.transpose(ps[:, c:c + P], pick[:, tt, 2 * i + ee, :].bitcast(f32), ident)
                    last.then_inc(full_of(f"PT {i}"), 1)
                gather([f"gather {i}" for i in range(4)], 0)
                for i in range(4):
                    if i >= 2:
                        pe.wait_ge(*t.read(f"gather {i}"))
                    pe.wait_ge(*t.read(f"PT {i}"))
                pe.wait_ge(*t.free("gslot"))
                ps = bank_of("gslot")
                for ee in range(NE):
                    for tt in range(2):
                        last = mm(ps[:, ee:ee + 1], pick[:, tt, ee, :].bitcast(f32), gate[:, tt, ee:ee + 1],
                                  start=tt == 0, stop=tt == 1)
                last.then_inc(full_of("gslot"), 1)
                with t.loop(NE, unit_loops("expert", fill_loops("expert")), NE) as e:
                    for j, (m, c, part) in enumerate(EXPERT_UNITS):
                        last_part = j + 1 == UPE or EXPERT_UNITS[j + 1][:2] != (m, c)
                        if m != "w2":
                            w = CHUNKS[c]
                            n_k = UNIT // w
                            b = 2 * (c % 2) + (m == "w3")
                            if part == 0:
                                pe.wait_ge(*t.free(f"{m} {c}"))
                            sl = arrived(u + j)
                            for kk in range(n_k):
                                kt = part * 4 + kk
                                r = slice(kk * w, kk * w + w)
                                last = mm3(bank[b][:, 0:w], xe_hi[:, kt, :], xe_lo[:, kt, :], whi[sl][:, r],
                                           wlo[sl][:, r], kt == 0, kt == KT - 1)
                        else:
                            if j == 8:
                                pe.wait_ge(*t.free("y 0"))
                                pe.wait_ge(*t.free("y 1"))
                            if part == 0:
                                pe.wait_ge(*t.read(f"T {c}"))
                            sl = arrived(u + j)
                            for kk in range(2):
                                ft = 2 * part + kk
                                for half in range(2):
                                    r = slice(kk * 1024 + half * 512, kk * 1024 + half * 512 + 512)
                                    last = mm3(bank[6 + half][:, :], hT_hi[:, c % 2, ft, :], hT_lo[:, c % 2, ft, :],
                                               whi[sl][:, r], wlo[sl][:, r], c == 0 and ft == 0,
                                               j == UPE - 1 and kk == 1)
                        last.then_inc(unit_used, 1)
                        if (m == "w1" and last_part and c) or j == UPE - 2:
                            c_t = c - 1 if m == "w1" else len(CHUNKS) - 1
                            pe.wait_ge(*t.read(f"w3 {c_t}"))
                            pe.wait_ge(*t.free(f"T {c_t}"))
                            ps = bank_of(f"T {c_t}")
                            for ft in range(CHUNKS[c_t] // P):
                                last = nc.tensor.transpose(ps[:, ft * P:ft * P + P],
                                                           hid[:, c_t % 2, ft * P:ft * P + P], ident)
                            last.then_inc(full_of(f"T {c_t}"), 1)
                        if j == UPE - 2:
                            gather([f"next {i}" for i in range(4)], e + 1)
                        if j == UPE - 1:
                            pe.wait_ge(*t.read("y 0"))
                            pe.wait_ge(*t.read("y 1"))
                            for i in range(4):
                                pe.wait_ge(*t.free(f"back {i}"))
                                ps = bank_of(f"back {i}")
                                for s in range(2):
                                    kt = 2 * i + s
                                    for part_, y in enumerate((y_hi, y_lo)):
                                        last = mm(ps[:, 256 * s:256 * s + 256], y[:, kt * P:kt * P + P],
                                                  pickT[:, ds(e, 1), :].rearrange("p a n -> p (a n)"),
                                                  start=part_ == 0, stop=part_ == 1)
                                last.then_inc(full_of(f"back {i}"), 1)
            t.loops.append((passes - 1, fill_loops("pass")))
            norm("f", SEQ, final=True)

        @block.gpsimd
        def _(pool):
            pass


def kernel(**inputs):
    import numpy as _np
    import concourse.bacc as _bacc
    from concourse import mybir as _mybir
    from concourse.bass_utils import run_bass_kernel_spmd as _run

    a = {name: _np.asarray(x) for name, x in inputs.items()}
    f32 = _np.float32

    stream = _np.zeros((N_UNITS + 2, P, UNIT), f32)
    at = [0]

    def put(block):
        rows, n = block.shape
        w = rows // P * n
        stream[at[0], :, 0:w].reshape(P, rows // P, n)[:] = block.reshape(rows // P, P, n).transpose(1, 0, 2)
        at[0] += 1

    for l in range(DEPTH):
        for c in range(0, 6 * D, 256):
            put(a["w_ada"][l][:, c:c + 256])
    for l in range(DEPTH):
        w = a["w_in"][l]
        assert at[0] == UNIT_AT[f"conv{l}"]
        for c in range(CT):
            s = slice(c * P, c * P + P)
            put(_np.concatenate([w[:, CONV:2 * CONV][:, s], w[:, 2 * CONV:3 * CONV][:, s]], axis=1))
        for c in range(2):
            put(w[:, 256 * c:256 * c + 256])
        q0 = 3 * CONV
        for c0 in (q0, q0 + 512, q0 + 1024, q0 + 1536 + 16):
            for half in range(2):
                put(w[512 * half:512 * half + 512, c0:c0 + 512])
        for c in range(4):
            put(a["w_out"][l][:, 256 * c:256 * c + 256])
        if l == 0:
            f0 = 0
            for nf in GROUPS:
                for c in range(f0, f0 + nf * P, 256):
                    put(a["ffn_w1"][0][:, c:c + 256])
                    put(a["ffn_w3"][0][:, c:c + 256])
                for c in range(4):
                    put(a["ffn_w2"][0][f0:f0 + nf * P, 256 * c:256 * c + 256])
                f0 += nf * P
    for e in range(NE):
        for m, c, part in EXPERT_UNITS:
            f0, w = 512 * c, CHUNKS[c]
            if m == "w2":
                put(a["moe_w2"][0, e][f0 + 256 * part:f0 + 256 * part + 256])
            elif w == 512:
                put(a["moe_" + m][0, e][512 * part:512 * part + 512, f0:f0 + w])
            else:
                put(a["moe_" + m][0, e][:, f0:f0 + w])
    assert at[0] == N_UNITS
    stream[N_UNITS:] = stream[UNIT_AT["moe"]:UNIT_AT["moe"] + 2]

    tokens = _np.concatenate([a["x"][0], a["ctx"][0]]).T.reshape(KT, P, NT).transpose(1, 0, 2)
    params = _np.zeros((P, NPAR), f32)

    def param(name, block):
        lo, hi = COL[name]
        params[:, lo:hi] = _np.broadcast_to(block, (P, hi - lo))

    def by_channel(x):
        x = x.reshape(-1, P, x.shape[1] if x.ndim > 1 else 1)
        return x.transpose(1, 0, 2).reshape(P, -1)

    row, col = _np.arange(P)[:, None], _np.arange(P)[None, :]
    param("ident", _np.eye(P, dtype=f32))
    param("ones", f32(1))
    param("mask_low", _np.where(col <= row, f32(0), f32(NEG)))
    param("mask_up", _np.where(col >= row, f32(0), f32(NEG)))
    param("up01", (row <= col).astype(f32))
    param("low01", (row >= col).astype(f32))
    param("iota", _np.arange(P, dtype=f32))
    param("rank", _np.arange(NE, 0, -1).astype(f32))
    param("eps", f32(EPS))
    param("cond", by_channel(_np.stack([a["c"][0], a["c_ctx"]], axis=1)))
    param("final_g", by_channel(a["final_norm_g"]))
    param("router", by_channel(a["moe_router"][0]))
    param("b_ada", by_channel(a["b_ada"].reshape(-1)))
    for l in range(DEPTH):
        param(f"norm1_{l}", by_channel(a["norm1_g"][l]))
        param(f"norm2_{l}", by_channel(a["norm2_g"][l]))
        param(f"conv_{l}", by_channel(a["conv_w"][l].T))
        param(f"mnorm_{l}", by_channel(a["mlstm_norm_g"][l]))
        param(f"bgates_{l}", a["b_gates"][l].reshape(-1))
        param(f"wgates_{l}", by_channel(a["w_in"][l][:, 3 * CONV + 1536:3 * CONV + 1552]))

    nc = _bacc.Bacc("TRN2", target_bir_lowering=False, num_devices=1)
    arrays = {"stream": stream, "tokens": _np.ascontiguousarray(tokens), "params": params}
    args = [nc.dram_tensor(name, x.shape, _mybir.dt.from_np(x.dtype), kind="ExternalInput").ap()
            for name, x in arrays.items()]
    out = nc.dram_tensor("out", (P, KT, SEQ), _mybir.dt.float32, kind="ExternalOutput").ap()
    backbone(nc, *args, out)
    r = _run(nc, [arrays], core_ids=[0])
    got = r.results[0]["out"]
    return _np.ascontiguousarray(got.transpose(2, 1, 0)).reshape(1, SEQ, D)
```

```python
from contextlib import ExitStack, contextmanager

import numpy as np
import concourse.bass as bass
from concourse import mybir

P = 128
D = 1024
KT = D // P
SEQ, CTX = 256, 256
NT = SEQ + CTX
TT = NT // P
GRID_W = 64
CONV = 512
CT = CONV // P
HEADS, HD = 4, 128
DFF = 2816
FT = DFF // P
NE = 8
DEPTH = 2
EPS = 1e-6
NEG = -1e30
UNIT = 2048
SLOTS = 3
HALVES = [slice(0, UNIT // 2), slice(UNIT // 2, UNIT)]
HE = HD + 1
GROUPS = [8, 8, 6]
CHUNKS = [512] * 5 + [256]
UPE = 33
ADA_UNITS = DEPTH * 6 * D // 256
LAT_STEPS = {0: [2, 3, 0, 1], 1: [3, 2, 1, 0]}

PARAMS = [("ident", P), ("ones", P), ("mask_low", P), ("mask_up", P), ("up01", P), ("low01", P), ("iota", P),
          ("rank", NE), ("comb", 2), ("eps", 1), ("cond", KT * 2), ("final_g", KT), ("router", KT * NE), ("b_ada", DEPTH * 48)]
for _l in range(DEPTH):
    PARAMS += [(f"norm1_{_l}", KT), (f"norm2_{_l}", KT), (f"conv_{_l}", CT * 3), (f"mnorm_{_l}", CT),
               (f"bgates_{_l}", 16), (f"wgates_{_l}", KT * 16)]
COL, _n = {}, 0
for _name, _w in PARAMS:
    COL[_name] = (_n, _n + _w)
    _n += _w
NPAR = _n


def expert_units():
    out = []
    for c, w in enumerate(CHUNKS):
        parts = 2 if w == 512 else 1
        out += [("w1", c, h) for h in range(parts)] + [("w3", c, h) for h in range(parts)]
        if c:
            out += [("w2", c - 1, h) for h in range(2)]
    return out + [("w2", len(CHUNKS) - 1, 0)]


EXPERT_UNITS = expert_units()
assert len(EXPERT_UNITS) == UPE
LAST_CHUNK = len(CHUNKS) - 1
T_AT = {j: c - 1 for j, (m, c, part) in enumerate(EXPERT_UNITS)
        if m == "w1" and c and EXPERT_UNITS[j + 1][:2] != (m, c)}
NEXT_AT = EXPERT_UNITS.index(("w3", LAST_CHUNK, 0))
T_AT[NEXT_AT + 1] = LAST_CHUNK
BACK_AT = 1


def first_units():
    at, n = {}, 0
    for name, k in ([("ada", ADA_UNITS), ("conv0", 6), ("qkvo0", 8), ("out0", 4)]
                    + [(f"ffn{g}", f + 4) for g, f in enumerate(GROUPS)]
                    + [("conv1", 6), ("qkvo1", 8), ("out1", 4), ("moe", NE * UPE)]):
        at[name] = n
        n += k
    return at, n


UNIT_AT, N_UNITS = first_units()
assert (N_UNITS + 2) % SLOTS == 0 and NE * UPE % SLOTS == 0


class Fills:

    def __init__(self):
        self.n, self.at = [0] * 16, {}

    def add(self, name, bank, unit=None):
        self.n[bank] += 1
        if unit is None:
            self.n[8 + bank] += 1
        self.at[name] = (bank, self.n[bank], unit, self.n[8 + bank])

    def repeat(self, before, trips):
        per = [b - a for a, b in zip(before, self.n)]
        self.n = [b + (trips - 1) * p for b, p in zip(self.n, per)]
        return per


def plan_fills():
    f, per = Fills(), {}
    f.add("mod", 7, ADA_UNITS - 1)
    before = list(f.n)
    for c in range(3):
        f.add(f"ada {c}", c, 2 * c + 1)
    per["ada"] = f.repeat(before, ADA_UNITS // 6)

    def norm(tag):
        f.add(f"norm {tag}", 0)

    for l in range(DEPTH):
        norm(f"1 {l}")
        u = UNIT_AT[f"conv{l}"]
        for k in range(6):
            for j in range(2):
                f.add(f"conv {l} {k} {j}", 2 * (k % 4) + j, u + k)
        u = UNIT_AT[f"qkvo{l}"]
        for c, name in enumerate("qkvo"):
            for t in range(TT if l == 0 or name in "kv" else 2):
                f.add(f"{name} {l} {t}", 4 * (c % 2) + t, u + 2 * c + 1)
        f.add(f"gates {l}", 0)
        for t in range(TT):
            if l == 0 or t < 2:
                f.add(f"qT {l} {t}", 4 + t)
                f.add(f"kT {l} {t}", t)
        f.add(f"cum {l}", 0)
        for a in range(2 * TT):
            f.add(f"G {l} {a}", a % 2)
        for t, d, k in scan_steps():
            if l == 0 or t < 2:
                f.add(f"M {l} {t} {d}", 0)
                f.add(f"S {l} {t} {d}", 1)
                f.add(f"num {l} {t} {d} 0", 2)
                f.add(f"num {l} {t} {d} 1", 3)
                if k:
                    f.add(f"int {l} {t} {d} 0", 4)
                    f.add(f"int {l} {t} {d} 1", 5)
            if k < 3:
                f.add(f"upd {l} {t} {d} 0", 6)
                f.add(f"upd {l} {t} {d} 1", 7)
        for t in range(TT if l == 0 else 2):
            f.add(f"yT {l} {t}", t)
        for k in range(4):
            for j in range(2):
                f.add(f"out {l} {k} {j}", 2 * (k % 4) + j, UNIT_AT[f"out{l}"] + k)
        norm(f"2 {l}")
        if l == 0:
            def group(g):
                u, nf = UNIT_AT[f"ffn{g}"], GROUPS[g]
                for k in range(nf + 4):
                    for j in range(2):
                        f.add(f"ffn {g} {k} {j}", 2 * (k % 4) + j, u + k)
            before = list(f.n)
            group(0)
            per["ffn"] = f.repeat(before, 2)
            group(2)
    f.add("logits", 0)
    f.add("count", 1)
    for i in range(8):
        f.add(f"utok {i}", 2 + i % 4)
    before_pass = list(f.n)
    for i in range(4):
        f.add(f"PT {i}", i)
    f.add("gslot", 6)
    for i in range(4):
        f.add(f"gather {i}", 4 + i % 2)
    before, u = list(f.n), UNIT_AT["moe"]
    aux = 0
    for j, (m, c, h) in enumerate(EXPERT_UNITS):
        last = j + 1 == UPE or EXPERT_UNITS[j + 1][:2] != (m, c)
        if m != "w2" and last:
            f.add(f"{m} {c}", 2 * (c % 2) + (m == "w3"), u + j)
        if j == UPE - 1:
            f.add("y 0", 6, u + j)
            f.add("y 1", 7, u + j)
        if j == BACK_AT:
            for i in range(4):
                f.add(f"back {i}", 4 + i % 2)
        if j in T_AT:
            f.add(f"T {T_AT[j]}", 4 + T_AT[j] % 2)
        if j == NEXT_AT:
            for i in range(4):
                f.add(f"next {i}", (5, 4, 0, 1)[i])
    per["expert"] = f.repeat(before, NE)
    for i in range(4):
        f.add(f"final back {i}", 4 + i % 2)
    per["pass"] = [b - a for a, b in zip(before_pass, f.n)]
    f.add("norm f", 0)
    return f, per


def scan_steps():
    return [(LAT_STEPS[d][k], d, k) for k in range(4) for d in range(2)]


FILLS, FILLS_PER = plan_fills()


def backbone(nc, stream, tokens, params, out):
    f32, f32r, i32 = mybir.dt.float32, mybir.dt.float32r, mybir.dt.int32
    ACT, ALU, AX = mybir.ActivationFunctionType, mybir.AluOpType, mybir.AxisListType
    ds = bass.ds

    ctx = ExitStack()
    with ctx:
        def tensors(stack):
            def sb(name, shape, dt=f32):
                return stack.enter_context(nc.sbuf_tensor(name, shape, dt))
            return sb

        sb = tensors(ctx)
        raw = [sb(f"raw{i}", [P, UNIT]) for i in range(SLOTS)]
        whi = [sb(f"whi{i}", [P, UNIT], f32r) for i in range(SLOTS)]
        wlo = [sb(f"wlo{i}", [P, UNIT], f32r) for i in range(SLOTS)]
        h = sb("h", [P, KT, NT])
        u_hi = sb("u_hi", [P, KT, NT], f32r)
        u_lo = sb("u_lo", [P, KT, NT], f32r)
        par = sb("par", [P, NPAR])
        cond4 = sb("cond4", [P, KT, 4], f32r)
        condf = sb("condf", [P, KT, 2])
        wg_hi = sb("wg_hi", [P, DEPTH, KT, 16], f32r)
        wg_lo = sb("wg_lo", [P, DEPTH, KT, 16], f32r)
        ro_hi = sb("ro_hi", [P, KT, NE], f32r)
        ro_lo = sb("ro_lo", [P, KT, NE], f32r)
        mod = sb("mod", [P, DEPTH * 48, 2])
        gain = sb("gain", [P, DEPTH, 2, KT, 2])
        npass = sb("npass", [1, 1], i32)
        with ExitStack() as stack:
            sb = tensors(stack)
            ada_row = sb("ada_row", [4, 3, 512])
        with ExitStack() as stack:
            sb = tensors(stack)
            square = sb("square", [P, 2, NT])
            std = sb("std", [P, NT])
            rstd = sb("rstd", [P, NT])
            scaled = sb("scaled", [P, 2, NT])
            modded = sb("modded", [P, 2, NT])
            result = sb("result", [P, KT, SEQ])
        with ExitStack() as stack:
            sb = tensors(stack)
            q = sb("q", [P, TT, 512])
            k = sb("k", [P, TT, 512])
            v = sb("v", [P, TT, HEADS, HE])
            o = sb("o", [P, TT, 512])
            qT = sb("qT", [P, HEADS, NT])
            kT = sb("kT", [P, HEADS, NT])
            conv = sb("conv", [P, CT, NT])
            hacc = q
            diag = sb("diag", [P, 2, 512])
            t512 = sb("t512", [P, 2, 512])
            inter = sb("inter", [P, HEADS, HE])
            u_sum = sb("u_sum", [P, HEADS, HE])
            kw = sb("kw", [P, 512])
            state = sb("state", [P, 2, HEADS, HE])
            hh, yprod = diag, t512[:, 0, :]
            gts = sb("gts", [P, TT * 2, 2, HEADS])
            lf = sb("lf", [P, TT * 2, HEADS])
            g_tmp = sb("g_tmp", [P, 2, TT * 2, HEADS])
            cum = sb("cum", [P, 2, TT * 2, HEADS])
            gg = sb("gg", [P, TT * 2, HEADS])
            gmax = sb("gmax", [P, TT * 2, HEADS])
            pmax = sb("pmax", [P, TT * 2, HEADS])
            mprev = sb("mprev", [P, TT * 2, HEADS])
            m_t = sb("m_t", [P, TT * 2, HEADS])
            m_l = sb("m_l", [P, TT * 2, HEADS])
            e_in = sb("e_in", [P, 4, TT * 2, HEADS])
            e_out = sb("e_out", [P, 4, TT * 2, HEADS])
            small = sb("small", [P, 3, HEADS])
            msq = sb("msq", [P, 3, TT, HEADS])
        with ExitStack() as stack:
            sb = tensors(stack)
            hid_hi = sb("hid_hi", [P, 8, NT], f32r)
            hid_lo = sb("hid_lo", [P, 8, NT], f32r)
            sil0 = sb("sil0", [P, 2, NT])
            hid0 = sb("hid0", [P, 2, NT])
        with ExitStack() as stack:
            sb = tensors(stack)
            pick = sb("pick", [P, 2, NE + 1, P], f32r)
            pickT = sb("pickT", [P, NE + 1, SEQ], f32r)
            utok_hi = sb("utok_hi", [P, 2, D], f32r)
            utok_lo = sb("utok_lo", [P, 2, D], f32r)
            xe_hi = sb("xe_hi", [P, KT, P], f32r)
            xe_lo = sb("xe_lo", [P, KT, P], f32r)
            sil = sb("sil", [P, 2, 512])
            hid = sb("hid", [P, 2, 512])
            hT_hi = sb("hT_hi", [P, 2, 4, P], f32r)
            hT_lo = sb("hT_lo", [P, 2, 4, P], f32r)
            y_hi = sb("y_hi", [P, D], f32r)
            y_lo = sb("y_lo", [P, D], f32r)
            gslot = sb("gslot", [P, NE])
            gcol = sb("gcol", [P, 1])
            lg = sb("lg", [P, 2, NE])
            sc8 = sb("sc8", [P, 6, 2, NE])
            one1 = sb("one1", [P, 2, NE])
            one2 = sb("one2", [P, 2, NE])
            gate = sb("gate", [P, 2, NE])
            sel = sb("sel", [P, 2, NE])
            slot_of = sb("slot_of", [P, 2, NE])
            s2 = sb("s2", [P, 8, 2])
        bank = [ctx.enter_context(nc.psum_tensor(f"bank{i}", [P, 512], f32)) for i in range(8)]

        def sem(name):
            return ctx.enter_context(nc.semaphore(name))

        raw_loaded = [sem(f"raw_loaded{i}") for i in range(SLOTS)]
        hi_ready, lo_ready, unit_used = sem("hi_ready"), sem("lo_ready"), sem("unit_used")
        bank_full = [sem(f"bank_full{i}") for i in range(8)]
        bank_read = [sem(f"bank_read{i}") for i in range(8)]
        params_loaded, tokens_loaded, out_stored = sem("params_loaded"), sem("tokens_loaded"), sem("out_stored")
        small_hi, small_lo = sem("small_hi"), sem("small_lo")
        cond_silu, mod_turned, mod_ready = sem("cond_silu"), sem("mod_turned"), sem("mod_ready")
        square_ready, square_used = sem("square_ready"), sem("square_used")
        scaled_ready, modded_ready, u_hi_ready, u_lo_ready = (sem("scaled_ready"), sem("modded_ready"),
                                                              sem("u_hi_ready"), sem("u_lo_ready"))
        conv_ready, conv_hi, conv_lo = sem("conv_ready"), sem("conv_hi"), sem("conv_lo")
        v_ones = sem("v_ones")
        gate_arg, gate_log, logf_ready = sem("gate_arg"), sem("gate_log"), sem("logf_ready")
        diag_ready, exp_arg, exp_done = sem("diag_ready"), sem("exp_arg"), sem("exp_done")
        decay_arg, decay_ready, kw_ready = sem("decay_arg"), sem("decay_ready"), sem("kw_ready")
        sumsq_ready, root_ready, normed, merged, y_hi_done = (sem("sumsq_ready"), sem("root_ready"), sem("normed"),
                                                              sem("merged"), sem("y_hi_done"))
        gg_ready, pmax_done, hacc_done = sem("gg_ready"), sem("pmax_done"), sem("hacc_done")
        hid_hi_ready, hid_lo_ready = sem("hid_hi_ready"), sem("hid_lo_ready")
        route_arg, route_exp, sel_ready, pick_ready, npass_ready = (
            sem("route_arg"), sem("route_exp"), sem("sel_ready"), sem("pick_ready"), sem("npass_ready"))
        silu_ready, hidden_ready, hT_hi_ready, y_hi_ready = (sem("silu_ready"), sem("hidden_ready"),
                                                             sem("hT_hi_ready"), sem("y_hi_ready"))
        result_ready = sem("result_ready")
        dve_chain, act_chain = sem("dve_chain"), sem("act_chain")

        class Counts:

            def __init__(self, eng):
                self.eng, self.n, self.loops = eng, {}, []

            def at(self, s, base):
                value = base
                for i, per in self.loops:
                    if per.get(s, 0):
                        assert base > 0, "a wait that may be for zero"
                        value = i * per[s] + value
                return value

            def next(self, s, k=1):
                self.n[s] = self.n.get(s, 0) + k
                return s, self.at(s, self.n[s])

            @contextmanager
            def loop(self, trips, per, count=None):
                before = dict(self.n)
                with self.eng.Fori(0, trips) as i:
                    self.loops.append((i, per))
                    yield i
                    self.loops.pop()
                for s, n in self.n.items():
                    step = n - before.get(s, 0)
                    assert step == per.get(s, 0), (s, step, per.get(s, 0))
                    self.n[s] += (count - 1) * step

            def full(self, name):
                b, _, unit, n = FILLS.at[name]
                s, n = (bank_full[b], n) if unit is None else (unit_used, unit + 1)
                return s, self.at(s, n)

            def read(self, name, later_turns=0):
                b, n = FILLS.at[name][:2]
                return bank_read[b], self.at(bank_read[b], n + later_turns * FILLS_PER["expert"][b])

            def free(self, name):
                b, n = FILLS.at[name][:2]
                return bank_read[b], self.at(bank_read[b], n - 1)

        def bank_of(name):
            return bank[FILLS.at[name][0]]

        def fill_loops(kind):
            out = {bank_read[b]: FILLS_PER[kind][b] for b in range(8)}
            out.update({bank_full[b]: FILLS_PER[kind][8 + b] for b in range(8)})
            return out

        def read_of(name):
            return bank_read[FILLS.at[name][0]]

        def full_of(name):
            return bank_full[FILLS.at[name][0]]

        def cols(name):
            a, b = COL[name]
            return par[:, a:b]

        ident, ones = cols("ident"), cols("ones")
        masks = {("A", 0): cols("mask_low"), ("A", 1): cols("mask_up"),
                 ("D", 0): cols("mask_up"), ("D", 1): cols("mask_low")}
        tri = [cols("up01"), cols("low01")]

        def mod_col(l, j, kt, s):
            return mod[:, 48 * l + 8 * j + kt, s:s + 1]

        def sets(width):
            return [(s, slice(256 * s, 256 * s + 256)) for s in range(width // 256)]

        outputs = [scan_steps(), [s for s in scan_steps() if s[0] < 2]]

        UNIT_LOOP = {"ada": 6, "ffn": 12, "expert": UPE, "pass": NE * UPE}

        def unit_loops(kind, extra=None):
            n = UNIT_LOOP[kind]
            out = {unit_used: n, hi_ready: 2 * n, lo_ready: n, **{s: 16 * n // SLOTS for s in raw_loaded}}
            out.update(extra or {})
            return out

        block = ctx.enter_context(nc.Block())

        @block.sync
        def _(sp):
            sp.dma_start(par[:, :], params).then_inc(params_loaded, 16)

            for n in range(SLOTS):
                sp.dma_start(raw[n][:, :], stream[n]).then_inc(raw_loaded[n], 16)
            sp.dma_start(h[:, :, :], tokens).then_inc(tokens_loaded, 16)

            def load_rest(first, turns, back):
                with sp.Fori(0, turns) as i:
                    for j in range(SLOTS):
                        slot = (first + j) % SLOTS
                        sp.wait_ge(lo_ready, i * SLOTS + (first + j - SLOTS + 1))
                        sp.dma_start(raw[slot][:, :],
                                     stream[ds(i * SLOTS + (first + j - back), 1)].rearrange("a p n -> p (a n)")
                                     ).then_inc(raw_loaded[slot], 16)

            load_rest(SLOTS, (N_UNITS + 2 - SLOTS) // SLOTS, 0)
            sp.wait_ge(npass_ready, 1)
            passes = sp.value_load(npass[0:1, 0:1], min_val=1, max_val=2)
            with sp.If(passes > 1):
                load_rest(N_UNITS + 2, NE * UPE // SLOTS, NE * UPE)
            with sp.Else():
                sp.nop()
            sp.wait_ge(result_ready, 1)
            sp.dma_start(out, result[:, :, :]).then_inc(out_stored, 16)
            sp.wait_ge(out_stored, 16)

        @block.scalar
        def _(act):
            t = Counts(act)

            def chain(ins):
                ins.then_inc(act_chain, 1)
                act.wait_ge(*t.next(act_chain))

            def split(n):
                act.wait_ge(raw_loaded[n % SLOTS], t.at(raw_loaded[n % SLOTS], 16 * (n // SLOTS + 1)))
                if n >= SLOTS:
                    act.wait_ge(unit_used, t.at(unit_used, n - SLOTS + 1))
                for c in HALVES:
                    nc.scalar.activation(whi[n % SLOTS][:, c], raw[n % SLOTS][:, c], ACT.Copy).then_inc(hi_ready, 1)

            ahead = [0]

            def split_to(n):
                while ahead[0] <= min(n, N_UNITS - 1):
                    split(ahead[0])
                    ahead[0] += 1

            def copy(dst, src, **kw_):
                return nc.scalar.activation(dst, src, ACT.Copy, **kw_)

            act.wait_ge(params_loaded, 16)
            cd = cols("cond").rearrange("p (k s) -> p k s", s=2)
            chain(nc.scalar.activation(condf[:, :, :], cd, ACT.Silu))
            copy(cond4[:, :, 0:2], condf[:, :, :]).then_inc(small_hi, 1)
            for l in range(DEPTH):
                copy(wg_hi[:, l, :, :], cols(f"wgates_{l}").rearrange("p (k c) -> p k c", c=16)).then_inc(small_hi, 1)
            copy(ro_hi[:, :, :], cols("router").rearrange("p (k c) -> p k c", c=NE)).then_inc(small_hi, 1)

            def norm(tag, width, final=False):
                for kt in range(KT):
                    if kt >= 2:
                        act.wait_ge(*t.next(square_used))
                    nc.scalar.activation(square[:, kt % 2, 0:width], h[:, kt, 0:width],
                                         ACT.Square).then_inc(square_ready, 1)
                act.wait_ge(*t.next(square_used))
                act.wait_ge(*t.full(f"norm {tag}"))
                ps = bank_of(f"norm {tag}")
                nc.scalar.activation(std[:, 0:width], ps[:, 0:width], ACT.Sqrt, bias=cols("eps"),
                                     scale=1.0 / D).then_inc(read_of(f"norm {tag}"), 1)
                if final:
                    return
                which, l = tag.split()
                which, l = int(which) - 1, int(l)
                for kt in range(KT):
                    act.wait_ge(*t.next(scaled_ready))
                    if kt >= 2:
                        act.wait_ge(*t.next(u_lo_ready))
                    for s, c in sets(width):
                        last = nc.scalar.activation(modded[:, kt % 2, c], scaled[:, kt % 2, c], ACT.Identity,
                                                    bias=mod_col(l, 3 * which, kt, s), scale=gain[:, l, which, kt, s:s + 1])
                    last.then_inc(modded_ready, 1)
                    act.wait_ge(*t.next(modded_ready))
                    copy(u_hi[:, kt, 0:width], modded[:, kt % 2, 0:width]).then_inc(u_hi_ready, 1)
                act.wait_ge(*t.next(u_lo_ready, 2))

            split_to(2 + 5)
            with t.loop(ADA_UNITS // 6 - 1, unit_loops("ada", fill_loops("ada")), ADA_UNITS // 6 - 1) as i:
                for j in range(6):
                    split(ahead[0] + j)
            ahead[0] = ADA_UNITS + 2

            act.wait_ge(tokens_loaded, 16)
            act.wait_ge(mod_ready, 1)
            for l in range(DEPTH):
                W = NT if l == 0 else SEQ
                norm(f"1 {l}", NT)
                u = UNIT_AT[f"conv{l}"]
                for c in range(6):
                    split_to(u + c + 2)
                    if c < CT:
                        act.wait_ge(*t.full(f"conv {l} {c} 1"))
                        ps = bank_of(f"conv {l} {c} 1")
                        if c >= 2:
                            act.wait_ge(*t.read(f"conv {l} {c - 2} 0"))
                        copy(hh[:, c % 2, 0:W], ps[:, 0:W]).then_inc(read_of(f"conv {l} {c} 1"), 1)
                u = UNIT_AT[f"qkvo{l}"]
                for c, name in enumerate("qkvo"):
                    split_to(u + 2 * c + 2)
                    split_to(u + 2 * c + 3)
                    for tt in range(TT if l == 0 or name in "kv" else 2):
                        if name == "k":
                            continue
                        act.wait_ge(*t.full(f"{name} {l} {tt}"))
                        ps = bank_of(f"{name} {l} {tt}")
                        if name == "q":
                            ins = copy(q[:, tt, :], ps[:, :])
                        elif name == "v":
                            ins = copy(v[:, tt, :, 0:HD], ps[:, :].rearrange("p (h d) -> p h d", h=HEADS))
                        else:
                            ins = nc.scalar.activation(o[:, tt, :], ps[:, :], ACT.Sigmoid)
                        ins.then_inc(read_of(f"{name} {l} {tt}"), 1)
                for c in (4, 5):
                    for j in range(2):
                        act.wait_ge(*t.read(f"conv {l} {c} {j}"))
                act.wait_ge(unit_used, t.at(unit_used, u + 8))
                act.wait_ge(*t.full(f"gates {l}"))
                copy(u_hi[:, 0:CT, 0:W], conv[:, :, 0:W]).then_inc(conv_hi, 1)
                act.wait_ge(*t.next(gate_arg))
                chain(nc.scalar.activation(g_tmp[:, 1], g_tmp[:, 0], ACT.Exp))
                nc.scalar.activation(g_tmp[:, 0], g_tmp[:, 1], ACT.Ln, bias=1.0).then_inc(gate_log, 1)
                for tt in range(TT if l == 0 else 2):
                    act.wait_ge(*t.full(f"qT {l} {tt}"))
                    ps = bank_of(f"qT {l} {tt}")
                    copy(qT[:, :, tt * P:tt * P + P], ps[:, :].rearrange("p (h s) -> p h s", h=HEADS)
                         ).then_inc(read_of(f"qT {l} {tt}"), 1)
                act.wait_ge(*t.next(exp_arg))
                nc.scalar.activation(e_out[:, :, :, :], e_in[:, :, :, :], ACT.Exp).then_inc(exp_done, 1)
                act.wait_ge(*t.next(exp_done))

                def decays(i):
                    tt, d, _ = outputs[l][i]
                    act.wait_ge(*t.read(f"M {l} {tt} {d}"))
                    for hd in range(HEADS):
                        c = slice(hd * P, hd * P + P)
                        last = nc.scalar.activation(t512[:, i % 2, c], t512[:, i % 2, c], ACT.Exp,
                                                    bias=gg[:, 2 * tt + d, hd:hd + 1])
                    last.then_inc(decay_ready, 1)

                decays(0)
                for i, (tt, d, kk) in enumerate(outputs[l]):
                    a = 2 * tt + d
                    if kk:
                        if i:
                            before = outputs[l][i - 1]
                            act.wait_ge(*t.read(f"num {l} {before[0]} {before[1]} 1"))
                        for part in range(2):
                            act.wait_ge(*t.full(f"int {l} {tt} {d} {part}"))
                            ps = bank_of(f"int {l} {tt} {d} {part}")
                            for j in range(2):
                                hd = 2 * part + j
                                last = copy(inter[:, hd, :], ps[:, 256 * j:256 * j + HE],
                                            scale=e_out[:, 0, a, hd:hd + 1])
                            last.then_inc(read_of(f"int {l} {tt} {d} {part}"), 1)
                    if i + 1 < len(outputs[l]):
                        decays(i + 1)
                act.wait_ge(*t.next(sumsq_ready, W // P))
                nc.scalar.activation(msq[:, 1, 0:W // P, :], msq[:, 0, 0:W // P, :], ACT.Sqrt, bias=cols("eps"),
                                     scale=1.0 / HD).then_inc(root_ready, 1)
                for tt in range(TT if l == 0 else 2):
                    act.wait_ge(*t.full(f"yT {l} {tt}"))
                    ps = bank_of(f"yT {l} {tt}")
                    for hd in range(HEADS):
                        last = copy(u_hi[:, CT + hd, tt * P:tt * P + P], ps[:, hd * P:hd * P + P],
                                    scale=cols(f"mnorm_{l}")[:, hd:hd + 1])
                    last.then_inc(y_hi_done, 1)
                u = UNIT_AT[f"out{l}"]
                for c in range(4):
                    split_to(u + c + 2)
                act.wait_ge(*t.read(f"out {l} 3 1"))
                norm(f"2 {l}", W)
                if l == 0:
                    def group(g, base):
                        u, nf = UNIT_AT[f"ffn{g}"], GROUPS[g]
                        for c in range(nf + 4):
                            split(base + c)
                            if c < nf and c % 2:
                                for j in range(2):
                                    act.wait_ge(*t.full(f"ffn {g} {c - 1} {j}"))
                                    ps = bank_of(f"ffn {g} {c - 1} {j}")
                                    nc.scalar.activation(sil0[:, j, :], ps[:, :], ACT.Silu
                                                         ).then_inc(read_of(f"ffn {g} {c - 1} {j}"), 1)
                                for j in range(2):
                                    act.wait_ge(*t.read(f"ffn {g} {c} {j}"))
                                    copy(hid_hi[:, c - 1 + j, :], hid0[:, j, :]).then_inc(hid_hi_ready, 1)
                    assert ahead[0] == UNIT_AT["ffn0"] + 2
                    with t.loop(2, unit_loops("ffn", fill_loops("ffn")), 2):
                        group(0, ahead[0])
                    ahead[0] += 24
                    group(2, ahead[0])
                    ahead[0] += 10
                    act.wait_ge(*t.read("ffn 2 9 1"))
            act.wait_ge(*t.next(route_arg))
            nc.scalar.activation(s2[:, 3, :], s2[:, 2, :], ACT.Exp).then_inc(route_exp, 1)
            for i in range(0, 8, 2):
                act.wait_ge(*t.full(f"utok {i}"))
                ps = bank_of(f"utok {i}")
                tt, half = i // 4, i // 2 % 2
                copy(utok_hi[:, tt, 512 * half:512 * half + 512], ps[:, :]).then_inc(read_of(f"utok {i}"), 1)
            act.wait_ge(npass_ready, 1)
            passes = act.value_load(npass[0:1, 0:1], min_val=1, max_val=2)
            assert ahead[0] == UNIT_AT["moe"] + 2

            def gathered(name, i):
                act.wait_ge(*t.full(name))
                ps = bank_of(name)
                copy(xe_hi[:, 2 * i:2 * i + 4, :], ps[:, :].rearrange("p (k s) -> p k s", k=4)
                     ).then_inc(read_of(name), 1)

            with t.loop(passes, {**unit_loops("pass", fill_loops("pass")), y_hi_ready: NE}, 1) as i_pass:
                for i in range(4):
                    act.wait_ge(*t.full(f"PT {i}"))
                    ps = bank_of(f"PT {i}")
                    copy(pickT[:, 2 * i + 1:2 * i + 3, :], ps[:, :].rearrange("p (e n) -> p e n", e=2)
                         ).then_inc(read_of(f"PT {i}"), 1)
                for i in (0, 2):
                    gathered(f"gather {i}", i)
                with t.loop(NE, {**unit_loops("expert", fill_loops("expert")), y_hi_ready: 1}, NE) as e:
                    for j, (m, c, part) in enumerate(EXPERT_UNITS):
                        split(ahead[0] + j)
                        last = j + 1 == UPE or EXPERT_UNITS[j + 1][:2] != (m, c)
                        if m == "w1" and last:
                            act.wait_ge(*t.full(f"w1 {c}"))
                            ps, w = bank_of(f"w1 {c}"), CHUNKS[c]
                            if c >= 2:
                                act.wait_ge(*t.read(f"w3 {c - 2}"))
                            nc.scalar.activation(sil[:, c % 2, 0:w], ps[:, 0:w], ACT.Silu
                                                 ).then_inc(read_of(f"w1 {c}"), 1)
                        if j in T_AT:
                            c_t = T_AT[j]
                            n_t = CHUNKS[c_t] // P
                            act.wait_ge(*t.full(f"T {c_t}"))
                            ps = bank_of(f"T {c_t}")
                            copy(hT_hi[:, c_t % 2, 0:n_t, :], ps[:, 0:n_t * P].rearrange("p (k s) -> p k s", k=n_t)
                                 ).then_inc(hT_hi_ready, 1)
                        if j == NEXT_AT:
                            for i in (0, 2):
                                gathered(f"next {i}", i)
                        if j == UPE - 1:
                            for half in range(2):
                                act.wait_ge(*t.full(f"y {half}"))
                                ps = bank_of(f"y {half}")
                                last_ins = copy(y_hi[:, 512 * half:512 * half + 512], ps[:, :], scale=gcol[:, :])
                            last_ins.then_inc(y_hi_ready, 1)
            t.loops.append((passes - 1, fill_loops("pass")))
            act.wait_ge(*t.read("final back 3"))
            norm("f", SEQ, final=True)

        @block.vector
        def _(dve):
            t = Counts(dve)
            TTn, STT = nc.vector.tensor_tensor, nc.vector.scalar_tensor_tensor

            def chain(ins):
                ins.then_inc(dve_chain, 1)
                dve.wait_ge(*t.next(dve_chain))

            def split(n):
                for i, c in enumerate(HALVES):
                    dve.wait_ge(hi_ready, t.at(hi_ready, 2 * n + 1 + i))
                    last = TTn(wlo[n % SLOTS][:, c], raw[n % SLOTS][:, c], whi[n % SLOTS][:, c].bitcast(f32),
                               ALU.subtract)
                last.then_inc(lo_ready, 1)

            ahead = [0]

            def split_to(n):
                while ahead[0] <= min(n, N_UNITS - 1):
                    split(ahead[0])
                    ahead[0] += 1

            def wide(x, n, shape):
                return x.unsqueeze(len(shape) - 1).broadcast_to(shape)

            dve.wait_ge(params_loaded, 16)
            dve.wait_ge(*t.next(small_hi))
            TTn(cond4[:, :, 2:4], condf[:, :, :], cond4[:, :, 0:2].bitcast(f32), ALU.subtract).then_inc(small_lo, 1)
            for l in range(DEPTH):
                dve.wait_ge(*t.next(small_hi))
                TTn(wg_lo[:, l, :, :], cols(f"wgates_{l}").rearrange("p (k c) -> p k c", c=16),
                    wg_hi[:, l, :, :].bitcast(f32), ALU.subtract).then_inc(small_lo, 1)
            dve.wait_ge(*t.next(small_hi))
            TTn(ro_lo[:, :, :], cols("router").rearrange("p (k c) -> p k c", c=NE), ro_hi[:, :, :].bitcast(f32),
                ALU.subtract).then_inc(small_lo, 1)

            def ada_rows(c):
                dve.wait_ge(*t.full(f"ada {c}"))
                nc.vector.tensor_copy(ada_row[:, c, :], bank_of(f"ada {c}")[0:4, :]).then_inc(read_of(f"ada {c}"), 1)

            split_to(1)
            with t.loop(ADA_UNITS // 6, unit_loops("ada", fill_loops("ada")), ADA_UNITS // 6) as i:
                for c in range(3):
                    split(ahead[0] + 2 * c)
                    ada_rows(c)
                    split(ahead[0] + 2 * c + 1)
            ahead[0] = ADA_UNITS + 2
            dve.wait_ge(mod_turned, ADA_UNITS // 6)
            ps = bank_of("mod")[:, 0:DEPTH * 48 * 2].rearrange("p (n c) -> p n c", c=2)
            TTn(mod[:, :, :], ps, wide(cols("b_ada"), 2, [P, DEPTH * 48, 2]), ALU.add).then_inc(read_of("mod"), 1)
            dve.wait_ge(*t.read("mod"))
            for l in range(DEPTH):
                for w in range(2):
                    s0 = 48 * l + 8 * (3 * w + 1)
                    last = STT(gain[:, l, w, :, :], mod[:, s0:s0 + 8, :], 1.0,
                               wide(cols(f"norm{w + 1}_{l}"), 2, [P, KT, 2]), ALU.add, ALU.mult)
            last.then_inc(mod_ready, 1)
            dve.wait_ge(*t.next(mod_ready))
            dve.wait_ge(tokens_loaded, 16)

            def norm(tag, width, final=False):
                dve.wait_ge(*t.read(f"norm {tag}"))
                chain(nc.vector.reciprocal(rstd[:, 0:width], std[:, 0:width]))
                if final:
                    for kt in range(KT):
                        last = STT(result[:, kt, :], h[:, kt, 0:width], cols("final_g")[:, kt:kt + 1],
                                   rstd[:, 0:width], ALU.mult, ALU.mult)
                    last.then_inc(result_ready, 1)
                    return

                def scale(kt):
                    TTn(scaled[:, kt % 2, 0:width], h[:, kt, 0:width], rstd[:, 0:width],
                        ALU.mult).then_inc(scaled_ready, 1)
                scale(0)
                scale(1)
                for kt in range(KT):
                    dve.wait_ge(*t.next(u_hi_ready))
                    TTn(u_lo[:, kt, 0:width], modded[:, kt % 2, 0:width], u_hi[:, kt, 0:width].bitcast(f32),
                        ALU.subtract).then_inc(u_lo_ready, 1)
                    if kt + 2 < KT:
                        scale(kt + 2)

            def residual(name, kt, width, l, j):
                dve.wait_ge(*t.full(name))
                ps = bank_of(name)
                for s, c in sets(width):
                    last = STT(h[:, kt, c], ps[:, c], mod_col(l, j, kt, s), h[:, kt, c], ALU.mult, ALU.add)
                last.then_inc(read_of(name), 1)

            for l in range(DEPTH):
                W = NT if l == 0 else SEQ
                norm(f"1 {l}", NT)
                nc.vector.memset(v[:, :, :, HD:HE], 1.0).then_inc(v_ones, 1)
                u = UNIT_AT[f"conv{l}"]
                cw = cols(f"conv_{l}").rearrange("p (c j) -> p c j", j=3)
                for c in range(6):
                    split_to(u + c + 2)
                    if c < CT:
                        dve.wait_ge(*t.full(f"conv {l} {c} 0"))
                        ps = bank_of(f"conv {l} {c} 0")
                        dve.wait_ge(*t.read(f"conv {l} {c} 1"))
                        TTn(yprod[:, 0:W], ps[:, 0:W], hh[:, c % 2, 0:W], ALU.mult).then_inc(
                            read_of(f"conv {l} {c} 0"), 1)
                        dve.wait_ge(*t.read(f"conv {l} {c} 0"))
                        chain(nc.vector.tensor_scalar(conv[:, c, 0:W], yprod[:, 0:W], cw[:, c, 1:2], None, ALU.mult))
                        rows = [(0, SEQ, GRID_W)] + ([(SEQ, NT, CTX)] if l == 0 else [])
                        for side in range(2):
                            for a, b, w in rows:
                                z = conv[:, c, a:b].rearrange("p (r w) -> p r w", w=w)
                                y = yprod[:, a:b].rearrange("p (r w) -> p r w", w=w)
                                to, of = (slice(1, w), slice(0, w - 1)) if side == 0 else (slice(0, w - 1), slice(1, w))
                                last = STT(z[:, :, to], y[:, :, of], cw[:, c, 2 * side:2 * side + 1], z[:, :, to],
                                           ALU.mult, ALU.add)
                            chain(last)
                    else:
                        for j in range(2):
                            ch = 2 * (c - CT) + j
                            name = f"conv {l} {c} {j}"
                            dve.wait_ge(*t.full(name))
                            ps = bank_of(name)
                            TTn(conv[:, ch, 0:W], conv[:, ch, 0:W], ps[:, 0:W], ALU.mult).then_inc(read_of(name), 1)
                u = UNIT_AT[f"qkvo{l}"]
                for c, name in enumerate("qkvo"):
                    split_to(u + 2 * c + 3)
                    if name == "k":
                        for tt in range(TT):
                            dve.wait_ge(*t.full(f"k {l} {tt}"))
                            ps = bank_of(f"k {l} {tt}")
                            nc.vector.tensor_scalar(k[:, tt, :], ps[:, :], HD ** -0.5, None,
                                                    ALU.mult).then_inc(read_of(f"k {l} {tt}"), 1)
                dve.wait_ge(*t.full(f"gates {l}"))
                ps = bank_of(f"gates {l}")
                TTn(gts[:, :, :, :].rearrange("p (t d) k h -> p t (d k h)", d=2),
                    ps[:, 0:TT * 16].rearrange("p (t c) -> p t c", c=16),
                    cols(f"bgates_{l}").unsqueeze(1).broadcast_to([P, TT, 16]), ALU.add
                    ).then_inc(read_of(f"gates {l}"), 1)
                dve.wait_ge(*t.read(f"gates {l}"))
                forget, inputg = gts[:, :, 1, :], gts[:, :, 0, :]
                STT(g_tmp[:, 0], forget, -1.0, forget, ALU.mult, ALU.min).then_inc(gate_arg, 1)
                dve.wait_ge(*t.next(conv_hi))
                TTn(u_lo[:, 0:CT, 0:W], conv[:, :, 0:W], u_hi[:, 0:CT, 0:W].bitcast(f32),
                    ALU.subtract).then_inc(conv_lo, 1)
                dve.wait_ge(*t.next(gate_log))
                STT(lf[:, :, :], forget, 0.0, g_tmp[:, 0], ALU.min, ALU.subtract).then_inc(logf_ready, 1)
                for tt in range(TT if l == 0 else 2):
                    dve.wait_ge(*t.full(f"kT {l} {tt}"))
                    ps = bank_of(f"kT {l} {tt}")
                    nc.vector.tensor_copy(kT[:, :, tt * P:tt * P + P], ps[:, :].rearrange("p (h s) -> p h s", h=HEADS)
                                          ).then_inc(read_of(f"kT {l} {tt}"), 1)
                dve.wait_ge(*t.full(f"cum {l}"))
                ps = bank_of(f"cum {l}")
                nc.vector.tensor_copy(cum[:, :, :, :].rearrange("p a b c -> p (a b c)"), ps[:, 0:64]
                                      ).then_inc(read_of(f"cum {l}"), 1)
                dve.wait_ge(*t.read(f"cum {l}"))
                TTn(gg[:, :, :], inputg, cum[:, 0], ALU.subtract).then_inc(gg_ready, 1)
                dve.wait_ge(*t.next(gg_ready))

                def prefix_max(a):
                    dve.wait_ge(*t.read(f"G {l} {a}"))
                    nc.vector.tensor_reduce(pmax[:, a, :], t512[:, a % 2, :].rearrange("p (h s) -> p h s", h=HEADS),
                                            AX.X, ALU.max).then_inc(pmax_done, 1)

                for a in range(2 * TT):
                    dve.wait_ge(*t.full(f"G {l} {a}"))
                    ps = bank_of(f"G {l} {a}")[:, :].rearrange("p (h s) -> p h s", h=HEADS)
                    nc.vector.tensor_reduce(gmax[:, a, :], ps, AX.X, ALU.max)
                    if a >= 2:
                        dve.wait_ge(*t.next(pmax_done))
                    TTn(t512[:, a % 2, :].rearrange("p (h s) -> p h s", h=HEADS), ps,
                        masks["A", a % 2].unsqueeze(1).broadcast_to([P, HEADS, P]), ALU.add
                        ).then_inc(read_of(f"G {l} {a}"), 1)
                    if a:
                        prefix_max(a - 1)
                prefix_max(2 * TT - 1)
                dve.wait_ge(*t.next(pmax_done, 2))
                for kk in range(4):
                    for d in range(2):
                        a = 2 * LAT_STEPS[d][kk] + d
                        if kk == 0:
                            chain(nc.vector.memset(mprev[:, a, :], 0.0))
                        TTn(m_t[:, a, :], pmax[:, a, :], mprev[:, a, :], ALU.max)
                        chain(TTn(m_l[:, a, :], gmax[:, a, :], mprev[:, a, :], ALU.max))
                        if kk < 3:
                            nxt = 2 * LAT_STEPS[d][kk + 1] + d
                            chain(TTn(mprev[:, nxt, :], cum[:, 1, a, :], m_l[:, a, :], ALU.add))
                TTn(e_in[:, 0], mprev[:, :, :], m_t[:, :, :], ALU.subtract)
                TTn(e_in[:, 1], gg[:, :, :], m_l[:, :, :], ALU.subtract)
                TTn(e_in[:, 2], mprev[:, :, :], m_l[:, :, :], ALU.subtract)
                STT(e_in[:, 3], cum[:, 0], -1.0, m_t[:, :, :], ALU.mult, ALU.subtract).then_inc(exp_arg, 1)
                dve.wait_ge(*t.next(exp_arg))
                dve.wait_ge(*t.next(exp_done))

                def decay_args(i):
                    tt, d, _ = outputs[l][i]
                    name = f"M {l} {tt} {d}"
                    dve.wait_ge(*t.full(name))
                    ps = bank_of(name)
                    STT(t512[:, i % 2, :].rearrange("p (h s) -> p h s", h=HEADS),
                        ps[:, :].rearrange("p (h s) -> p h s", h=HEADS), -1.0,
                        masks["D", d].unsqueeze(1).broadcast_to([P, HEADS, P]), ALU.mult, ALU.add
                        ).then_inc(read_of(name), 1)

                decay_args(0)
                for tt, d, kk in scan_steps():
                    a = 2 * tt + d
                    full = (tt, d, kk) in outputs[l]
                    if full:
                        i = outputs[l].index((tt, d, kk))
                        dve.wait_ge(*t.next(decay_ready))
                        name = f"S {l} {tt} {d}"
                        dve.wait_ge(*t.full(name))
                        ps = bank_of(name)
                        TTn(t512[:, i % 2, :], ps[:, :], t512[:, i % 2, :], ALU.mult).then_inc(read_of(name), 1)
                        if i + 1 < len(outputs[l]):
                            decay_args(i + 1)
                    if kk < 3:
                        for part in range(2):
                            name = f"upd {l} {tt} {d} {part}"
                            dve.wait_ge(*t.full(name))
                            ps = bank_of(name)
                            for j in range(2):
                                hd = 2 * part + j
                                src = ps[:, 256 * j:256 * j + HE]
                                if kk:
                                    last = STT(state[:, d, hd, :], state[:, d, hd, :], e_out[:, 2, a, hd:hd + 1], src,
                                               ALU.mult, ALU.add)
                                else:
                                    last = nc.vector.tensor_copy(state[:, d, hd, :], src)
                            last.then_inc(read_of(name), 1)
                            dve.wait_ge(*t.read(name))
                    if full:
                        for part in range(2):
                            name = f"num {l} {tt} {d} {part}"
                            dve.wait_ge(*t.full(name))
                            ps = bank_of(name)[:, :].rearrange("p (h s) -> p h s", h=2)[:, :, 0:HE]
                            dst = u_sum[:, 2 * part:2 * part + 2, :]
                            if kk:
                                dve.wait_ge(*t.read(f"int {l} {tt} {d} {part}"))
                                ins = TTn(dst, ps, inter[:, 2 * part:2 * part + 2, :], ALU.add)
                            else:
                                ins = nc.vector.tensor_copy(dst, ps)
                            ins.then_inc(read_of(name), 1)
                            dve.wait_ge(*t.read(name))
                        den = u_sum[:, :, HD]
                        chain(STT(small[:, 0, :], den, -1.0, den, ALU.mult, ALU.max))
                        chain(TTn(small[:, 1, :], small[:, 0, :], e_out[:, 3, a, :], ALU.max))
                        chain(nc.vector.reciprocal(small[:, 2, :], small[:, 1, :]))
                        later = 2 * LAT_STEPS[1 - d].index(tt) + 1 - d < 2 * kk + d
                        for hd in range(HEADS):
                            dst = hacc[:, tt, hd * P:hd * P + P]
                            if later:
                                last = STT(dst, u_sum[:, hd, 0:HD], small[:, 2, hd:hd + 1], dst, ALU.mult, ALU.add)
                            else:
                                last = nc.vector.tensor_scalar(dst, u_sum[:, hd, 0:HD], small[:, 2, hd:hd + 1], None,
                                                               ALU.mult)
                        last.then_inc(hacc_done, 1)
                        dve.wait_ge(*t.next(hacc_done))
                for tt in range(W // P):
                    if tt >= 2:
                        dve.wait_ge(*t.next(sumsq_ready))
                    chain(TTn(t512[:, tt % 2, :], hacc[:, tt, :], hacc[:, tt, :], ALU.mult))
                    nc.vector.tensor_reduce(msq[:, 0, tt, :], t512[:, tt % 2, :].rearrange("p (h s) -> p h s", h=HEADS),
                                            AX.X, ALU.add).then_inc(sumsq_ready, 1)
                dve.wait_ge(*t.next(sumsq_ready, 2))
                dve.wait_ge(*t.next(root_ready))
                chain(nc.vector.reciprocal(msq[:, 2, 0:W // P, :], msq[:, 1, 0:W // P, :]))
                for tt in range(W // P):
                    hv = hacc[:, tt, :].rearrange("p (h s) -> p h s", h=HEADS)
                    TTn(hv, hv, wide(msq[:, 2, tt, :], P, [P, HEADS, P]), ALU.mult).then_inc(normed, 1)
                for tt in range(TT if l == 0 else 2):
                    name = f"yT {l} {tt}"
                    dve.wait_ge(*t.full(name))
                    ps = bank_of(name)
                    dve.wait_ge(*t.next(y_hi_done))
                    for hd in range(HEADS):
                        c = slice(tt * P, tt * P + P)
                        last = STT(u_lo[:, CT + hd, c], ps[:, hd * P:hd * P + P], cols(f"mnorm_{l}")[:, hd:hd + 1],
                                   u_hi[:, CT + hd, c].bitcast(f32), ALU.mult, ALU.subtract)
                    last.then_inc(read_of(name), 1)
                u = UNIT_AT[f"out{l}"]
                for c in range(4):
                    split_to(u + c + 2)
                    for j in range(2):
                        residual(f"out {l} {c} {j}", 2 * c + j, W, l, 2)
                norm(f"2 {l}", W)
                if l == 0:
                    def group(g, base):
                        nf = GROUPS[g]
                        for c in range(nf + 4):
                            split(base + c)
                            if c and c % 2 == 0 and c <= nf:
                                dve.wait_ge(*t.next(hid_lo_ready, 2))
                            if c < nf and c % 2:
                                for j in range(2):
                                    dve.wait_ge(*t.full(f"ffn {g} {c} {j}"))
                                    ps = bank_of(f"ffn {g} {c} {j}")
                                    dve.wait_ge(*t.read(f"ffn {g} {c - 1} {j}"))
                                    TTn(hid0[:, j, :], ps[:, :], sil0[:, j, :], ALU.mult
                                        ).then_inc(read_of(f"ffn {g} {c} {j}"), 1)
                                for j in range(2):
                                    dve.wait_ge(*t.next(hid_hi_ready))
                                    TTn(hid_lo[:, c - 1 + j, :], hid0[:, j, :], hid_hi[:, c - 1 + j, :].bitcast(f32),
                                        ALU.subtract).then_inc(hid_lo_ready, 1)
                            if c >= nf:
                                for j in range(2):
                                    residual(f"ffn {g} {c} {j}", 2 * (c - nf) + j, NT, 0, 5)
                    with t.loop(2, unit_loops("ffn", {**fill_loops("ffn"), hid_hi_ready: 8, hid_lo_ready: 8}), 2):
                        group(0, ahead[0])
                    ahead[0] += 24
                    group(2, ahead[0])
                    ahead[0] += 10

            dve.wait_ge(*t.full("logits"))
            ps = bank_of("logits")
            nc.vector.tensor_copy(lg[:, :, :].rearrange("p t e -> p (t e)"), ps[:, 0:2 * NE]
                                  ).then_inc(read_of("logits"), 1)
            dve.wait_ge(*t.read("logits"))
            shape = [P, 2, NE]
            rank = cols("rank").unsqueeze(1).broadcast_to(shape)
            for i, one in enumerate((one1, one2)):
                chain(nc.vector.tensor_reduce(s2[:, i, :], lg[:, :, :], AX.X, ALU.max))
                chain(TTn(sc8[:, 0], lg[:, :, :], wide(s2[:, i, :], NE, shape), ALU.is_equal))
                chain(TTn(sc8[:, 1], sc8[:, 0], rank, ALU.mult))
                chain(nc.vector.tensor_reduce(s2[:, 7, :], sc8[:, 1], AX.X, ALU.max))
                chain(TTn(one[:, :, :], sc8[:, 1], wide(s2[:, 7, :], NE, shape), ALU.is_equal))
                if i == 0:
                    chain(STT(lg[:, :, :], one[:, :, :], NEG, lg[:, :, :], ALU.mult, ALU.add))
            TTn(sel[:, :, :], one1[:, :, :], one2[:, :, :], ALU.add).then_inc(sel_ready, 1)
            TTn(s2[:, 2, :], s2[:, 1, :], s2[:, 0, :], ALU.subtract).then_inc(route_arg, 1)
            dve.wait_ge(*t.next(route_exp))
            chain(nc.vector.tensor_scalar(s2[:, 4, :], s2[:, 3, :], 1.0, None, ALU.add))
            chain(nc.vector.reciprocal(s2[:, 5, :], s2[:, 4, :]))
            chain(TTn(s2[:, 6, :], s2[:, 5, :], s2[:, 3, :], ALU.mult))
            TTn(sc8[:, 2], one1[:, :, :], wide(s2[:, 5, :], NE, shape), ALU.mult)
            chain(TTn(sc8[:, 3], one2[:, :, :], wide(s2[:, 6, :], NE, shape), ALU.mult))
            chain(TTn(gate[:, :, :], sc8[:, 2], sc8[:, 3], ALU.add))
            dve.wait_ge(*t.full("count"))
            ps = bank_of("count")
            chain(nc.vector.tensor_reduce(s2[:, 7, 0:1], ps[:, 16:24], AX.X, ALU.max))
            nc.vector.tensor_scalar(npass[0:1, 0:1], s2[0:1, 7, 0:1], float(P), 1.0, ALU.is_gt, ALU.add
                                    ).then_inc(npass_ready, 1)
            dve.wait_ge(*t.next(npass_ready))
            dve.wait_ge(*t.next(sel_ready))
            TTn(sc8[:, 4], ps[:, 0:16].rearrange("p (t e) -> p t e", t=2), sel[:, :, :], ALU.mult
                ).then_inc(read_of("count"), 1)
            dve.wait_ge(*t.read("count"))
            chain(nc.vector.tensor_scalar(slot_of[:, :, :], sc8[:, 4], -1.0, None, ALU.add))
            for i in range(1, 8, 2):
                dve.wait_ge(*t.full(f"utok {i}"))
                ps = bank_of(f"utok {i}")
                tt, half = i // 4, i // 2 % 2
                nc.vector.tensor_copy(utok_lo[:, tt, 512 * half:512 * half + 512], ps[:, :]
                                      ).then_inc(read_of(f"utok {i}"), 1)
            passes = dve.value_load(npass[0:1, 0:1], min_val=1, max_val=2)

            def gathered(name, i):
                dve.wait_ge(*t.full(name))
                ps = bank_of(name)
                nc.vector.tensor_copy(xe_lo[:, 2 * i - 2:2 * i + 2, :], ps[:, :].rearrange("p (k s) -> p k s", k=4)
                                      ).then_inc(read_of(name), 1)

            chain(nc.vector.memset(pick[:, :, NE, :].bitcast(f32), 0.0))

            def give_back(which):
                for i in range(4):
                    dve.wait_ge(*t.full(f"{which} {i}"))
                    ps = bank_of(f"{which} {i}")
                    for j in range(2):
                        kt = 2 * i + j
                        last = STT(h[:, kt, 0:SEQ], ps[:, 256 * j:256 * j + 256], mod_col(1, 5, kt, 0),
                                   h[:, kt, 0:SEQ], ALU.mult, ALU.add)
                    last.then_inc(read_of(f"{which} {i}"), 1)
                    dve.wait_ge(*t.read(f"{which} {i}"))

            nc.vector.memset(pickT[:, 0, :].bitcast(f32), 0.0)
            nc.vector.memset(y_hi[:, :].bitcast(f32), 0.0)
            chain(nc.vector.memset(y_lo[:, :].bitcast(f32), 0.0))
            per_expert = {dve_chain: 1, y_hi_ready: 1, hT_hi_ready: len(CHUNKS)}
            per_pass = {y_hi_ready: NE, hT_hi_ready: NE * len(CHUNKS), dve_chain: 1 + NE, pick_ready: 1}
            with t.loop(passes, {**unit_loops("pass", fill_loops("pass")), **per_pass}, 1):
                for tt in range(2):
                    last = TTn(pick[:, tt, 0:NE, :], cols("iota").unsqueeze(1).broadcast_to([P, NE, P]),
                               wide(slot_of[:, tt, :], P, [P, NE, P]), ALU.is_equal)
                last.then_inc(pick_ready, 1)
                dve.wait_ge(*t.next(pick_ready))
                chain(nc.vector.tensor_scalar(slot_of[:, :, :], slot_of[:, :, :], -float(P), None, ALU.add))
                for i in (1, 3):
                    gathered(f"gather {i}", i)
                dve.wait_ge(*t.full("gslot"))
                ps = bank_of("gslot")
                nc.vector.tensor_copy(gslot[:, :], ps[:, 0:NE]).then_inc(read_of("gslot"), 1)
                with t.loop(NE, {**unit_loops("expert", fill_loops("expert")), **per_expert}, NE) as e:
                    for j, (m, c, part) in enumerate(EXPERT_UNITS):
                        split(ahead[0] + j)
                        if j == 0:
                            dve.wait_ge(*t.read("gslot"))
                            dve.wait_ge(*t.free("y 1"))
                            chain(nc.vector.tensor_copy(gcol[:, :], gslot[:, ds(e, 1)]))
                        last_part = j + 1 == UPE or EXPERT_UNITS[j + 1][:2] != (m, c)
                        if m == "w3" and last_part:
                            dve.wait_ge(*t.full(f"w3 {c}"))
                            ps, w = bank_of(f"w3 {c}"), CHUNKS[c]
                            dve.wait_ge(*t.read(f"w1 {c}"))
                            TTn(hid[:, c % 2, 0:w], ps[:, 0:w], sil[:, c % 2, 0:w], ALU.mult
                                ).then_inc(read_of(f"w3 {c}"), 1)
                        if j == BACK_AT:
                            give_back("back")
                        if j in T_AT:
                            c_t = T_AT[j]
                            n_t = CHUNKS[c_t] // P
                            dve.wait_ge(*t.full(f"T {c_t}"))
                            ps = bank_of(f"T {c_t}")
                            dve.wait_ge(*t.next(hT_hi_ready))
                            TTn(hT_lo[:, c_t % 2, 0:n_t, :], ps[:, 0:n_t * P].rearrange("p (k s) -> p k s", k=n_t),
                                hT_hi[:, c_t % 2, 0:n_t, :].bitcast(f32), ALU.subtract
                                ).then_inc(read_of(f"T {c_t}"), 1)
                        if j == NEXT_AT:
                            for i in (1, 3):
                                gathered(f"next {i}", i)
                        if j == UPE - 1:
                            dve.wait_ge(*t.next(y_hi_ready))
                            for half in range(2):
                                c_ = slice(512 * half, 512 * half + 512)
                                dve.wait_ge(*t.full(f"y {half}"))
                                ps = bank_of(f"y {half}")
                                STT(y_lo[:, c_], ps[:, :], gcol[:, :], y_hi[:, c_].bitcast(f32),
                                    ALU.mult, ALU.subtract).then_inc(read_of(f"y {half}"), 1)
                give_back("final back")
            t.loops.append((passes - 1, {**fill_loops("pass"), dve_chain: per_pass[dve_chain]}))
            norm("f", SEQ, final=True)

        @block.tensor
        def _(pe):
            t = Counts(pe)
            mm = nc.tensor.matmul

            def mm3(dst, a_hi, a_lo, b_hi, b_lo, start, stop):
                mm(dst, a_hi, b_hi, start=start, stop=False)
                mm(dst, a_hi, b_lo, start=False, stop=False)
                return mm(dst, a_lo, b_hi, start=False, stop=stop)

            def arrived(n):
                pe.wait_ge(lo_ready, t.at(lo_ready, n + 1))
                return n % SLOTS

            pe.wait_ge(*t.next(small_lo, DEPTH + 2))
            comb = cols("comb")[0:4, :]
            with t.loop(ADA_UNITS // 6, unit_loops("ada", fill_loops("ada")), ADA_UNITS // 6) as i:
                for c in range(3):
                    ps = bank_of(f"ada {c}")
                    for part in range(2):
                        sl = arrived(2 * c + part)
                        for kk in range(4):
                            kt = 4 * part + kk
                            for w in (whi, wlo):
                                last = mm(ps[0:4, :], cond4[:, kt, :], w[sl][:, kk * 512:kk * 512 + 512],
                                          start=kt == 0 and w is whi, stop=kt == KT - 1 and w is wlo)
                        last.then_inc(unit_used, 1)
                    pe.wait_ge(*t.read(f"ada {c}"))
                    for j in range(4):
                        last = mm(bank_of("mod")[:, ds(i * 24 + (8 * c + 2 * j), 2)], ada_row[:, c, j * P:j * P + P],
                                  comb, start=True, stop=True)
                last.then_inc(mod_turned, 1)

            def norm(tag, width, final=False):
                pe.wait_ge(*t.free(f"norm {tag}"))
                ps = bank_of(f"norm {tag}")
                for kt in range(KT):
                    pe.wait_ge(*t.next(square_ready))
                    last = mm(ps[:, 0:width], ones, square[:, kt % 2, 0:width], start=kt == 0, stop=kt == KT - 1)
                    if kt < KT - 1:
                        last.then_inc(square_used, 1)
                last.then_inc(full_of(f"norm {tag}"), 1)

            def columns(u, width, n_k, names, hi, lo, before=None):
                sl = arrived(u)
                for j in range(2):
                    pe.wait_ge(*t.free(names[j]))
                    ps = bank_of(names[j])
                    for kt in range(n_k):
                        if before:
                            before(kt)
                        w = slice(kt * 256 + j * P, kt * 256 + j * P + P)
                        last = mm3(ps[:, 0:width], whi[sl][:, w], wlo[sl][:, w], hi[:, kt, 0:width],
                                   lo[:, kt, 0:width], kt == 0, kt == n_k - 1)
                last.then_inc(unit_used, 1)

            for l in range(DEPTH):
                W = NT if l == 0 else SEQ
                norm(f"1 {l}", NT)
                done = [0]

                def u_part(kt):
                    if done[0] <= kt:
                        pe.wait_ge(*t.next(u_lo_ready))
                        done[0] += 1

                u = UNIT_AT[f"conv{l}"]
                for c in range(6):
                    columns(u + c, W, KT, [f"conv {l} {c} {j}" for j in range(2)], u_hi, u_lo, u_part)
                u = UNIT_AT[f"qkvo{l}"]
                for c, name in enumerate("qkvo"):
                    for part in range(2):
                        sl = arrived(u + 2 * c + part)
                        for tt in range(TT if l == 0 or name in "kv" else 2):
                            if part == 0:
                                pe.wait_ge(*t.free(f"{name} {l} {tt}"))
                            ps = bank_of(f"{name} {l} {tt}")
                            for kk in range(4):
                                kt = 4 * part + kk
                                w = slice(kk * 512, kk * 512 + 512)
                                last = mm3(ps[:, :], u_hi[:, kt, tt * P:tt * P + P], u_lo[:, kt, tt * P:tt * P + P],
                                           whi[sl][:, w], wlo[sl][:, w], kt == 0, kt == KT - 1)
                        last.then_inc(unit_used, 1)
                pe.wait_ge(*t.free(f"gates {l}"))
                ps = bank_of(f"gates {l}")
                for tt in range(TT):
                    for kt in range(KT):
                        last = mm3(ps[:, tt * 16:tt * 16 + 16], u_hi[:, kt, tt * P:tt * P + P],
                                   u_lo[:, kt, tt * P:tt * P + P], wg_hi[:, l, kt, :], wg_lo[:, l, kt, :],
                                   kt == 0, kt == KT - 1)
                last.then_inc(full_of(f"gates {l}"), 1)
                for tt in range(TT if l == 0 else 2):
                    pe.wait_ge(*t.read(f"q {l} {tt}"))
                    pe.wait_ge(*t.read(f"k {l} {tt}"))
                    for name, src in ((f"qT {l} {tt}", q), (f"kT {l} {tt}", k)):
                        pe.wait_ge(*t.free(name))
                        ps = bank_of(name)
                        for hd in range(HEADS):
                            last = nc.tensor.transpose(ps[:, hd * P:hd * P + P], src[:, tt, hd * P:hd * P + P], ident)
                        last.then_inc(full_of(name), 1)
                pe.wait_ge(*t.free(f"cum {l}"))
                ps = bank_of(f"cum {l}")
                pe.wait_ge(*t.next(logf_ready))
                for d in range(2):
                    dst = ps[:, 0:32].rearrange("p (t d h) -> p t d h", d=2, h=HEADS)[:, :, d, :]
                    mm(dst, tri[d], lf[:, :, :].rearrange("p (t d) h -> p t d h", d=2)[:, :, d, :], start=True, stop=True)
                mm(ps[:, 32:64], ones, lf[:, :, :].rearrange("p a h -> p (a h)"), start=True, stop=True
                   ).then_inc(full_of(f"cum {l}"), 1)
                for a in range(2 * TT):
                    pe.wait_ge(*t.free(f"G {l} {a}"))
                    ps = bank_of(f"G {l} {a}")
                    pe.wait_ge(*t.next(diag_ready))
                    mm(ps[:, :], ones, diag[:, a % 2, :], start=True, stop=True).then_inc(full_of(f"G {l} {a}"), 1)
                for tt in range(TT if l == 0 else 2):
                    pe.wait_ge(*t.read(f"qT {l} {tt}"))
                    pe.wait_ge(*t.read(f"kT {l} {tt}"))
                for tt in range(TT):
                    pe.wait_ge(*t.read(f"v {l} {tt}"))
                pe.wait_ge(v_ones, t.at(v_ones, l + 1))
                previous = {}

                def spread_m(i):
                    tt, d, _ = outputs[l][i]
                    name = f"M {l} {tt} {d}"
                    pe.wait_ge(*t.free(name))
                    ps = bank_of(name)
                    pe.wait_ge(*t.next(diag_ready))
                    mm(ps[:, :], ones, diag[:, i % 2, :], start=True, stop=True).then_inc(full_of(name), 1)

                def scores(i):
                    tt, d, _ = outputs[l][i]
                    c = slice(tt * P, tt * P + P)
                    name = f"S {l} {tt} {d}"
                    pe.wait_ge(*t.free(name))
                    ps = bank_of(name)
                    for hd in range(HEADS):
                        last = mm(ps[:, hd * P:hd * P + P], kT[:, hd, c], qT[:, hd, c], start=True, stop=True)
                    last.then_inc(full_of(name), 1)

                spread_m(0)
                scores(0)
                for tt, d, kk in scan_steps():
                    full = (tt, d, kk) in outputs[l]
                    i = outputs[l].index((tt, d, kk)) if full else None
                    c = slice(tt * P, tt * P + P)
                    if full:
                        if kk:
                            for part in range(2):
                                pe.wait_ge(*t.read(previous[d][part]))
                                name = f"int {l} {tt} {d} {part}"
                                pe.wait_ge(*t.free(name))
                                ps = bank_of(name)
                                for j in range(2):
                                    last = mm(ps[:, 256 * j:256 * j + HE], qT[:, 2 * part + j, c],
                                              state[:, d, 2 * part + j, :], start=True, stop=True)
                                last.then_inc(full_of(name), 1)
                    if kk < 3:
                        pe.wait_ge(*t.next(kw_ready))
                        for part in range(2):
                            name = f"upd {l} {tt} {d} {part}"
                            pe.wait_ge(*t.free(name))
                            ps = bank_of(name)
                            for j in range(2):
                                hd = 2 * part + j
                                last = mm(ps[:, 256 * j:256 * j + HE], kw[:, hd * P:hd * P + P], v[:, tt, hd, :],
                                          start=True, stop=True)
                            last.then_inc(full_of(name), 1)
                        previous[d] = [f"upd {l} {tt} {d} {part}" for part in range(2)]
                    if full:
                        more = i + 1 < len(outputs[l])
                        if more:
                            spread_m(i + 1)
                        pe.wait_ge(*t.read(f"S {l} {tt} {d}"))
                        for part in range(2):
                            name = f"num {l} {tt} {d} {part}"
                            pe.wait_ge(*t.free(name))
                            ps = bank_of(name)
                            for j in range(2):
                                hd = 2 * part + j
                                last = mm(ps[:, 256 * j:256 * j + HE], t512[:, i % 2, hd * P:hd * P + P],
                                          v[:, tt, hd, :], start=True, stop=True)
                            last.then_inc(full_of(name), 1)
                        if more:
                            scores(i + 1)
                for tt in range(TT if l == 0 else 2):
                    name = f"yT {l} {tt}"
                    pe.wait_ge(*t.free(name))
                    ps = bank_of(name)
                    pe.wait_ge(*t.next(merged))
                    for hd in range(HEADS):
                        last = nc.tensor.transpose(ps[:, hd * P:hd * P + P], hacc[:, tt, hd * P:hd * P + P], ident)
                    last.then_inc(full_of(name), 1)
                pe.wait_ge(*t.next(conv_lo))
                for tt in range(TT if l == 0 else 2):
                    pe.wait_ge(*t.read(f"yT {l} {tt}"))
                u = UNIT_AT[f"out{l}"]
                for c in range(4):
                    columns(u + c, W, KT, [f"out {l} {c} {j}" for j in range(2)], u_hi, u_lo)
                norm(f"2 {l}", W)
                pe.wait_ge(*t.next(u_lo_ready, KT))
                if l == 0:
                    def group(g):
                        u, nf = UNIT_AT[f"ffn{g}"], GROUPS[g]
                        for c in range(nf + 4):
                            names = [f"ffn {g} {c} {j}" for j in range(2)]
                            if c < nf:
                                columns(u + c, NT, KT, names, u_hi, u_lo)
                            else:
                                if c == nf:
                                    pe.wait_ge(*t.next(hid_lo_ready, nf))
                                columns(u + c, NT, nf, names, hid_hi, hid_lo)
                    with t.loop(2, unit_loops("ffn", {**fill_loops("ffn"), hid_lo_ready: 8}), 2):
                        group(0)
                    group(2)

            pe.wait_ge(*t.free("logits"))
            ps = bank_of("logits")
            for tt in range(2):
                for kt in range(KT):
                    c = slice(tt * P, tt * P + P)
                    last = mm3(ps[:, tt * NE:tt * NE + NE], u_hi[:, kt, c], u_lo[:, kt, c], ro_hi[:, kt, :],
                               ro_lo[:, kt, :], kt == 0, kt == KT - 1)
            last.then_inc(full_of("logits"), 1)

            def token_major(i):
                pe.wait_ge(*t.free(f"utok {i}"))
                ps = bank_of(f"utok {i}")
                tt, half, src = i // 4, i // 2 % 2, (u_hi, u_lo)[i % 2]
                for j in range(4):
                    last = nc.tensor.transpose(ps[:, j * P:j * P + P],
                                               src[:, 4 * half + j, tt * P:tt * P + P].bitcast(f32), ident)
                last.then_inc(full_of(f"utok {i}"), 1)

            for i in range(4):
                token_major(i)
            pe.wait_ge(*t.free("count"))
            ps = bank_of("count")
            pe.wait_ge(*t.next(sel_ready))
            mm(ps[:, 0:8], tri[0], sel[:, 0, :], start=True, stop=True)
            mm(ps[:, 8:16], ones, sel[:, 0, :], start=True, stop=False)
            mm(ps[:, 8:16], tri[0], sel[:, 1, :], start=False, stop=True)
            mm(ps[:, 16:24], ones, sel[:, 0, :], start=True, stop=False)
            mm(ps[:, 16:24], ones, sel[:, 1, :], start=False, stop=True).then_inc(full_of("count"), 1)
            for i in range(4, 8):
                token_major(i)
            pe.wait_ge(npass_ready, 1)
            passes = pe.value_load(npass[0:1, 0:1], min_val=1, max_val=2)
            for i in range(8):
                pe.wait_ge(*t.read(f"utok {i}"))

            def gather(names, e):
                for i in range(4):
                    src = (utok_hi, utok_lo)[i % 2]
                    pe.wait_ge(*t.free(names[i]))
                    ps = bank_of(names[i])
                    for j in range(4):
                        kt = 4 * (i // 2) + j
                        for tt in range(2):
                            last = mm(ps[:, j * P:j * P + P], src[:, tt, kt * P:kt * P + P],
                                      pick[:, tt, ds(e, 1), :].rearrange("p a s -> p (a s)") if not isinstance(e, int)
                                      else pick[:, tt, e, :], start=tt == 0, stop=tt == 1)
                    last.then_inc(full_of(names[i]), 1)

            def give_back(which, e):
                for half in range(2):
                    name = f"y {half}"
                    pe.wait_ge(*(t.free(name) if which == "back" else t.read(name, later_turns=NE - 1)))
                for i in range(4):
                    pe.wait_ge(*t.free(f"{which} {i}"))
                    ps = bank_of(f"{which} {i}")
                    for j in range(2):
                        kt = 2 * i + j
                        for part, y in enumerate((y_hi, y_lo)):
                            last = mm(ps[:, 256 * j:256 * j + 256], y[:, kt * P:kt * P + P],
                                      pickT[:, ds(e, 1), :].rearrange("p a n -> p (a n)"),
                                      start=part == 0, stop=part == 1)
                    last.then_inc(full_of(f"{which} {i}"), 1)

            u = UNIT_AT["moe"]
            with t.loop(passes, {**unit_loops("pass", fill_loops("pass")), pick_ready: 1,
                                 hidden_ready: 0}, 1):
                pe.wait_ge(*t.next(pick_ready))
                for i in range(4):
                    pe.wait_ge(*t.free(f"PT {i}"))
                    ps = bank_of(f"PT {i}")
                    for ee in range(2):
                        for tt in range(2):
                            c = ee * SEQ + tt * P
                            last = nc.tensor.transpose(ps[:, c:c + P], pick[:, tt, 2 * i + ee, :].bitcast(f32), ident)
                    last.then_inc(full_of(f"PT {i}"), 1)
                gather([f"gather {i}" for i in range(4)], 0)
                for i in range(4):
                    if i >= 2:
                        pe.wait_ge(*t.read(f"gather {i}"))
                    pe.wait_ge(*t.read(f"PT {i}"))
                pe.wait_ge(*t.free("gslot"))
                ps = bank_of("gslot")
                for ee in range(NE):
                    for tt in range(2):
                        last = mm(ps[:, ee:ee + 1], pick[:, tt, ee, :].bitcast(f32), gate[:, tt, ee:ee + 1],
                                  start=tt == 0, stop=tt == 1)
                last.then_inc(full_of("gslot"), 1)
                with t.loop(NE, unit_loops("expert", fill_loops("expert")), NE) as e:
                    for j, (m, c, part) in enumerate(EXPERT_UNITS):
                        last_part = j + 1 == UPE or EXPERT_UNITS[j + 1][:2] != (m, c)
                        if m != "w2":
                            w = CHUNKS[c]
                            n_k = UNIT // w
                            b = 2 * (c % 2) + (m == "w3")
                            if part == 0:
                                pe.wait_ge(*t.free(f"{m} {c}"))
                            sl = arrived(u + j)
                            for kk in range(n_k):
                                kt = part * 4 + kk
                                r = slice(kk * w, kk * w + w)
                                last = mm3(bank[b][:, 0:w], xe_hi[:, kt, :], xe_lo[:, kt, :], whi[sl][:, r],
                                           wlo[sl][:, r], kt == 0, kt == KT - 1)
                        else:
                            if j == 8:
                                pe.wait_ge(*t.free("y 0"))
                                pe.wait_ge(*t.free("y 1"))
                            if part == 0:
                                pe.wait_ge(*t.read(f"T {c}"))
                            if j == UPE - 1:
                                for i in (2, 3, 1):
                                    pe.wait_ge(*t.read(f"next {i}"))
                            sl = arrived(u + j)
                            for kk in range(2):
                                ft = 2 * part + kk
                                for half in range(2):
                                    r = slice(kk * 1024 + half * 512, kk * 1024 + half * 512 + 512)
                                    last = mm3(bank[6 + half][:, :], hT_hi[:, c % 2, ft, :], hT_lo[:, c % 2, ft, :],
                                               whi[sl][:, r], wlo[sl][:, r], c == 0 and ft == 0,
                                               j == UPE - 1 and kk == 1)
                        last.then_inc(unit_used, 1)
                        if j == BACK_AT:
                            give_back("back", e)
                        if j in T_AT:
                            c_t = T_AT[j]
                            pe.wait_ge(*t.read(f"w3 {c_t}"))
                            pe.wait_ge(*t.free(f"T {c_t}"))
                            ps = bank_of(f"T {c_t}")
                            for ft in range(CHUNKS[c_t] // P):
                                last = nc.tensor.transpose(ps[:, ft * P:ft * P + P],
                                                           hid[:, c_t % 2, ft * P:ft * P + P], ident)
                            last.then_inc(full_of(f"T {c_t}"), 1)
                        if j == NEXT_AT:
                            gather([f"next {i}" for i in range(4)], e + 1)
                give_back("final back", NE)
            t.loops.append((passes - 1, fill_loops("pass")))
            norm("f", SEQ, final=True)

        @block.gpsimd
        def _(pool):
            t = Counts(pool)
            TTp = nc.gpsimd.tensor_tensor

            def wide(x):
                return x.unsqueeze(2).broadcast_to([P, HEADS, P])

            def diagonal(src, a, slot):
                TTp(diag[:, slot, :].rearrange("p (h s) -> p h s", h=HEADS),
                    ident.unsqueeze(1).broadcast_to([P, HEADS, P]), wide(src[:, a, :]), ALU.mult).then_inc(diag_ready, 1)

            pool.wait_ge(params_loaded, 16)
            for l in range(DEPTH):
                W = NT if l == 0 else SEQ
                pool.wait_ge(*t.next(gg_ready))
                for a in range(2 * TT):
                    if a >= 2:
                        pool.wait_ge(*t.full(f"G {l} {a - 2}"))
                    diagonal(gg, a, a % 2)
                for tt in range(TT):
                    pool.wait_ge(*t.read(f"k {l} {tt}"))
                pool.wait_ge(*t.next(exp_done))
                pool.wait_ge(*t.full(f"G {l} {2 * TT - 2}"))

                def diagonal_m(i):
                    tt, d, _ = outputs[l][i]
                    diagonal(m_t, 2 * tt + d, i % 2)

                diagonal_m(0)
                updates = [s for s in scan_steps() if s[2] < 3]
                for n, (tt, d, kk) in enumerate(scan_steps()):
                    full = (tt, d, kk) in outputs[l]
                    if kk < 3:
                        if n:
                            before = updates[n - 1]
                            pool.wait_ge(*t.full(f"upd {l} {before[0]} {before[1]} 1"))
                        TTp(kw[:, :].rearrange("p (h s) -> p h s", h=HEADS),
                            k[:, tt, :].rearrange("p (h s) -> p h s", h=HEADS),
                            wide(e_out[:, 1, 2 * tt + d, :]), ALU.mult).then_inc(kw_ready, 1)
                    if full:
                        i = outputs[l].index((tt, d, kk))
                        if i + 1 < len(outputs[l]):
                            if i:
                                b, bd, _ = outputs[l][i - 1]
                                pool.wait_ge(*t.full(f"M {l} {b} {bd}"))
                            else:
                                pool.wait_ge(*t.full(f"G {l} {2 * TT - 1}"))
                            diagonal_m(i + 1)
                for tt in range(W // P):
                    pool.wait_ge(*t.read(f"o {l} {tt}"))
                for tt in range(W // P):
                    pool.wait_ge(*t.next(normed))
                    TTp(hacc[:, tt, :], hacc[:, tt, :], o[:, tt, :], ALU.mult).then_inc(merged, 1)


def kernel(**inputs):
    import numpy as _np
    import concourse.bacc as _bacc
    from concourse import mybir as _mybir
    from concourse.bass_utils import run_bass_kernel_spmd as _run

    a = {name: _np.asarray(x) for name, x in inputs.items()}
    f32 = _np.float32

    stream = _np.zeros((N_UNITS + 2, P, UNIT), f32)
    at = [0]

    def put(block):
        rows, n = block.shape
        w = rows // P * n
        stream[at[0], :, 0:w].reshape(P, rows // P, n)[:] = block.reshape(rows // P, P, n).transpose(1, 0, 2)
        at[0] += 1

    for l in range(DEPTH):
        for c in range(0, 6 * D, 512):
            for half in range(2):
                put(a["w_ada"][l][512 * half:512 * half + 512, c:c + 512])
    for l in range(DEPTH):
        w = a["w_in"][l]
        assert at[0] == UNIT_AT[f"conv{l}"]
        for c in range(CT):
            s = slice(c * P, c * P + P)
            put(_np.concatenate([w[:, CONV:2 * CONV][:, s], w[:, 2 * CONV:3 * CONV][:, s]], axis=1))
        for c in range(2):
            put(w[:, 256 * c:256 * c + 256])
        q0 = 3 * CONV
        for c0 in (q0, q0 + 512, q0 + 1024, q0 + 1536 + 16):
            for half in range(2):
                put(w[512 * half:512 * half + 512, c0:c0 + 512])
        for c in range(4):
            put(a["w_out"][l][:, 256 * c:256 * c + 256])
        if l == 0:
            f0 = 0
            for nf in GROUPS:
                for c in range(f0, f0 + nf * P, 256):
                    put(a["ffn_w1"][0][:, c:c + 256])
                    put(a["ffn_w3"][0][:, c:c + 256])
                for c in range(4):
                    put(a["ffn_w2"][0][f0:f0 + nf * P, 256 * c:256 * c + 256])
                f0 += nf * P
    for e in range(NE):
        for m, c, part in EXPERT_UNITS:
            f0, w = 512 * c, CHUNKS[c]
            if m == "w2":
                put(a["moe_w2"][0, e][f0 + 256 * part:f0 + 256 * part + 256])
            elif w == 512:
                put(a["moe_" + m][0, e][512 * part:512 * part + 512, f0:f0 + w])
            else:
                put(a["moe_" + m][0, e][:, f0:f0 + w])
    assert at[0] == N_UNITS
    stream[N_UNITS:] = stream[UNIT_AT["moe"]:UNIT_AT["moe"] + 2]

    tokens = _np.concatenate([a["x"][0], a["ctx"][0]]).T.reshape(KT, P, NT).transpose(1, 0, 2)
    params = _np.zeros((P, NPAR), f32)

    def param(name, block):
        lo, hi = COL[name]
        params[:, lo:hi] = _np.broadcast_to(block, (P, hi - lo))

    def by_channel(x):
        x = x.reshape(-1, P, x.shape[1] if x.ndim > 1 else 1)
        return x.transpose(1, 0, 2).reshape(P, -1)

    row, col = _np.arange(P)[:, None], _np.arange(P)[None, :]
    param("ident", _np.eye(P, dtype=f32))
    param("ones", f32(1))
    param("mask_low", _np.where(col <= row, f32(0), f32(NEG)))
    param("mask_up", _np.where(col >= row, f32(0), f32(NEG)))
    param("up01", (row <= col).astype(f32))
    param("low01", (row >= col).astype(f32))
    param("iota", _np.arange(P, dtype=f32))
    param("comb", (_np.arange(P)[:, None] % 2 == _np.arange(2)[None, :]).astype(f32))
    param("rank", _np.arange(NE, 0, -1).astype(f32))
    param("eps", f32(EPS))
    param("cond", by_channel(_np.stack([a["c"][0], a["c_ctx"]], axis=1)))
    param("final_g", by_channel(a["final_norm_g"]))
    param("router", by_channel(a["moe_router"][0]))
    param("b_ada", by_channel(a["b_ada"].reshape(-1)))
    for l in range(DEPTH):
        param(f"norm1_{l}", by_channel(a["norm1_g"][l]))
        param(f"norm2_{l}", by_channel(a["norm2_g"][l]))
        param(f"conv_{l}", by_channel(a["conv_w"][l].T))
        param(f"mnorm_{l}", by_channel(a["mlstm_norm_g"][l]))
        param(f"bgates_{l}", a["b_gates"][l].reshape(-1))
        param(f"wgates_{l}", by_channel(a["w_in"][l][:, 3 * CONV + 1536:3 * CONV + 1552]))

    nc = _bacc.Bacc("TRN2", target_bir_lowering=False, num_devices=1)
    arrays = {"stream": stream, "tokens": _np.ascontiguousarray(tokens), "params": params}
    args = [nc.dram_tensor(name, x.shape, _mybir.dt.from_np(x.dtype), kind="ExternalInput").ap()
            for name, x in arrays.items()]
    out = nc.dram_tensor("out", (P, KT, SEQ), _mybir.dt.float32, kind="ExternalOutput").ap()
    backbone(nc, *args, out)
    r = _run(nc, [arrays], core_ids=[0])
    got = r.results[0]["out"]
    return _np.ascontiguousarray(got.transpose(2, 1, 0)).reshape(1, SEQ, D)
```

```python
from contextlib import ExitStack, contextmanager

import numpy as np
import concourse.bass as bass
from concourse import mybir

P = 128
D = 1024
KT = D // P
SEQ, CTX = 256, 256
NT = SEQ + CTX
TT = NT // P
GRID_W = 64
CONV = 512
CT = CONV // P
HEADS, HD = 4, 128
DFF = 2816
FT = DFF // P
NE = 8
DEPTH = 2
EPS = 1e-6
NEG = -1e30
UNIT = 2048
SLOTS = 3
HALVES = [slice(0, UNIT // 2), slice(UNIT // 2, UNIT)]
HE = HD + 1
GROUPS = [8, 8, 6]
CHUNKS = [512] * 5 + [256]
UPE = 33
ADA_UNITS = DEPTH * 6 * D // 256
ADA_TURNS = ADA_UNITS // 6 - 1
LAT_STEPS = {0: [2, 3, 0, 1], 1: [3, 2, 1, 0]}

PARAMS = [("ident", P), ("ones", P), ("mask_low", P), ("mask_up", P), ("up01", P), ("low01", P), ("iota", P),
          ("rank", NE), ("comb", 2), ("eps", 1), ("cond", KT * 2), ("final_g", KT), ("router", KT * NE), ("b_ada", DEPTH * 48)]
for _l in range(DEPTH):
    PARAMS += [(f"norm1_{_l}", KT), (f"norm2_{_l}", KT), (f"conv_{_l}", CT * 3), (f"mnorm_{_l}", CT),
               (f"bgates_{_l}", 16), (f"wgates_{_l}", KT * 16)]
COL, _n = {}, 0
for _name, _w in PARAMS:
    COL[_name] = (_n, _n + _w)
    _n += _w
NPAR = _n


def expert_units():
    out = []
    for c, w in enumerate(CHUNKS):
        parts = 2 if w == 512 else 1
        out += [("w1", c, h) for h in range(parts)] + [("w3", c, h) for h in range(parts)]
        if c:
            out += [("w2", c - 1, h) for h in range(2)]
    return out + [("w2", len(CHUNKS) - 1, 0)]


EXPERT_UNITS = expert_units()
assert len(EXPERT_UNITS) == UPE
LAST_CHUNK = len(CHUNKS) - 1
T_AT = {j: c - 1 for j, (m, c, part) in enumerate(EXPERT_UNITS)
        if m == "w1" and c and EXPERT_UNITS[j + 1][:2] != (m, c)}
NEXT_AT = EXPERT_UNITS.index(("w3", LAST_CHUNK, 0))
T_AT[NEXT_AT + 1] = LAST_CHUNK
BACK_AT = 1


def first_units():
    at, n = {}, 0
    for name, k in ([("ada", ADA_UNITS), ("conv0", 6), ("qkov0", 8), ("out0", 4)]
                    + [(f"ffn{g}", f + 4) for g, f in enumerate(GROUPS)]
                    + [("conv1", 6), ("qkov1", 8), ("out1", 4), ("moe", NE * UPE)]):
        at[name] = n
        n += k
    return at, n


UNIT_AT, N_UNITS = first_units()
assert (N_UNITS + 2) % SLOTS == 0 and NE * UPE % SLOTS == 0


class Fills:

    def __init__(self):
        self.n, self.at = [0] * 16, {}

    def add(self, name, bank, unit=None):
        self.n[bank] += 1
        if unit is None:
            self.n[8 + bank] += 1
        self.at[name] = (bank, self.n[bank], unit, self.n[8 + bank])

    def repeat(self, before, trips):
        per = [b - a for a, b in zip(before, self.n)]
        self.n = [b + (trips - 1) * p for b, p in zip(self.n, per)]
        return per


def turned_in(l, n):
    t = n - 4
    return [f"qT {l} {t}", f"kT {l} {t}"] if t >= 0 and (l == 0 or t < 2) else []


def beside(l, n):
    if n == 0:
        return [f"gates {l}"]
    if n == 1:
        return [f"cum {l}"]
    return [f"G {l} {a}" for a in (2 * n - 4, 2 * n - 3)] if n < 6 else []


def plan_fills():
    f, per = Fills(), {}
    f.add("mod", 7, ADA_UNITS - 1)
    before = list(f.n)
    for c in range(3):
        f.add(f"ada {c}", c, 2 * c + 1)
    per["ada"] = f.repeat(before, ADA_TURNS)
    for c in range(3):
        f.add(f"ada last {c}", c, 6 * ADA_TURNS + 2 * c + 1)

    def norm(tag, bank=0):
        f.add(f"norm {tag}", bank)

    for l in range(DEPTH):
        norm(f"1 {l}", 3 if l == 0 else 2 * (GROUPS[2] % 4))
        u = UNIT_AT[f"conv{l}"]
        for k in range(6):
            for j in range(2):
                f.add(f"conv {l} {k} {j}", 2 * (k % 4) + j, u + k)
        u = UNIT_AT[f"qkov{l}"]
        f.add(f"gatesT {l}", 6)
        for c, name in enumerate("qkov"):
            for t in range(TT if l == 0 or name in "kv" else 2):
                f.add(f"{name} {l} {t}", (4 * c + t) % 6, u + 2 * c + 1)
        for n in range(8):
            for name in (turned_in(l, n) + beside(l, n)):
                f.add(name, 7 if name[:2] in ("qT", "ga") or name[0] == "G" and int(name[-1]) % 2 else 6)
        for t, d, k in scan_steps():
            if l == 0 or t < 2:
                f.add(f"M {l} {t} {d}", 4)
                f.add(f"S {l} {t} {d}", 5)
                f.add(f"num {l} {t} {d} 0", 2)
                f.add(f"num {l} {t} {d} 1", 3)
                if k:
                    f.add(f"int {l} {t} {d} 0", 0)
                    f.add(f"int {l} {t} {d} 1", 1)
            if k < 3:
                f.add(f"upd {l} {t} {d} 0", 6)
                f.add(f"upd {l} {t} {d} 1", 7)
        for t in range(TT if l == 0 else 2):
            f.add(f"yT {l} {t}", 6 + t % 2)
        for k in range(4):
            for j in range(2):
                f.add(f"out {l} {k} {j}", 2 * (k % 4) + j, UNIT_AT[f"out{l}"] + k)
        norm(f"2 {l}")
        if l == 0:
            def group(g):
                u, nf = UNIT_AT[f"ffn{g}"], GROUPS[g]
                for k in range(nf + 4):
                    for j in range(2):
                        f.add(f"ffn {g} {k} {j}", 2 * (k % 4) + j, u + k)
            before = list(f.n)
            group(0)
            per["ffn"] = f.repeat(before, 2)
            group(2)
    f.add("logitsT", 1)
    for i in range(7):
        f.add(f"utok {i}", (2, 3, 4, 5, 6, 7, 0)[i])
    f.add("logits", 1)
    f.add("utok 7", 2)
    f.add("count", 1)
    before_pass = list(f.n)
    for i in range(4):
        f.add(f"gather {i}", 4 + i)
    f.add("gslot", 3)
    for i in range(4):
        f.add(f"PT {i}", i)
    before, u = list(f.n), UNIT_AT["moe"]
    for j, (m, c, h) in enumerate(EXPERT_UNITS):
        last = j + 1 == UPE or EXPERT_UNITS[j + 1][:2] != (m, c)
        if m != "w2" and last:
            f.add(f"{m} {c}", 2 * (c % 2) + (m == "w3"), u + j)
        if j == UPE - 1:
            f.add("y 0", 6, u + j)
            f.add("y 1", 7, u + j)
        if j == BACK_AT:
            for i in range(4):
                f.add(f"back {i}", 4 + i)
        if j in T_AT:
            f.add(f"T {T_AT[j]}", 4 + T_AT[j] % 2)
        if j == NEXT_AT:
            for i in range(4):
                f.add(f"next {i}", (5, 4, 0, 1)[i])
    per["expert"] = f.repeat(before, NE)
    for i in range(4):
        f.add(f"final back {i}", 4 + i)
    per["pass"] = [b - a for a, b in zip(before_pass, f.n)]
    f.add("norm f", 0)
    return f, per


def scan_steps():
    return [(LAT_STEPS[d][k], d, k) for k in range(4) for d in range(2)]


FILLS, FILLS_PER = plan_fills()


def backbone(nc, stream, tokens, params, out):
    f32, f32r, i32 = mybir.dt.float32, mybir.dt.float32r, mybir.dt.int32
    ACT, ALU, AX = mybir.ActivationFunctionType, mybir.AluOpType, mybir.AxisListType
    ds = bass.ds

    ctx = ExitStack()
    with ctx:
        def tensors(stack):
            def sb(name, shape, dt=f32):
                return stack.enter_context(nc.sbuf_tensor(name, shape, dt))
            return sb

        sb = tensors(ctx)
        raw = [sb(f"raw{i}", [P, UNIT]) for i in range(SLOTS)]
        whi = [sb(f"whi{i}", [P, UNIT], f32r) for i in range(SLOTS)]
        wlo = [sb(f"wlo{i}", [P, UNIT], f32r) for i in range(SLOTS)]
        h = sb("h", [P, KT, NT])
        u_hi = sb("u_hi", [P, KT, NT], f32r)
        u_lo = sb("u_lo", [P, KT, NT], f32r)
        par = sb("par", [P, NPAR])
        cond4 = sb("cond4", [P, KT, 4], f32r)
        condf = sb("condf", [P, KT, 2])
        wg_hi = sb("wg_hi", [P, DEPTH, KT, 16], f32r)
        wg_lo = sb("wg_lo", [P, DEPTH, KT, 16], f32r)
        ro_hi = sb("ro_hi", [P, KT, NE], f32r)
        ro_lo = sb("ro_lo", [P, KT, NE], f32r)
        mod = sb("mod", [P, DEPTH * 48, 2])
        gain = sb("gain", [P, DEPTH, 2, KT, 2])
        npass = sb("npass", [1, 1], i32)
        with ExitStack() as stack:
            sb = tensors(stack)
            sb("buffers_of_norm", [P, 6, NT])
            ada_row = sb("ada_row", [4, 3, 512])
        with ExitStack() as stack:
            sb = tensors(stack)
            square = sb("square", [P, 2, NT])
            std = sb("std", [P, NT])
            rstd = sb("rstd", [P, NT])
            scaled = sb("scaled", [P, 2, NT])
            result = sb("result", [P, KT, SEQ])
        with ExitStack() as stack:
            sb = tensors(stack)
            q = sb("q", [P, TT, 512])
            k = sb("k", [P, TT, 512])
            v = sb("v", [P, TT, HEADS, HE])
            o = sb("o", [P, TT, 512])
            qT = sb("qT", [P, HEADS, NT])
            kT = sb("kT", [P, HEADS, NT])
            conv = sb("conv", [P, CT, NT])
            hacc = q
            diag = sb("diag", [P, 2, 512])
            t512 = sb("t512", [P, 2, 512])
            inter = sb("inter", [P, HEADS, HE])
            u_sum = sb("u_sum", [P, HEADS, HE])
            kw = sb("kw", [P, 512])
            state = sb("state", [P, 2, HEADS, HE])
            gatesT = kw[0:16, :]
            hh, yprod = diag, t512[:, 0, :]
            gts = sb("gts", [P, TT * 2, 2, HEADS])
            lf = sb("lf", [P, TT * 2, HEADS])
            g_tmp = sb("g_tmp", [P, 2, TT * 2, HEADS])
            cum = sb("cum", [P, 2, TT * 2, HEADS])
            gg = sb("gg", [P, TT * 2, HEADS])
            gmax = sb("gmax", [P, TT * 2, HEADS])
            pmax = sb("pmax", [P, TT * 2, HEADS])
            mprev = sb("mprev", [P, TT * 2, HEADS])
            m_t = sb("m_t", [P, TT * 2, HEADS])
            m_l = sb("m_l", [P, TT * 2, HEADS])
            e_in = sb("e_in", [P, 4, TT * 2, HEADS])
            e_out = sb("e_out", [P, 4, TT * 2, HEADS])
            small = sb("small", [P, 3, HEADS])
            msq = sb("msq", [P, 3, TT, HEADS])
        with ExitStack() as stack:
            sb = tensors(stack)
            sb("squares_of_norm", [P, 2, NT])
            hid_hi = sb("hid_hi", [P, 8, NT], f32r)
            hid_lo = sb("hid_lo", [P, 8, NT], f32r)
            sil0 = sb("sil0", [P, 2, NT])
            hid0 = sb("hid0", [P, 2, NT])
        with ExitStack() as stack:
            sb = tensors(stack)
            pick = sb("pick", [P, 2, NE + 1, P], f32r)
            pickT = sb("pickT", [P, NE + 1, SEQ], f32r)
            utok_hi = sb("utok_hi", [P, 2, D], f32r)
            utok_lo = sb("utok_lo", [P, 2, D], f32r)
            xe_hi = sb("xe_hi", [P, KT, P], f32r)
            xe_lo = sb("xe_lo", [P, KT, P], f32r)
            sil = sb("sil", [P, 2, 512])
            hid = sb("hid", [P, 2, 512])
            hT_hi = sb("hT_hi", [P, 2, 4, P], f32r)
            hT_lo = sb("hT_lo", [P, 2, 4, P], f32r)
            y_hi = sb("y_hi", [P, D], f32r)
            y_lo = sb("y_lo", [P, D], f32r)
            gslot = sb("gslot", [P, NE])
            gate_parts = sb("gate_parts", [P, 2, NE, 2], f32r)
            lgT = sb("lgT", [NE, SEQ])
            gcol = sb("gcol", [P, 1])
            lg = sb("lg", [P, 2, NE])
            sc8 = sb("sc8", [P, 6, 2, NE])
            one1 = sb("one1", [P, 2, NE])
            one2 = sb("one2", [P, 2, NE])
            gate = sb("gate", [P, 2, NE])
            sel = sb("sel", [P, 2, NE])
            slot_of = sb("slot_of", [P, 2, NE])
            s2 = sb("s2", [P, 8, 2])
        bank = [ctx.enter_context(nc.psum_tensor(f"bank{i}", [P, 512], f32)) for i in range(8)]

        def sem(name):
            return ctx.enter_context(nc.semaphore(name))

        raw_loaded = [[sem(f"raw_loaded{i}_{half}") for half in range(2)] for i in range(SLOTS)]
        hi_ready, lo_ready, unit_used = sem("hi_ready"), sem("lo_ready"), sem("unit_used")
        bank_full = [sem(f"bank_full{i}") for i in range(8)]
        bank_read = [sem(f"bank_read{i}") for i in range(8)]
        params_loaded, tokens_loaded, out_stored = sem("params_loaded"), sem("tokens_loaded"), sem("out_stored")
        small_hi, small_lo = sem("small_hi"), sem("small_lo")
        mod_turned, mod_ready = sem("mod_turned"), sem("mod_ready")
        square_ready, square_used = sem("square_ready"), sem("square_used")
        scaled_ready, u_hi_ready, u_lo_ready = sem("scaled_ready"), sem("u_hi_ready"), sem("u_lo_ready")
        conv_hi, conv_lo = sem("conv_hi"), sem("conv_lo")
        v_ones = sem("v_ones")
        gate_arg, gate_log, logf_ready = sem("gate_arg"), sem("gate_log"), sem("logf_ready")
        diag_ready, exp_arg, exp_done = sem("diag_ready"), sem("exp_arg"), sem("exp_done")
        decay_ready, kw_ready = sem("decay_ready"), sem("kw_ready")
        sumsq_ready, root_ready, normed, merged, y_hi_done = (sem("sumsq_ready"), sem("root_ready"), sem("normed"),
                                                              sem("merged"), sem("y_hi_done"))
        gg_ready, pmax_done, hacc_done = sem("gg_ready"), sem("pmax_done"), sem("hacc_done")
        hid_hi_ready, hid_lo_ready = sem("hid_hi_ready"), sem("hid_lo_ready")
        zeros_ready, gates_split = sem("zeros_ready"), sem("gates_split")
        route_arg, route_exp, sel_ready, pick_ready, npass_ready = (
            sem("route_arg"), sem("route_exp"), sem("sel_ready"), sem("pick_ready"), sem("npass_ready"))
        hT_hi_ready, y_hi_ready = sem("hT_hi_ready"), sem("y_hi_ready")
        result_ready = sem("result_ready")
        dve_chain, act_chain = sem("dve_chain"), sem("act_chain")

        class Counts:

            def __init__(self, eng):
                self.eng, self.n, self.loops = eng, {}, []

            def at(self, s, base):
                value = base
                for i, per in self.loops:
                    if per.get(s, 0):
                        assert base > 0, "a wait that may be for zero"
                        value = i * per[s] + value
                return value

            def next(self, s, k=1):
                self.n[s] = self.n.get(s, 0) + k
                return s, self.at(s, self.n[s])

            @contextmanager
            def loop(self, trips, per, count=None):
                before = dict(self.n)
                with self.eng.Fori(0, trips) as i:
                    self.loops.append((i, per))
                    yield i
                    self.loops.pop()
                for s, n in self.n.items():
                    step = n - before.get(s, 0)
                    assert step == per.get(s, 0), (s, step, per.get(s, 0))
                    self.n[s] += (count - 1) * step

            def full(self, name):
                b, _, unit, n = FILLS.at[name]
                s, n = (bank_full[b], n) if unit is None else (unit_used, unit + 1)
                return s, self.at(s, n)

            def read(self, name, later_turns=0):
                b, n = FILLS.at[name][:2]
                return bank_read[b], self.at(bank_read[b], n + later_turns * FILLS_PER["expert"][b])

            def free(self, name):
                b, n = FILLS.at[name][:2]
                return bank_read[b], self.at(bank_read[b], n - 1)

        def bank_of(name):
            return bank[FILLS.at[name][0]]

        def fill_loops(kind):
            out = {bank_read[b]: FILLS_PER[kind][b] for b in range(8)}
            out.update({bank_full[b]: FILLS_PER[kind][8 + b] for b in range(8)})
            return out

        def read_of(name):
            return bank_read[FILLS.at[name][0]]

        def full_of(name):
            return bank_full[FILLS.at[name][0]]

        def cols(name):
            a, b = COL[name]
            return par[:, a:b]

        ident, ones = cols("ident"), cols("ones")
        masks = {("A", 0): cols("mask_low"), ("A", 1): cols("mask_up"),
                 ("D", 0): cols("mask_up"), ("D", 1): cols("mask_low")}
        tri = [cols("up01"), cols("low01")]

        def mod_col(l, j, kt, s):
            return mod[:, 48 * l + 8 * j + kt, s:s + 1]

        def sets(width):
            return [(s, slice(256 * s, 256 * s + 256)) for s in range(width // 256)]

        outputs = [scan_steps(), [s for s in scan_steps() if s[0] < 2]]

        UNIT_LOOP = {"ada": 6, "ffn": 12, "expert": UPE, "pass": NE * UPE}

        def unit_loops(kind, extra=None):
            n = UNIT_LOOP[kind]
            out = {unit_used: n, hi_ready: 2 * n, lo_ready: 2 * n,
                   **{s: 16 * n // SLOTS for halves in raw_loaded for s in halves}}
            out.update(extra or {})
            return out

        block = ctx.enter_context(nc.Block())

        @block.sync
        def _(sp):
            sp.dma_start(par[:, :], params).then_inc(params_loaded, 16)

            for n in range(SLOTS):
                for half, c in enumerate(HALVES):
                    sp.dma_start(raw[n][:, c], stream[n, :, c]).then_inc(raw_loaded[n][half], 16)
            sp.dma_start(h[:, :, :], tokens).then_inc(tokens_loaded, 16)

            def load_rest(first, turns, back):
                with sp.Fori(0, turns) as i:
                    for j in range(SLOTS):
                        slot = (first + j) % SLOTS
                        for half, c in enumerate(HALVES):
                            sp.wait_ge(lo_ready, i * (2 * SLOTS) + (2 * (first + j - SLOTS) + half + 1))
                            sp.dma_start(raw[slot][:, c],
                                         stream[ds(i * SLOTS + (first + j - back), 1), :, c]
                                         .rearrange("a p n -> p (a n)")).then_inc(raw_loaded[slot][half], 16)

            load_rest(SLOTS, (N_UNITS + 2 - SLOTS) // SLOTS, 0)
            sp.wait_ge(npass_ready, 1)
            passes = sp.value_load(npass[0:1, 0:1], min_val=1, max_val=2)
            with sp.If(passes > 1):
                load_rest(N_UNITS + 2, NE * UPE // SLOTS, NE * UPE)
            with sp.Else():
                sp.nop()
            for half in range(2):
                sp.wait_ge(result_ready, half + 1)
                c = slice(4 * half, 4 * half + 4)
                sp.dma_start(out[:, c, :], result[:, c, :]).then_inc(out_stored, 16)
            sp.wait_ge(out_stored, 32)

        @block.scalar
        def _(act):
            t = Counts(act)

            def chain(ins):
                ins.then_inc(act_chain, 1)
                act.wait_ge(*t.next(act_chain))

            def split(n):
                if n >= SLOTS:
                    act.wait_ge(unit_used, t.at(unit_used, n - SLOTS + 1))
                for half, c in enumerate(HALVES):
                    loaded = raw_loaded[n % SLOTS][half]
                    act.wait_ge(loaded, t.at(loaded, 16 * (n // SLOTS + 1)))
                    nc.scalar.activation(whi[n % SLOTS][:, c], raw[n % SLOTS][:, c], ACT.Copy).then_inc(hi_ready, 1)

            ahead = [0]

            def split_to(n):
                while ahead[0] <= min(n, N_UNITS - 1):
                    split(ahead[0])
                    ahead[0] += 1

            def copy(dst, src, **kw_):
                return nc.scalar.activation(dst, src, ACT.Copy, **kw_)

            act.wait_ge(params_loaded, 16)
            cd = cols("cond").rearrange("p (k s) -> p k s", s=2)
            chain(nc.scalar.activation(condf[:, :, :], cd, ACT.Silu))
            copy(cond4[:, :, 0:2], condf[:, :, :]).then_inc(small_hi, 1)
            for l in range(DEPTH):
                copy(wg_hi[:, l, :, :], cols(f"wgates_{l}").rearrange("p (k c) -> p k c", c=16)).then_inc(small_hi, 1)
            copy(ro_hi[:, :, :], cols("router").rearrange("p (k c) -> p k c", c=NE)).then_inc(small_hi, 1)

            def squares(kt, width):
                if kt >= 2:
                    act.wait_ge(*t.next(square_used))
                nc.scalar.activation(square[:, kt % 2, 0:width], h[:, kt, 0:width], ACT.Square).then_inc(square_ready, 1)

            def norm(tag, width, final=False):
                act.wait_ge(*t.next(square_used))
                act.wait_ge(*t.full(f"norm {tag}"))
                ps = bank_of(f"norm {tag}")
                nc.scalar.activation(std[:, 0:width], ps[:, 0:width], ACT.Sqrt, bias=cols("eps"),
                                     scale=1.0 / D).then_inc(read_of(f"norm {tag}"), 1)
                if final:
                    return
                which, l = tag.split()
                which, l = int(which) - 1, int(l)
                for kt in range(KT):
                    act.wait_ge(*t.next(scaled_ready))
                    for s, c in sets(width):
                        last = nc.scalar.activation(u_hi[:, kt, c], scaled[:, kt % 2, c], ACT.Identity,
                                                    bias=mod_col(l, 3 * which, kt, s))
                    last.then_inc(u_hi_ready, 1)

            split_to(2 + 5)
            with t.loop(ADA_TURNS - 1, unit_loops("ada", fill_loops("ada")), ADA_TURNS - 1) as i:
                for j in range(6):
                    split(ahead[0] + j)
            ahead[0] = 6 * ADA_TURNS + 2
            act.wait_ge(tokens_loaded, 16)
            for kt in range(KT):
                if kt < 6:
                    split_to(6 * ADA_TURNS + 2 + kt)
                squares(kt, NT)
            for l in range(DEPTH):
                W = NT if l == 0 else SEQ
                norm(f"1 {l}", NT)
                u = UNIT_AT[f"conv{l}"]
                for c in range(6):
                    split_to(u + c + 2)
                    if c < CT:
                        act.wait_ge(*t.full(f"conv {l} {c} 1"))
                        ps = bank_of(f"conv {l} {c} 1")
                        if c >= 2:
                            act.wait_ge(*t.read(f"conv {l} {c - 2} 0"))
                        copy(hh[:, c % 2, 0:W], ps[:, 0:W]).then_inc(read_of(f"conv {l} {c} 1"), 1)
                u = UNIT_AT[f"qkov{l}"]
                for n in range(8):
                    split_to(u + n + 2)
                    if n == 0:
                        act.wait_ge(*t.next(gate_arg))
                        chain(nc.scalar.activation(g_tmp[:, 1], g_tmp[:, 0], ACT.Exp))
                        nc.scalar.activation(g_tmp[:, 0], g_tmp[:, 1], ACT.Ln, bias=1.0).then_inc(gate_log, 1)
                    if n in (1, 5):
                        name = "q" if n == 1 else "o"
                        for tt in range(W // P):
                            act.wait_ge(*t.full(f"{name} {l} {tt}"))
                            ps = bank_of(f"{name} {l} {tt}")
                            if name == "q":
                                ins = copy(q[:, tt, :], ps[:, :])
                            else:
                                ins = nc.scalar.activation(o[:, tt, :], ps[:, :], ACT.Sigmoid)
                            ins.then_inc(read_of(f"{name} {l} {tt}"), 1)
                    if turned_in(l, n):
                        name = turned_in(l, n)[0]
                        tt = n - 4
                        act.wait_ge(*t.full(name))
                        ps = bank_of(name)
                        copy(qT[:, :, tt * P:tt * P + P], ps[:, :].rearrange("p (h s) -> p h s", h=HEADS)
                             ).then_inc(read_of(name), 1)
                    if n == 6:
                        act.wait_ge(*t.next(exp_arg))
                        nc.scalar.activation(e_out[:, :, :, :], e_in[:, :, :, :], ACT.Exp).then_inc(exp_done, 1)
                        act.wait_ge(*t.next(exp_done))

                def decays(i):
                    tt, d, _ = outputs[l][i]
                    act.wait_ge(*t.read(f"M {l} {tt} {d}"))
                    for hd in range(HEADS):
                        c = slice(hd * P, hd * P + P)
                        last = nc.scalar.activation(t512[:, i % 2, c], t512[:, i % 2, c], ACT.Exp,
                                                    bias=gg[:, 2 * tt + d, hd:hd + 1])
                    last.then_inc(decay_ready, 1)

                decays(0)
                for tt in (2, 3):
                    act.wait_ge(*t.full(f"v {l} {tt}"))
                    ps = bank_of(f"v {l} {tt}")
                    copy(v[:, tt, :, 0:HD], ps[:, :].rearrange("p (h d) -> p h d", h=HEADS)
                         ).then_inc(read_of(f"v {l} {tt}"), 1)
                for c in (4, 5):
                    for j in range(2):
                        act.wait_ge(*t.read(f"conv {l} {c} {j}"))
                act.wait_ge(unit_used, t.at(unit_used, u + 8))
                copy(u_hi[:, 0:CT, 0:W], conv[:, :, 0:W]).then_inc(conv_hi, 1)
                split_to(UNIT_AT[f"out{l}"] + 2)
                for i, (tt, d, kk) in enumerate(outputs[l]):
                    a = 2 * tt + d
                    if kk:
                        if i:
                            before = outputs[l][i - 1]
                            act.wait_ge(*t.read(f"num {l} {before[0]} {before[1]} 1"))
                        for part in range(2):
                            act.wait_ge(*t.full(f"int {l} {tt} {d} {part}"))
                            ps = bank_of(f"int {l} {tt} {d} {part}")
                            for j in range(2):
                                hd = 2 * part + j
                                last = copy(inter[:, hd, :], ps[:, 256 * j:256 * j + HE],
                                            scale=e_out[:, 0, a, hd:hd + 1])
                            last.then_inc(read_of(f"int {l} {tt} {d} {part}"), 1)
                    if i + 1 < len(outputs[l]):
                        decays(i + 1)
                act.wait_ge(*t.next(sumsq_ready, W // P))
                nc.scalar.activation(msq[:, 1, 0:W // P, :], msq[:, 0, 0:W // P, :], ACT.Sqrt, bias=cols("eps"),
                                     scale=1.0 / HD).then_inc(root_ready, 1)
                for tt in range(TT if l == 0 else 2):
                    act.wait_ge(*t.full(f"yT {l} {tt}"))
                    ps = bank_of(f"yT {l} {tt}")
                    for hd in range(HEADS):
                        last = copy(u_hi[:, CT + hd, tt * P:tt * P + P], ps[:, hd * P:hd * P + P],
                                    scale=cols(f"mnorm_{l}")[:, hd:hd + 1])
                    last.then_inc(y_hi_done, 1)
                u = UNIT_AT[f"out{l}"]
                for c in range(4):
                    split_to(u + c + 2)
                    if c:
                        for j in range(2):
                            act.wait_ge(*t.read(f"out {l} {c - 1} {j}"))
                            squares(2 * c - 2 + j, W)
                for j in range(2):
                    act.wait_ge(*t.read(f"out {l} 3 {j}"))
                    squares(6 + j, W)
                norm(f"2 {l}", W)
                if l == 0:
                    def group(g, base):
                        u, nf = UNIT_AT[f"ffn{g}"], GROUPS[g]
                        for c in range(nf + 4):
                            split(base + c)
                            if g == 2 and c > nf:
                                for j in range(2):
                                    act.wait_ge(*t.read(f"ffn 2 {c - 1} {j}"))
                                    squares(2 * (c - 1 - nf) + j, NT)
                            if c < nf and c % 2:
                                for j in range(2):
                                    act.wait_ge(*t.full(f"ffn {g} {c - 1} {j}"))
                                    ps = bank_of(f"ffn {g} {c - 1} {j}")
                                    nc.scalar.activation(sil0[:, j, :], ps[:, :], ACT.Silu
                                                         ).then_inc(read_of(f"ffn {g} {c - 1} {j}"), 1)
                                for j in range(2):
                                    act.wait_ge(*t.read(f"ffn {g} {c} {j}"))
                                    copy(hid_hi[:, c - 1 + j, :], hid0[:, j, :]).then_inc(hid_hi_ready, 1)
                    assert ahead[0] == UNIT_AT["ffn0"] + 2
                    with t.loop(2, unit_loops("ffn", fill_loops("ffn")), 2):
                        group(0, ahead[0])
                    ahead[0] += 24
                    group(2, ahead[0])
                    ahead[0] += 10
                    for j in range(2):
                        act.wait_ge(*t.read(f"ffn 2 9 {j}"))
                        squares(6 + j, NT)
            act.wait_ge(*t.next(route_arg))
            nc.scalar.activation(s2[:, 3, :], s2[:, 2, :], ACT.Exp).then_inc(route_exp, 1)
            for i in range(0, 8, 2):
                act.wait_ge(*t.full(f"utok {i}"))
                ps = bank_of(f"utok {i}")
                half, tt = i // 4, i // 2 % 2
                copy(utok_hi[:, tt, 512 * half:512 * half + 512], ps[:, :]).then_inc(read_of(f"utok {i}"), 1)
            act.wait_ge(npass_ready, 1)
            passes = act.value_load(npass[0:1, 0:1], min_val=1, max_val=2)
            assert ahead[0] == UNIT_AT["moe"] + 2

            def gathered(name, i):
                act.wait_ge(*t.full(name))
                ps = bank_of(name)
                copy(xe_hi[:, 2 * i:2 * i + 4, :], ps[:, :].rearrange("p (k s) -> p k s", k=4)
                     ).then_inc(read_of(name), 1)

            with t.loop(passes, {**unit_loops("pass", fill_loops("pass")), y_hi_ready: NE}, 1) as i_pass:
                for i in (0, 2):
                    gathered(f"gather {i}", i)
                for i in range(4):
                    act.wait_ge(*t.full(f"PT {i}"))
                    ps = bank_of(f"PT {i}")
                    copy(pickT[:, 2 * i + 1:2 * i + 3, :], ps[:, :].rearrange("p (e n) -> p e n", e=2)
                         ).then_inc(read_of(f"PT {i}"), 1)
                with t.loop(NE, {**unit_loops("expert", fill_loops("expert")), y_hi_ready: 1}, NE) as e:
                    for j, (m, c, part) in enumerate(EXPERT_UNITS):
                        split(ahead[0] + j)
                        last = j + 1 == UPE or EXPERT_UNITS[j + 1][:2] != (m, c)
                        if m == "w1" and last:
                            act.wait_ge(*t.full(f"w1 {c}"))
                            ps, w = bank_of(f"w1 {c}"), CHUNKS[c]
                            if c >= 2:
                                act.wait_ge(*t.read(f"w3 {c - 2}"))
                            nc.scalar.activation(sil[:, c % 2, 0:w], ps[:, 0:w], ACT.Silu
                                                 ).then_inc(read_of(f"w1 {c}"), 1)
                        if j in T_AT:
                            c_t = T_AT[j]
                            n_t = CHUNKS[c_t] // P
                            act.wait_ge(*t.full(f"T {c_t}"))
                            ps = bank_of(f"T {c_t}")
                            copy(hT_hi[:, c_t % 2, 0:n_t, :], ps[:, 0:n_t * P].rearrange("p (k s) -> p k s", k=n_t)
                                 ).then_inc(hT_hi_ready, 1)
                        if j == NEXT_AT:
                            for i in (0, 2):
                                gathered(f"next {i}", i)
                        if j == UPE - 1:
                            for half in range(2):
                                act.wait_ge(*t.full(f"y {half}"))
                                ps = bank_of(f"y {half}")
                                last_ins = copy(y_hi[:, 512 * half:512 * half + 512], ps[:, :], scale=gcol[:, :])
                            last_ins.then_inc(y_hi_ready, 1)
            t.loops.append((passes - 1, fill_loops("pass")))
            for kt in range(KT):
                act.wait_ge(*t.read(f"final back {kt // 2}"))
                squares(kt, SEQ)
            norm("f", SEQ, final=True)

        @block.vector
        def _(dve):
            t = Counts(dve)
            TTn, STT = nc.vector.tensor_tensor, nc.vector.scalar_tensor_tensor

            def chain(ins):
                ins.then_inc(dve_chain, 1)
                dve.wait_ge(*t.next(dve_chain))

            def split(n):
                for i, c in enumerate(HALVES):
                    dve.wait_ge(hi_ready, t.at(hi_ready, 2 * n + 1 + i))
                    TTn(wlo[n % SLOTS][:, c], raw[n % SLOTS][:, c], whi[n % SLOTS][:, c].bitcast(f32),
                        ALU.subtract).then_inc(lo_ready, 1)

            ahead = [0]

            def split_to(n):
                while ahead[0] <= min(n, N_UNITS - 1):
                    split(ahead[0])
                    ahead[0] += 1

            def wide(x, n, shape):
                return x.unsqueeze(len(shape) - 1).broadcast_to(shape)

            dve.wait_ge(params_loaded, 16)
            dve.wait_ge(*t.next(small_hi))
            TTn(cond4[:, :, 2:4], condf[:, :, :], cond4[:, :, 0:2].bitcast(f32), ALU.subtract).then_inc(small_lo, 1)
            for l in range(DEPTH):
                dve.wait_ge(*t.next(small_hi))
                TTn(wg_lo[:, l, :, :], cols(f"wgates_{l}").rearrange("p (k c) -> p k c", c=16),
                    wg_hi[:, l, :, :].bitcast(f32), ALU.subtract).then_inc(small_lo, 1)
            dve.wait_ge(*t.next(small_hi))
            TTn(ro_lo[:, :, :], cols("router").rearrange("p (k c) -> p k c", c=NE), ro_hi[:, :, :].bitcast(f32),
                ALU.subtract).then_inc(small_lo, 1)

            def ada_rows(name, c):
                dve.wait_ge(*t.full(name))
                nc.vector.tensor_copy(ada_row[:, c, :], bank_of(name)[0:4, :]).then_inc(read_of(name), 1)

            split_to(1)
            with t.loop(ADA_TURNS, unit_loops("ada", fill_loops("ada")), ADA_TURNS) as i:
                for c in range(3):
                    split(ahead[0] + 2 * c)
                    ada_rows(f"ada {c}", c)
                    split(ahead[0] + 2 * c + 1)
            ahead[0] = 6 * ADA_TURNS + 2
            for c in range(3):
                split_to(6 * ADA_TURNS + 2 * c + 2)
                ada_rows(f"ada last {c}", c)
                split_to(6 * ADA_TURNS + 2 * c + 3)
            dve.wait_ge(*t.read("norm 1 0"))
            chain(nc.vector.reciprocal(rstd[:, :], std[:, :]))
            dve.wait_ge(mod_turned, ADA_UNITS // 6)
            ps = bank_of("mod")[:, 0:DEPTH * 48 * 2].rearrange("p (n c) -> p n c", c=2)
            TTn(mod[:, :, :], ps, wide(cols("b_ada"), 2, [P, DEPTH * 48, 2]), ALU.add).then_inc(read_of("mod"), 1)
            dve.wait_ge(*t.read("mod"))
            for l in range(DEPTH):
                for w in range(2):
                    s0 = 48 * l + 8 * (3 * w + 1)
                    last = STT(gain[:, l, w, :, :], mod[:, s0:s0 + 8, :], 1.0,
                               wide(cols(f"norm{w + 1}_{l}"), 2, [P, KT, 2]), ALU.add, ALU.mult)
            last.then_inc(mod_ready, 1)
            dve.wait_ge(*t.next(mod_ready))
            dve.wait_ge(tokens_loaded, 16)

            def norm(tag, width, final=False):
                if tag != "1 0":
                    dve.wait_ge(*t.read(f"norm {tag}"))
                    chain(nc.vector.reciprocal(rstd[:, 0:width], std[:, 0:width]))
                if final:
                    for kt in range(KT):
                        last = STT(result[:, kt, :], h[:, kt, 0:width], cols("final_g")[:, kt:kt + 1],
                                   rstd[:, 0:width], ALU.mult, ALU.mult)
                        if kt % 4 == 3:
                            last.then_inc(result_ready, 1)
                    return

                which, l = tag.split()
                which, l = int(which) - 1, int(l)

                def scale(kt):
                    for s, c in sets(width):
                        last = STT(scaled[:, kt % 2, c], h[:, kt, c], gain[:, l, which, kt, s:s + 1], rstd[:, c],
                                   ALU.mult, ALU.mult)
                    last.then_inc(scaled_ready, 1)
                scale(0)
                scale(1)
                for kt in range(KT):
                    dve.wait_ge(*t.next(u_hi_ready))
                    for s, c in sets(width):
                        last = STT(u_lo[:, kt, c], scaled[:, kt % 2, c], mod_col(l, 3 * which, kt, s),
                                   u_hi[:, kt, c].bitcast(f32), ALU.add, ALU.subtract)
                    last.then_inc(u_lo_ready, 1)
                    dve.wait_ge(*t.next(scaled_ready))
                    if kt + 2 < KT:
                        dve.wait_ge(*t.next(u_lo_ready))
                        scale(kt + 2)
                dve.wait_ge(*t.next(u_lo_ready, 2))

            def residual(name, kt, width, l, j):
                dve.wait_ge(*t.full(name))
                ps = bank_of(name)
                for s, c in sets(width):
                    last = STT(h[:, kt, c], ps[:, c], mod_col(l, j, kt, s), h[:, kt, c], ALU.mult, ALU.add)
                last.then_inc(read_of(name), 1)

            for l in range(DEPTH):
                W = NT if l == 0 else SEQ
                norm(f"1 {l}", NT)
                nc.vector.memset(v[:, :, :, HD:HE], 1.0).then_inc(v_ones, 1)
                u = UNIT_AT[f"conv{l}"]
                cw = cols(f"conv_{l}").rearrange("p (c j) -> p c j", j=3)
                for c in range(6):
                    split_to(u + c + 2)
                    if c < CT:
                        dve.wait_ge(*t.full(f"conv {l} {c} 0"))
                        ps = bank_of(f"conv {l} {c} 0")
                        dve.wait_ge(*t.read(f"conv {l} {c} 1"))
                        TTn(yprod[:, 0:W], ps[:, 0:W], hh[:, c % 2, 0:W], ALU.mult).then_inc(
                            read_of(f"conv {l} {c} 0"), 1)
                        dve.wait_ge(*t.read(f"conv {l} {c} 0"))
                        chain(nc.vector.tensor_scalar(conv[:, c, 0:W], yprod[:, 0:W], cw[:, c, 1:2], None, ALU.mult))
                        rows = [(0, SEQ, GRID_W)] + ([(SEQ, NT, CTX)] if l == 0 else [])
                        for side in range(2):
                            for a, b, w in rows:
                                z = conv[:, c, a:b].rearrange("p (r w) -> p r w", w=w)
                                y = yprod[:, a:b].rearrange("p (r w) -> p r w", w=w)
                                to, of = (slice(1, w), slice(0, w - 1)) if side == 0 else (slice(0, w - 1), slice(1, w))
                                last = STT(z[:, :, to], y[:, :, of], cw[:, c, 2 * side:2 * side + 1], z[:, :, to],
                                           ALU.mult, ALU.add)
                            chain(last)
                    else:
                        for j in range(2):
                            ch = 2 * (c - CT) + j
                            name = f"conv {l} {c} {j}"
                            dve.wait_ge(*t.full(name))
                            ps = bank_of(name)
                            TTn(conv[:, ch, 0:W], conv[:, ch, 0:W], ps[:, 0:W], ALU.mult).then_inc(read_of(name), 1)
                dve.wait_ge(*t.full(f"gatesT {l}"))
                ps = bank_of(f"gatesT {l}")
                nc.vector.tensor_copy(gatesT, ps[0:16, :]).then_inc(read_of(f"gatesT {l}"), 1)
                forget, inputg = gts[:, :, 1, :], gts[:, :, 0, :]

                def prefix_max(a):
                    dve.wait_ge(*t.read(f"G {l} {a}"))
                    nc.vector.tensor_reduce(pmax[:, a, :], t512[:, a % 2, :].rearrange("p (h s) -> p h s", h=HEADS),
                                            AX.X, ALU.max).then_inc(pmax_done, 1)

                def decay_args(i):
                    tt, d, _ = outputs[l][i]
                    name = f"M {l} {tt} {d}"
                    dve.wait_ge(*t.full(name))
                    ps = bank_of(name)
                    STT(t512[:, i % 2, :].rearrange("p (h s) -> p h s", h=HEADS),
                        ps[:, :].rearrange("p (h s) -> p h s", h=HEADS), -1.0,
                        masks["D", d].unsqueeze(1).broadcast_to([P, HEADS, P]), ALU.mult, ALU.add
                        ).then_inc(read_of(name), 1)

                u = UNIT_AT[f"qkov{l}"]
                for n in range(8):
                    split_to(u + n + 2)
                    if n == 3:
                        for tt in range(TT):
                            dve.wait_ge(*t.full(f"k {l} {tt}"))
                            ps = bank_of(f"k {l} {tt}")
                            nc.vector.tensor_scalar(k[:, tt, :], ps[:, :], HD ** -0.5, None,
                                                    ALU.mult).then_inc(read_of(f"k {l} {tt}"), 1)
                    if turned_in(l, n):
                        name = turned_in(l, n)[1]
                        tt = n - 4
                        dve.wait_ge(*t.full(name))
                        ps = bank_of(name)
                        nc.vector.tensor_copy(kT[:, :, tt * P:tt * P + P], ps[:, :].rearrange("p (h s) -> p h s", h=HEADS)
                                              ).then_inc(read_of(name), 1)
                    if n == 0:
                        dve.wait_ge(*t.full(f"gates {l}"))
                        ps = bank_of(f"gates {l}")
                        TTn(gts[:, :, :, :].rearrange("p (t d) k h -> p t (d k h)", d=2),
                            ps[:, 0:TT * 16].rearrange("p (t c) -> p t c", c=16),
                            cols(f"bgates_{l}").unsqueeze(1).broadcast_to([P, TT, 16]), ALU.add
                            ).then_inc(read_of(f"gates {l}"), 1)
                        dve.wait_ge(*t.read(f"gates {l}"))
                        STT(g_tmp[:, 0], forget, -1.0, forget, ALU.mult, ALU.min).then_inc(gate_arg, 1)
                        dve.wait_ge(*t.next(gate_log))
                        STT(lf[:, :, :], forget, 0.0, g_tmp[:, 0], ALU.min, ALU.subtract).then_inc(logf_ready, 1)
                    if n == 1:
                        dve.wait_ge(*t.full(f"cum {l}"))
                        ps = bank_of(f"cum {l}")
                        nc.vector.tensor_copy(cum[:, :, :, :].rearrange("p a b c -> p (a b c)"), ps[:, 0:64]
                                              ).then_inc(read_of(f"cum {l}"), 1)
                        dve.wait_ge(*t.read(f"cum {l}"))
                        TTn(gg[:, :, :], inputg, cum[:, 0], ALU.subtract).then_inc(gg_ready, 1)
                        dve.wait_ge(*t.next(gg_ready))
                    if 2 <= n < 6:
                        for a in (2 * n - 4, 2 * n - 3):
                            dve.wait_ge(*t.full(f"G {l} {a}"))
                            ps = bank_of(f"G {l} {a}")[:, :].rearrange("p (h s) -> p h s", h=HEADS)
                            nc.vector.tensor_reduce(gmax[:, a, :], ps, AX.X, ALU.max)
                            if a >= 2:
                                dve.wait_ge(*t.next(pmax_done))
                            TTn(t512[:, a % 2, :].rearrange("p (h s) -> p h s", h=HEADS), ps,
                                masks["A", a % 2].unsqueeze(1).broadcast_to([P, HEADS, P]), ALU.add
                                ).then_inc(read_of(f"G {l} {a}"), 1)
                            if a:
                                prefix_max(a - 1)
                    if n == 5:
                        prefix_max(2 * TT - 1)
                        dve.wait_ge(*t.next(pmax_done, 2))
                        for kk in range(4):
                            for d in range(2):
                                a = 2 * LAT_STEPS[d][kk] + d
                                if kk == 0:
                                    chain(nc.vector.memset(mprev[:, a, :], 0.0))
                                TTn(m_t[:, a, :], pmax[:, a, :], mprev[:, a, :], ALU.max)
                                chain(TTn(m_l[:, a, :], gmax[:, a, :], mprev[:, a, :], ALU.max))
                                if kk < 3:
                                    nxt = 2 * LAT_STEPS[d][kk + 1] + d
                                    chain(TTn(mprev[:, nxt, :], cum[:, 1, a, :], m_l[:, a, :], ALU.add))
                        TTn(e_in[:, 0], mprev[:, :, :], m_t[:, :, :], ALU.subtract)
                        TTn(e_in[:, 1], gg[:, :, :], m_l[:, :, :], ALU.subtract)
                        TTn(e_in[:, 2], mprev[:, :, :], m_l[:, :, :], ALU.subtract)
                        STT(e_in[:, 3], cum[:, 0], -1.0, m_t[:, :, :], ALU.mult, ALU.subtract).then_inc(exp_arg, 1)
                    if n == 6:
                        dve.wait_ge(*t.next(exp_arg))
                        dve.wait_ge(*t.next(exp_done))
                    if n == 7:
                        decay_args(0)
                        for tt in (0, 1):
                            dve.wait_ge(*t.full(f"v {l} {tt}"))
                            ps = bank_of(f"v {l} {tt}")
                            nc.vector.tensor_copy(v[:, tt, :, 0:HD], ps[:, :].rearrange("p (h d) -> p h d", h=HEADS)
                                                  ).then_inc(read_of(f"v {l} {tt}"), 1)

                for tt, d, kk in scan_steps():
                    a = 2 * tt + d
                    full = (tt, d, kk) in outputs[l]
                    if full:
                        i = outputs[l].index((tt, d, kk))
                        dve.wait_ge(*t.next(decay_ready))
                        name = f"S {l} {tt} {d}"
                        dve.wait_ge(*t.full(name))
                        ps = bank_of(name)
                        TTn(t512[:, i % 2, :], ps[:, :], t512[:, i % 2, :], ALU.mult).then_inc(read_of(name), 1)
                        if i + 1 < len(outputs[l]):
                            decay_args(i + 1)
                        if i == 1:
                            dve.wait_ge(*t.next(conv_hi))
                            TTn(u_lo[:, 0:CT, 0:W], conv[:, :, 0:W], u_hi[:, 0:CT, 0:W].bitcast(f32),
                                ALU.subtract).then_inc(conv_lo, 1)
                        if i == 2:
                            split_to(UNIT_AT[f"out{l}"] + 2)
                    if kk < 3:
                        for part in range(2):
                            name = f"upd {l} {tt} {d} {part}"
                            dve.wait_ge(*t.full(name))
                            ps = bank_of(name)
                            for j in range(2):
                                hd = 2 * part + j
                                src = ps[:, 256 * j:256 * j + HE]
                                if kk:
                                    last = STT(state[:, d, hd, :], state[:, d, hd, :], e_out[:, 2, a, hd:hd + 1], src,
                                               ALU.mult, ALU.add)
                                else:
                                    last = nc.vector.tensor_copy(state[:, d, hd, :], src)
                            last.then_inc(read_of(name), 1)
                            dve.wait_ge(*t.read(name))
                    if full:
                        for part in range(2):
                            name = f"num {l} {tt} {d} {part}"
                            dve.wait_ge(*t.full(name))
                            ps = bank_of(name)[:, :].rearrange("p (h s) -> p h s", h=2)[:, :, 0:HE]
                            dst = u_sum[:, 2 * part:2 * part + 2, :]
                            if kk:
                                dve.wait_ge(*t.read(f"int {l} {tt} {d} {part}"))
                                ins = TTn(dst, ps, inter[:, 2 * part:2 * part + 2, :], ALU.add)
                            else:
                                ins = nc.vector.tensor_copy(dst, ps)
                            ins.then_inc(read_of(name), 1)
                            dve.wait_ge(*t.read(name))
                        den = u_sum[:, :, HD]
                        chain(STT(small[:, 0, :], den, -1.0, den, ALU.mult, ALU.max))
                        chain(TTn(small[:, 1, :], small[:, 0, :], e_out[:, 3, a, :], ALU.max))
                        chain(nc.vector.reciprocal(small[:, 2, :], small[:, 1, :]))
                        later = 2 * LAT_STEPS[1 - d].index(tt) + 1 - d < 2 * kk + d
                        for hd in range(HEADS):
                            dst = hacc[:, tt, hd * P:hd * P + P]
                            if later:
                                last = STT(dst, u_sum[:, hd, 0:HD], small[:, 2, hd:hd + 1], dst, ALU.mult, ALU.add)
                            else:
                                last = nc.vector.tensor_scalar(dst, u_sum[:, hd, 0:HD], small[:, 2, hd:hd + 1], None,
                                                               ALU.mult)
                        last.then_inc(hacc_done, 1)
                        dve.wait_ge(*t.next(hacc_done))
                for tt in range(W // P):
                    if tt >= 2:
                        dve.wait_ge(*t.next(sumsq_ready))
                    chain(TTn(t512[:, tt % 2, :], hacc[:, tt, :], hacc[:, tt, :], ALU.mult))
                    nc.vector.tensor_reduce(msq[:, 0, tt, :], t512[:, tt % 2, :].rearrange("p (h s) -> p h s", h=HEADS),
                                            AX.X, ALU.add).then_inc(sumsq_ready, 1)
                dve.wait_ge(*t.next(sumsq_ready, 2))
                dve.wait_ge(*t.next(root_ready))
                chain(nc.vector.reciprocal(msq[:, 2, 0:W // P, :], msq[:, 1, 0:W // P, :]))
                for tt in range(W // P):
                    hv = hacc[:, tt, :].rearrange("p (h s) -> p h s", h=HEADS)
                    TTn(hv, hv, wide(msq[:, 2, tt, :], P, [P, HEADS, P]), ALU.mult).then_inc(normed, 1)
                for tt in range(TT if l == 0 else 2):
                    name = f"yT {l} {tt}"
                    dve.wait_ge(*t.full(name))
                    ps = bank_of(name)
                    dve.wait_ge(*t.next(y_hi_done))
                    for hd in range(HEADS):
                        c = slice(tt * P, tt * P + P)
                        last = STT(u_lo[:, CT + hd, c], ps[:, hd * P:hd * P + P], cols(f"mnorm_{l}")[:, hd:hd + 1],
                                   u_hi[:, CT + hd, c].bitcast(f32), ALU.mult, ALU.subtract)
                    last.then_inc(read_of(name), 1)
                u = UNIT_AT[f"out{l}"]
                for c in range(4):
                    split_to(u + c + 2)
                    for j in range(2):
                        residual(f"out {l} {c} {j}", 2 * c + j, W, l, 2)
                norm(f"2 {l}", W)
                if l == 0:
                    def group(g, base):
                        nf = GROUPS[g]
                        for c in range(nf + 4):
                            split(base + c)
                            if c and c % 2 == 0 and c <= nf:
                                dve.wait_ge(*t.next(hid_lo_ready, 2))
                            if c < nf and c % 2:
                                for j in range(2):
                                    dve.wait_ge(*t.full(f"ffn {g} {c} {j}"))
                                    ps = bank_of(f"ffn {g} {c} {j}")
                                    dve.wait_ge(*t.read(f"ffn {g} {c - 1} {j}"))
                                    TTn(hid0[:, j, :], ps[:, :], sil0[:, j, :], ALU.mult
                                        ).then_inc(read_of(f"ffn {g} {c} {j}"), 1)
                                for j in range(2):
                                    dve.wait_ge(*t.next(hid_hi_ready))
                                    TTn(hid_lo[:, c - 1 + j, :], hid0[:, j, :], hid_hi[:, c - 1 + j, :].bitcast(f32),
                                        ALU.subtract).then_inc(hid_lo_ready, 1)
                            if c >= nf:
                                for j in range(2):
                                    residual(f"ffn {g} {c} {j}", 2 * (c - nf) + j, NT, 0, 5)
                    with t.loop(2, unit_loops("ffn", {**fill_loops("ffn"), hid_hi_ready: 8, hid_lo_ready: 8}), 2):
                        group(0, ahead[0])
                    ahead[0] += 24
                    group(2, ahead[0])
                    ahead[0] += 10

            dve.wait_ge(*t.full("logitsT"))
            nc.vector.tensor_copy(lgT[:, :], bank_of("logitsT")[0:NE, 0:SEQ]).then_inc(read_of("logitsT"), 1)
            dve.wait_ge(*t.full("logits"))
            ps = bank_of("logits")
            nc.vector.tensor_copy(lg[:, :, :].rearrange("p t e -> p (t e)"), ps[:, 0:2 * NE]
                                  ).then_inc(read_of("logits"), 1)
            dve.wait_ge(*t.read("logits"))
            shape = [P, 2, NE]
            rank = cols("rank").unsqueeze(1).broadcast_to(shape)
            for i, one in enumerate((one1, one2)):
                chain(nc.vector.tensor_reduce(s2[:, i, :], lg[:, :, :], AX.X, ALU.max))
                chain(TTn(sc8[:, 0], lg[:, :, :], wide(s2[:, i, :], NE, shape), ALU.is_equal))
                chain(TTn(sc8[:, 1], sc8[:, 0], rank, ALU.mult))
                chain(nc.vector.tensor_reduce(s2[:, 7, :], sc8[:, 1], AX.X, ALU.max))
                chain(TTn(one[:, :, :], sc8[:, 1], wide(s2[:, 7, :], NE, shape), ALU.is_equal))
                if i == 0:
                    chain(STT(lg[:, :, :], one[:, :, :], NEG, lg[:, :, :], ALU.mult, ALU.add))
            TTn(sel[:, :, :], one1[:, :, :], one2[:, :, :], ALU.add).then_inc(sel_ready, 1)
            TTn(s2[:, 2, :], s2[:, 1, :], s2[:, 0, :], ALU.subtract).then_inc(route_arg, 1)
            dve.wait_ge(*t.next(route_exp))
            chain(nc.vector.tensor_scalar(s2[:, 4, :], s2[:, 3, :], 1.0, None, ALU.add))
            chain(nc.vector.reciprocal(s2[:, 5, :], s2[:, 4, :]))
            chain(TTn(s2[:, 6, :], s2[:, 5, :], s2[:, 3, :], ALU.mult))
            TTn(sc8[:, 2], one1[:, :, :], wide(s2[:, 5, :], NE, shape), ALU.mult)
            chain(TTn(sc8[:, 3], one2[:, :, :], wide(s2[:, 6, :], NE, shape), ALU.mult))
            chain(TTn(gate[:, :, :], sc8[:, 2], sc8[:, 3], ALU.add))
            chain(nc.vector.tensor_copy(gate_parts[:, :, :, 0], gate[:, :, :]))
            TTn(gate_parts[:, :, :, 1], gate[:, :, :], gate_parts[:, :, :, 0].bitcast(f32), ALU.subtract
                ).then_inc(gates_split, 1)
            dve.wait_ge(*t.full("count"))
            ps = bank_of("count")
            chain(nc.vector.tensor_reduce(s2[:, 7, 0:1], ps[:, 16:24], AX.X, ALU.max))
            nc.vector.tensor_scalar(npass[0:1, 0:1], s2[0:1, 7, 0:1], float(P), 1.0, ALU.is_gt, ALU.add
                                    ).then_inc(npass_ready, 1)
            dve.wait_ge(*t.next(npass_ready))
            dve.wait_ge(*t.next(sel_ready))
            TTn(sc8[:, 4], ps[:, 0:16].rearrange("p (t e) -> p t e", t=2), sel[:, :, :], ALU.mult
                ).then_inc(read_of("count"), 1)
            dve.wait_ge(*t.read("count"))
            chain(nc.vector.tensor_scalar(slot_of[:, :, :], sc8[:, 4], -1.0, None, ALU.add))
            for i in range(1, 8, 2):
                dve.wait_ge(*t.full(f"utok {i}"))
                ps = bank_of(f"utok {i}")
                half, tt = i // 4, i // 2 % 2
                nc.vector.tensor_copy(utok_lo[:, tt, 512 * half:512 * half + 512], ps[:, :]
                                      ).then_inc(read_of(f"utok {i}"), 1)
            passes = dve.value_load(npass[0:1, 0:1], min_val=1, max_val=2)

            def gathered(name, i):
                dve.wait_ge(*t.full(name))
                ps = bank_of(name)
                nc.vector.tensor_copy(xe_lo[:, 2 * i - 2:2 * i + 2, :], ps[:, :].rearrange("p (k s) -> p k s", k=4)
                                      ).then_inc(read_of(name), 1)

            def give_back(which, fills):
                for i in fills:
                    dve.wait_ge(*t.full(f"{which} {i}"))
                    ps = bank_of(f"{which} {i}")
                    for j in range(2):
                        kt = 2 * i + j
                        last = STT(h[:, kt, 0:SEQ], ps[:, 256 * j:256 * j + 256], mod_col(1, 5, kt, 0),
                                   h[:, kt, 0:SEQ], ALU.mult, ALU.add)
                    last.then_inc(read_of(f"{which} {i}"), 1)
                    dve.wait_ge(*t.read(f"{which} {i}"))

            per_expert = {dve_chain: 1, y_hi_ready: 1, hT_hi_ready: len(CHUNKS)}
            per_pass = {y_hi_ready: NE, hT_hi_ready: NE * len(CHUNKS), dve_chain: 1 + NE, pick_ready: 2}
            with t.loop(passes, {**unit_loops("pass", fill_loops("pass")), **per_pass}, 1):
                TTn(pick[:, :, 0, :], cols("iota").unsqueeze(1).broadcast_to([P, 2, P]),
                    wide(slot_of[:, :, 0], P, [P, 2, P]), ALU.is_equal).then_inc(pick_ready, 1)
                for tt in range(2):
                    last = TTn(pick[:, tt, 1:NE, :], cols("iota").unsqueeze(1).broadcast_to([P, NE - 1, P]),
                               wide(slot_of[:, tt, 1:NE], P, [P, NE - 1, P]), ALU.is_equal)
                last.then_inc(pick_ready, 1)
                for i in (1, 3):
                    gathered(f"gather {i}", i)
                dve.wait_ge(*t.next(pick_ready, 2))
                chain(nc.vector.tensor_scalar(slot_of[:, :, :], slot_of[:, :, :], -float(P), None, ALU.add))
                dve.wait_ge(*t.full("gslot"))
                ps = bank_of("gslot")
                nc.vector.tensor_reduce(gslot[:, :], ps[:, 0:2 * NE].rearrange("p (e k) -> p e k", k=2), AX.X, ALU.add
                                        ).then_inc(read_of("gslot"), 1)
                with t.loop(NE, {**unit_loops("expert", fill_loops("expert")), **per_expert}, NE) as e:
                    for j, (m, c, part) in enumerate(EXPERT_UNITS):
                        split(ahead[0] + j)
                        if j == 0:
                            dve.wait_ge(*t.read("gslot"))
                            dve.wait_ge(*t.free("back 3"))
                            chain(nc.vector.tensor_copy(gcol[:, :], gslot[:, ds(e, 1)]))
                        last_part = j + 1 == UPE or EXPERT_UNITS[j + 1][:2] != (m, c)
                        if m == "w3" and last_part:
                            dve.wait_ge(*t.full(f"w3 {c}"))
                            ps, w = bank_of(f"w3 {c}"), CHUNKS[c]
                            dve.wait_ge(*t.read(f"w1 {c}"))
                            TTn(hid[:, c % 2, 0:w], ps[:, 0:w], sil[:, c % 2, 0:w], ALU.mult
                                ).then_inc(read_of(f"w3 {c}"), 1)
                        if j in (BACK_AT, BACK_AT + 1):
                            give_back("back", (0, 1) if j == BACK_AT else (2, 3))
                        if j in T_AT:
                            c_t = T_AT[j]
                            n_t = CHUNKS[c_t] // P
                            dve.wait_ge(*t.full(f"T {c_t}"))
                            ps = bank_of(f"T {c_t}")
                            dve.wait_ge(*t.next(hT_hi_ready))
                            TTn(hT_lo[:, c_t % 2, 0:n_t, :], ps[:, 0:n_t * P].rearrange("p (k s) -> p k s", k=n_t),
                                hT_hi[:, c_t % 2, 0:n_t, :].bitcast(f32), ALU.subtract
                                ).then_inc(read_of(f"T {c_t}"), 1)
                        if j == NEXT_AT:
                            for i in (1, 3):
                                gathered(f"next {i}", i)
                        if j == UPE - 1:
                            dve.wait_ge(*t.next(y_hi_ready))
                            for half in range(2):
                                c_ = slice(512 * half, 512 * half + 512)
                                dve.wait_ge(*t.full(f"y {half}"))
                                ps = bank_of(f"y {half}")
                                STT(y_lo[:, c_], ps[:, :], gcol[:, :], y_hi[:, c_].bitcast(f32),
                                    ALU.mult, ALU.subtract).then_inc(read_of(f"y {half}"), 1)
                give_back("final back", range(4))
            t.loops.append((passes - 1, {**fill_loops("pass"), dve_chain: per_pass[dve_chain]}))
            norm("f", SEQ, final=True)

        @block.tensor
        def _(pe):
            t = Counts(pe)
            mm = nc.tensor.matmul

            def mm3(dst, a_hi, a_lo, b_hi, b_lo, start, stop):
                mm(dst, a_hi, b_hi, start=start, stop=False)
                mm(dst, a_hi, b_lo, start=False, stop=False)
                return mm(dst, a_lo, b_hi, start=False, stop=stop)

            def arrived(n, half=1):
                pe.wait_ge(lo_ready, t.at(lo_ready, 2 * n + half + 1))
                return n % SLOTS

            pe.wait_ge(*t.next(small_lo, DEPTH + 2))
            comb = cols("comb")[0:4, :]
            def norm_sum(tag, kt, width):
                if kt == 0:
                    pe.wait_ge(*t.free(f"norm {tag}"))
                pe.wait_ge(*t.next(square_ready))
                ins = mm(bank_of(f"norm {tag}")[:, 0:width], ones, square[:, kt % 2, 0:width], start=kt == 0,
                         stop=kt == KT - 1)
                if kt < KT - 1:
                    ins.then_inc(square_used, 1)
                else:
                    ins.then_inc(full_of(f"norm {tag}"), 1)

            def modulations(turn, first, kind, beside=None):
                for c in range(3):
                    name = f"{kind} {c}"
                    ps = bank_of(name)
                    for part in range(2):
                        for kk in range(4):
                            if kk % 2 == 0:
                                sl = arrived(first + 2 * c + part, kk // 2)
                            kt = 4 * part + kk
                            for w in (whi, wlo):
                                last = mm(ps[0:4, :], cond4[:, kt, :], w[sl][:, kk * 512:kk * 512 + 512],
                                          start=kt == 0 and w is whi, stop=kt == KT - 1 and w is wlo)
                        last.then_inc(unit_used, 1)
                        if beside:
                            beside(2 * c + part)
                    pe.wait_ge(*t.read(name))
                    for j in range(4):
                        last = mm(bank_of("mod")[:, ds(turn * 24 + (8 * c + 2 * j), 2)], ada_row[:, c, j * P:j * P + P],
                                  comb, start=True, stop=True)
                last.then_inc(mod_turned, 1)

            with t.loop(ADA_TURNS, unit_loops("ada", fill_loops("ada")), ADA_TURNS) as i:
                modulations(i, 0, "ada")
            modulations(ADA_TURNS, 6 * ADA_TURNS, "ada last", lambda kt: norm_sum("1 0", kt, NT))

            def columns(units, width, kts, names, hi, lo, before=None, last_kt=KT - 1, js=(0, 1)):
                for i, u in enumerate(units):
                    sl = arrived(u)
                    for j in js:
                        if 0 in kts:
                            pe.wait_ge(*t.free(names[i][j]))
                for kt in kts:
                    if before:
                        before(kt)
                    for i, u in enumerate(units):
                        sl = u % SLOTS
                        for j in js:
                            w = slice(kt * 256 + j * P, kt * 256 + j * P + P)
                            last = mm3(bank_of(names[i][j])[:, 0:width], whi[sl][:, w], wlo[sl][:, w],
                                       hi[:, kt, 0:width], lo[:, kt, 0:width], kt == 0, kt == last_kt)
                        if kt == last_kt:
                            last.then_inc(unit_used, 1)

            for l in range(DEPTH):
                W = NT if l == 0 else SEQ
                if l == 0:
                    for kt in (6, 7):
                        norm_sum("1 0", kt, NT)
                done = [0]

                def u_part(kt):
                    if done[0] <= kt:
                        pe.wait_ge(*t.next(u_lo_ready))
                        done[0] += 1

                u = UNIT_AT[f"conv{l}"]
                names = [[f"conv {l} {c} {j}" for j in range(2)] for c in range(6)]
                columns([u, u + 1], W, range(KT), names[0:2], u_hi, u_lo, u_part)
                for c in range(2, 6):
                    columns([u + c], W, range(KT), names[c:c + 1], u_hi, u_lo)

                def spread_m(i):
                    tt, d, _ = outputs[l][i]
                    name = f"M {l} {tt} {d}"
                    pe.wait_ge(*t.free(name))
                    ps = bank_of(name)
                    pe.wait_ge(*t.next(diag_ready))
                    mm(ps[:, :], ones, diag[:, i % 2, :], start=True, stop=True).then_inc(full_of(name), 1)

                def scores(i):
                    tt, d, _ = outputs[l][i]
                    c = slice(tt * P, tt * P + P)
                    name = f"S {l} {tt} {d}"
                    pe.wait_ge(*t.free(name))
                    ps = bank_of(name)
                    for hd in range(HEADS):
                        last = mm(ps[:, hd * P:hd * P + P], kT[:, hd, c], qT[:, hd, c], start=True, stop=True)
                    last.then_inc(full_of(name), 1)

                pe.wait_ge(*t.free(f"gatesT {l}"))
                ps = bank_of(f"gatesT {l}")
                for kt in range(KT):
                    last = mm3(ps[0:16, :], wg_hi[:, l, kt, :], wg_lo[:, l, kt, :], u_hi[:, kt, :], u_lo[:, kt, :],
                               kt == 0, kt == KT - 1)
                last.then_inc(full_of(f"gatesT {l}"), 1)
                u = UNIT_AT[f"qkov{l}"]
                for n in range(8):
                    name, part = "qkov"[n // 2], n % 2
                    sl = arrived(u + n)
                    for tt in range(TT if l == 0 or name in "kv" else 2):
                        if part == 0:
                            pe.wait_ge(*t.free(f"{name} {l} {tt}"))
                        ps = bank_of(f"{name} {l} {tt}")
                        for kk in range(4):
                            kt = 4 * part + kk
                            w = slice(kk * 512, kk * 512 + 512)
                            last = mm3(ps[:, :], u_hi[:, kt, tt * P:tt * P + P], u_lo[:, kt, tt * P:tt * P + P],
                                       whi[sl][:, w], wlo[sl][:, w], kt == 0, kt == KT - 1)
                        if tt == 1 and turned_in(l, n):
                            t_ = n - 4
                            pe.wait_ge(*t.read(f"q {l} {t_}"))
                            pe.wait_ge(*t.read(f"k {l} {t_}"))
                            for turned, src in zip(turned_in(l, n), (q, k)):
                                pe.wait_ge(*t.free(turned))
                                ps = bank_of(turned)
                                for hd in range(HEADS):
                                    turn = nc.tensor.transpose(ps[:, hd * P:hd * P + P], src[:, t_, hd * P:hd * P + P],
                                                               ident)
                                turn.then_inc(full_of(turned), 1)
                    last.then_inc(unit_used, 1)
                    if n == 0:
                        pe.wait_ge(*t.read(f"gatesT {l}"))
                        pe.wait_ge(*t.free(f"gates {l}"))
                        ps = bank_of(f"gates {l}")
                        for tt in range(TT):
                            last = nc.tensor.transpose(ps[:, tt * 16:tt * 16 + 16], gatesT[:, tt * P:tt * P + P],
                                                       ident[0:16, 0:16])
                        last.then_inc(full_of(f"gates {l}"), 1)
                    if n == 1:
                        pe.wait_ge(*t.free(f"cum {l}"))
                        ps = bank_of(f"cum {l}")
                        pe.wait_ge(*t.next(logf_ready))
                        for d in range(2):
                            dst = ps[:, 0:32].rearrange("p (t d h) -> p t d h", d=2, h=HEADS)[:, :, d, :]
                            mm(dst, tri[d], lf[:, :, :].rearrange("p (t d) h -> p t d h", d=2)[:, :, d, :],
                               start=True, stop=True)
                        mm(ps[:, 32:64], ones, lf[:, :, :].rearrange("p a h -> p (a h)"), start=True, stop=True
                           ).then_inc(full_of(f"cum {l}"), 1)
                    if 2 <= n < 6:
                        for a in (2 * n - 4, 2 * n - 3):
                            pe.wait_ge(*t.free(f"G {l} {a}"))
                            ps = bank_of(f"G {l} {a}")
                            pe.wait_ge(*t.next(diag_ready))
                            mm(ps[:, :], ones, diag[:, a % 2, :], start=True, stop=True
                               ).then_inc(full_of(f"G {l} {a}"), 1)
                    if n == 6:
                        pe.wait_ge(*t.read(f"qT {l} {outputs[l][0][0]}"))
                        pe.wait_ge(*t.read(f"kT {l} {outputs[l][0][0]}"))
                        spread_m(0)
                        scores(0)
                for tt in range(TT if l == 0 else 2):
                    pe.wait_ge(*t.read(f"qT {l} {tt}"))
                    pe.wait_ge(*t.read(f"kT {l} {tt}"))
                for tt in range(TT):
                    pe.wait_ge(*t.read(f"v {l} {tt}"))
                pe.wait_ge(v_ones, t.at(v_ones, l + 1))
                previous = {}

                for tt, d, kk in scan_steps():
                    full = (tt, d, kk) in outputs[l]
                    i = outputs[l].index((tt, d, kk)) if full else None
                    c = slice(tt * P, tt * P + P)
                    if full:
                        if kk:
                            for part in range(2):
                                pe.wait_ge(*t.read(previous[d][part]))
                                name = f"int {l} {tt} {d} {part}"
                                pe.wait_ge(*t.free(name))
                                ps = bank_of(name)
                                for j in range(2):
                                    last = mm(ps[:, 256 * j:256 * j + HE], qT[:, 2 * part + j, c],
                                              state[:, d, 2 * part + j, :], start=True, stop=True)
                                last.then_inc(full_of(name), 1)
                    if kk < 3:
                        pe.wait_ge(*t.next(kw_ready))
                        for part in range(2):
                            name = f"upd {l} {tt} {d} {part}"
                            pe.wait_ge(*t.free(name))
                            ps = bank_of(name)
                            for j in range(2):
                                hd = 2 * part + j
                                last = mm(ps[:, 256 * j:256 * j + HE], kw[:, hd * P:hd * P + P], v[:, tt, hd, :],
                                          start=True, stop=True)
                            last.then_inc(full_of(name), 1)
                        previous[d] = [f"upd {l} {tt} {d} {part}" for part in range(2)]
                    if full:
                        more = i + 1 < len(outputs[l])
                        if more:
                            spread_m(i + 1)
                        pe.wait_ge(*t.read(f"S {l} {tt} {d}"))
                        for part in range(2):
                            name = f"num {l} {tt} {d} {part}"
                            pe.wait_ge(*t.free(name))
                            ps = bank_of(name)
                            for j in range(2):
                                hd = 2 * part + j
                                last = mm(ps[:, 256 * j:256 * j + HE], t512[:, i % 2, hd * P:hd * P + P],
                                          v[:, tt, hd, :], start=True, stop=True)
                            last.then_inc(full_of(name), 1)
                        if more:
                            scores(i + 1)
                pe.wait_ge(*t.next(conv_lo))
                u = UNIT_AT[f"out{l}"]
                names = [[f"out {l} {c} {j}" for j in range(2)] for c in range(4)]

                def turn_merged(tiles):
                    for tt in tiles:
                        name = f"yT {l} {tt}"
                        pe.wait_ge(*t.free(name))
                        ps = bank_of(name)
                        pe.wait_ge(*t.next(merged))
                        for hd in range(HEADS):
                            last = nc.tensor.transpose(ps[:, hd * P:hd * P + P], hacc[:, tt, hd * P:hd * P + P], ident)
                        last.then_inc(full_of(name), 1)

                for c in range(2):
                    columns([u + c], W, range(CT), names[c:c + 1], u_hi, u_lo)
                if l == 0:
                    turn_merged((0, 1))
                columns([u + 2], W, range(CT), names[2:3], u_hi, u_lo, js=(0,))
                turn_merged((2, 3) if l == 0 else (0, 1))
                columns([u + 2], W, range(CT), names[2:3], u_hi, u_lo, js=(1,))
                for tt in range(TT if l == 0 else 2):
                    pe.wait_ge(*t.read(f"yT {l} {tt}"))
                for c in range(4):
                    columns([u + c], W, range(CT if c < 3 else 0, KT), names[c:c + 1], u_hi, u_lo)
                    if c:
                        for kt in (2 * c - 2, 2 * c - 1):
                            norm_sum(f"2 {l}", kt, W)
                for kt in (6, 7):
                    norm_sum(f"2 {l}", kt, W)
                u_base = t.n[u_lo_ready]
                t.next(u_lo_ready, KT)
                if l == 0:
                    def u_ready(kt):
                        pe.wait_ge(u_lo_ready, u_base + kt + 1)

                    def hidden(kt):
                        pe.wait_ge(*t.next(hid_lo_ready))

                    def group(g):
                        u, nf = UNIT_AT[f"ffn{g}"], GROUPS[g]
                        names = [[f"ffn {g} {c} {j}" for j in range(2)] for c in range(nf + 4)]
                        columns([u, u + 1], NT, range(KT), names[0:2], u_hi, u_lo, u_ready if g == 0 else None)
                        for c in range(2, nf + 4):
                            if c < nf:
                                columns([u + c], NT, range(KT), names[c:c + 1], u_hi, u_lo)
                            else:
                                columns([u + c], NT, range(nf), names[c:c + 1], hid_hi, hid_lo,
                                        hidden if c == nf else None, nf - 1)
                            if g == 2 and c > nf:
                                for j in range(2):
                                    norm_sum("1 1", 2 * (c - 1 - nf) + j, NT)
                    with t.loop(2, unit_loops("ffn", {**fill_loops("ffn"), hid_lo_ready: 8}), 2):
                        group(0)
                    group(2)
                    for kt in (6, 7):
                        norm_sum("1 1", kt, NT)

            def token_major(i, kt):
                half, tt, src = i // 4, i // 2 % 2, (u_hi, u_lo)[i % 2]
                j = kt - 4 * half
                if j == 0:
                    pe.wait_ge(*t.free(f"utok {i}"))
                ps = bank_of(f"utok {i}")
                last = nc.tensor.transpose(ps[:, j * P:j * P + P], src[:, kt, tt * P:tt * P + P].bitcast(f32), ident)
                if j == 3:
                    last.then_inc(full_of(f"utok {i}"), 1)

            pe.wait_ge(*t.free("logitsT"))
            ps = bank_of("logitsT")
            for kt in range(KT):
                pe.wait_ge(u_lo_ready, u_base + kt + 1)
                last = mm3(ps[0:NE, 0:SEQ], ro_hi[:, kt, :], ro_lo[:, kt, :], u_hi[:, kt, 0:SEQ], u_lo[:, kt, 0:SEQ],
                           kt == 0, kt == KT - 1)
                if kt == KT - 1:
                    last.then_inc(full_of("logitsT"), 1)
                for i in range(4):
                    if 4 * (kt // 4) + i < 7:
                        token_major(4 * (kt // 4) + i, kt)
            pe.wait_ge(*t.read("logitsT"))
            ps = bank_of("logits")
            for tt in range(2):
                last = nc.tensor.transpose(ps[:, tt * NE:tt * NE + NE], lgT[:, tt * P:tt * P + P], ident[0:NE, 0:NE])
            last.then_inc(full_of("logits"), 1)
            for kt in range(4, KT):
                token_major(7, kt)
            pe.wait_ge(*t.free("count"))
            ps = bank_of("count")
            pe.wait_ge(*t.next(sel_ready))
            mm(ps[:, 0:8], tri[0], sel[:, 0, :], start=True, stop=True)
            mm(ps[:, 8:16], ones, sel[:, 0, :], start=True, stop=False)
            mm(ps[:, 8:16], tri[0], sel[:, 1, :], start=False, stop=True)
            mm(ps[:, 16:24], ones, sel[:, 0, :], start=True, stop=False)
            mm(ps[:, 16:24], ones, sel[:, 1, :], start=False, stop=True).then_inc(full_of("count"), 1)
            pe.wait_ge(npass_ready, 1)
            passes = pe.value_load(npass[0:1, 0:1], min_val=1, max_val=2)
            for i in range(8):
                pe.wait_ge(*t.read(f"utok {i}"))
            pe.wait_ge(zeros_ready, 1)
            pe.wait_ge(gates_split, 1)

            def gather(names, e):
                for i in range(4):
                    src = (utok_hi, utok_lo)[i % 2]
                    pe.wait_ge(*t.free(names[i]))
                    ps = bank_of(names[i])
                    for j in range(4):
                        kt = 4 * (i // 2) + j
                        for tt in range(2):
                            last = mm(ps[:, j * P:j * P + P], src[:, tt, kt * P:kt * P + P],
                                      pick[:, tt, ds(e, 1), :].rearrange("p a s -> p (a s)") if not isinstance(e, int)
                                      else pick[:, tt, e, :], start=tt == 0, stop=tt == 1)
                    last.then_inc(full_of(names[i]), 1)

            def give_back(which, e):
                for half in range(2):
                    pe.wait_ge(*(t.free(f"back {2 + half}") if which == "back"
                                 else t.read(f"y {half}", later_turns=NE - 1)))
                if which == "back":
                    for i in range(4):
                        pe.wait_ge(*t.read(f"PT {i}"))
                for i in range(4):
                    pe.wait_ge(*t.free(f"{which} {i}"))
                    ps = bank_of(f"{which} {i}")
                    for j in range(2):
                        kt = 2 * i + j
                        for part, y in enumerate((y_hi, y_lo)):
                            last = mm(ps[:, 256 * j:256 * j + 256], y[:, kt * P:kt * P + P],
                                      pickT[:, ds(e, 1), :].rearrange("p a n -> p (a n)"),
                                      start=part == 0, stop=part == 1)
                    last.then_inc(full_of(f"{which} {i}"), 1)

            u = UNIT_AT["moe"]
            with t.loop(passes, {**unit_loops("pass", fill_loops("pass")), pick_ready: 2}, 1):
                pe.wait_ge(*t.next(pick_ready))
                gather([f"gather {i}" for i in range(4)], 0)
                pe.wait_ge(*t.next(pick_ready))
                pe.wait_ge(*t.free("gslot"))
                ps = bank_of("gslot")
                for ee in range(NE):
                    for tt in range(2):
                        last = mm(ps[:, 2 * ee:2 * ee + 2], pick[:, tt, ee, :], gate_parts[:, tt, ee, :],
                                  start=tt == 0, stop=tt == 1)
                last.then_inc(full_of("gslot"), 1)
                for i in range(4):
                    pe.wait_ge(*t.free(f"PT {i}"))
                    pe.wait_ge(*t.read(f"gather {i}"))
                    ps = bank_of(f"PT {i}")
                    for ee in range(2):
                        for tt in range(2):
                            c = ee * SEQ + tt * P
                            last = nc.tensor.transpose(ps[:, c:c + P], pick[:, tt, 2 * i + ee, :].bitcast(f32), ident)
                    last.then_inc(full_of(f"PT {i}"), 1)
                with t.loop(NE, unit_loops("expert", fill_loops("expert")), NE) as e:
                    for j, (m, c, part) in enumerate(EXPERT_UNITS):
                        last_part = j + 1 == UPE or EXPERT_UNITS[j + 1][:2] != (m, c)
                        if m != "w2":
                            w = CHUNKS[c]
                            n_k = UNIT // w
                            b = 2 * (c % 2) + (m == "w3")
                            if part == 0:
                                pe.wait_ge(*t.free(f"{m} {c}"))
                            for kk in range(n_k):
                                if kk % (n_k // 2) == 0:
                                    sl = arrived(u + j, kk // (n_k // 2))
                                kt = part * 4 + kk
                                r = slice(kk * w, kk * w + w)
                                last = mm3(bank[b][:, 0:w], xe_hi[:, kt, :], xe_lo[:, kt, :], whi[sl][:, r],
                                           wlo[sl][:, r], kt == 0, kt == KT - 1)
                        else:
                            if j == 8:
                                pe.wait_ge(*t.free("y 0"))
                                pe.wait_ge(*t.free("y 1"))
                            if part == 0:
                                pe.wait_ge(*t.read(f"T {c}"))
                            if j == UPE - 1:
                                for i in (2, 3, 1):
                                    pe.wait_ge(*t.read(f"next {i}"))
                            for kk in range(2):
                                sl = arrived(u + j, kk)
                                ft = 2 * part + kk
                                for half in range(2):
                                    r = slice(kk * 1024 + half * 512, kk * 1024 + half * 512 + 512)
                                    last = mm3(bank[6 + half][:, :], hT_hi[:, c % 2, ft, :], hT_lo[:, c % 2, ft, :],
                                               whi[sl][:, r], wlo[sl][:, r], c == 0 and ft == 0,
                                               j == UPE - 1 and kk == 1)
                        last.then_inc(unit_used, 1)
                        if j == BACK_AT:
                            give_back("back", e)
                        if j in T_AT:
                            c_t = T_AT[j]
                            pe.wait_ge(*t.read(f"w3 {c_t}"))
                            pe.wait_ge(*t.free(f"T {c_t}"))
                            ps = bank_of(f"T {c_t}")
                            for ft in range(CHUNKS[c_t] // P):
                                last = nc.tensor.transpose(ps[:, ft * P:ft * P + P],
                                                           hid[:, c_t % 2, ft * P:ft * P + P], ident)
                            last.then_inc(full_of(f"T {c_t}"), 1)
                        if j == NEXT_AT:
                            gather([f"next {i}" for i in range(4)], e + 1)
                give_back("final back", NE)
            t.loops.append((passes - 1, fill_loops("pass")))
            for kt in range(KT):
                norm_sum("f", kt, SEQ)

        @block.gpsimd
        def _(pool):
            t = Counts(pool)
            TTp = nc.gpsimd.tensor_tensor

            def wide(x):
                return x.unsqueeze(2).broadcast_to([P, HEADS, P])

            def diagonal(src, a, slot):
                TTp(diag[:, slot, :].rearrange("p (h s) -> p h s", h=HEADS),
                    ident.unsqueeze(1).broadcast_to([P, HEADS, P]), wide(src[:, a, :]), ALU.mult).then_inc(diag_ready, 1)

            pool.wait_ge(params_loaded, 16)
            for l in range(DEPTH):
                W = NT if l == 0 else SEQ
                pool.wait_ge(*t.next(gg_ready))
                for a in range(2 * TT):
                    if a >= 2:
                        pool.wait_ge(*t.full(f"G {l} {a - 2}"))
                    diagonal(gg, a, a % 2)
                for tt in range(TT):
                    pool.wait_ge(*t.read(f"k {l} {tt}"))
                pool.wait_ge(*t.next(exp_done))
                pool.wait_ge(*t.full(f"G {l} {2 * TT - 2}"))

                def diagonal_m(i):
                    tt, d, _ = outputs[l][i]
                    diagonal(m_t, 2 * tt + d, i % 2)

                diagonal_m(0)
                updates = [s for s in scan_steps() if s[2] < 3]
                for n, (tt, d, kk) in enumerate(scan_steps()):
                    full = (tt, d, kk) in outputs[l]
                    if kk < 3:
                        if n:
                            before = updates[n - 1]
                            pool.wait_ge(*t.full(f"upd {l} {before[0]} {before[1]} 1"))
                        TTp(kw[:, :].rearrange("p (h s) -> p h s", h=HEADS),
                            k[:, tt, :].rearrange("p (h s) -> p h s", h=HEADS),
                            wide(e_out[:, 1, 2 * tt + d, :]), ALU.mult).then_inc(kw_ready, 1)
                    if full:
                        i = outputs[l].index((tt, d, kk))
                        if i + 1 < len(outputs[l]):
                            if i:
                                b, bd, _ = outputs[l][i - 1]
                                pool.wait_ge(*t.full(f"M {l} {b} {bd}"))
                            else:
                                pool.wait_ge(*t.full(f"G {l} {2 * TT - 1}"))
                            diagonal_m(i + 1)
                for tt in range(W // P):
                    pool.wait_ge(*t.read(f"o {l} {tt}"))
                for tt in range(W // P):
                    pool.wait_ge(*t.next(normed))
                    TTp(hacc[:, tt, :], hacc[:, tt, :], o[:, tt, :], ALU.mult).then_inc(merged, 1)
            pool.wait_ge(u_lo_ready, DEPTH * 2 * KT)
            nc.gpsimd.memset(pick[:, :, NE, :].bitcast(f32), 0.0)
            nc.gpsimd.memset(pickT[:, 0, :].bitcast(f32), 0.0)
            nc.gpsimd.memset(y_hi[:, :].bitcast(f32), 0.0)
            nc.gpsimd.memset(y_lo[:, :].bitcast(f32), 0.0).then_inc(zeros_ready, 1)


def kernel(**inputs):
    import numpy as _np
    import concourse.bacc as _bacc
    from concourse import mybir as _mybir
    from concourse.bass_utils import run_bass_kernel_spmd as _run

    a = {name: _np.asarray(x) for name, x in inputs.items()}
    f32 = _np.float32

    stream = _np.zeros((N_UNITS + 2, P, UNIT), f32)
    at = [0]

    def put(block):
        rows, n = block.shape
        w = rows // P * n
        stream[at[0], :, 0:w].reshape(P, rows // P, n)[:] = block.reshape(rows // P, P, n).transpose(1, 0, 2)
        at[0] += 1

    for l in range(DEPTH):
        for c in range(0, 6 * D, 512):
            for half in range(2):
                put(a["w_ada"][l][512 * half:512 * half + 512, c:c + 512])
    for l in range(DEPTH):
        w = a["w_in"][l]
        assert at[0] == UNIT_AT[f"conv{l}"]
        for c in range(CT):
            s = slice(c * P, c * P + P)
            put(_np.concatenate([w[:, CONV:2 * CONV][:, s], w[:, 2 * CONV:3 * CONV][:, s]], axis=1))
        for c in range(2):
            put(w[:, 256 * c:256 * c + 256])
        q0 = 3 * CONV
        for c0 in (q0, q0 + 512, q0 + 1536 + 16, q0 + 1024):
            for half in range(2):
                put(w[512 * half:512 * half + 512, c0:c0 + 512])
        for c in range(4):
            put(a["w_out"][l][:, 256 * c:256 * c + 256])
        if l == 0:
            f0 = 0
            for nf in GROUPS:
                for c in range(f0, f0 + nf * P, 256):
                    put(a["ffn_w1"][0][:, c:c + 256])
                    put(a["ffn_w3"][0][:, c:c + 256])
                for c in range(4):
                    put(a["ffn_w2"][0][f0:f0 + nf * P, 256 * c:256 * c + 256])
                f0 += nf * P
    for e in range(NE):
        for m, c, part in EXPERT_UNITS:
            f0, w = 512 * c, CHUNKS[c]
            if m == "w2":
                put(a["moe_w2"][0, e][f0 + 256 * part:f0 + 256 * part + 256])
            elif w == 512:
                put(a["moe_" + m][0, e][512 * part:512 * part + 512, f0:f0 + w])
            else:
                put(a["moe_" + m][0, e][:, f0:f0 + w])
    assert at[0] == N_UNITS
    stream[N_UNITS:] = stream[UNIT_AT["moe"]:UNIT_AT["moe"] + 2]

    tokens = _np.concatenate([a["x"][0], a["ctx"][0]]).T.reshape(KT, P, NT).transpose(1, 0, 2)
    params = _np.zeros((P, NPAR), f32)

    def param(name, block):
        lo, hi = COL[name]
        params[:, lo:hi] = _np.broadcast_to(block, (P, hi - lo))

    def by_channel(x):
        x = x.reshape(-1, P, x.shape[1] if x.ndim > 1 else 1)
        return x.transpose(1, 0, 2).reshape(P, -1)

    row, col = _np.arange(P)[:, None], _np.arange(P)[None, :]
    param("ident", _np.eye(P, dtype=f32))
    param("ones", f32(1))
    param("mask_low", _np.where(col <= row, f32(0), f32(NEG)))
    param("mask_up", _np.where(col >= row, f32(0), f32(NEG)))
    param("up01", (row <= col).astype(f32))
    param("low01", (row >= col).astype(f32))
    param("iota", _np.arange(P, dtype=f32))
    param("comb", (_np.arange(P)[:, None] % 2 == _np.arange(2)[None, :]).astype(f32))
    param("rank", _np.arange(NE, 0, -1).astype(f32))
    param("eps", f32(EPS))
    param("cond", by_channel(_np.stack([a["c"][0], a["c_ctx"]], axis=1)))
    param("final_g", by_channel(a["final_norm_g"]))
    param("router", by_channel(a["moe_router"][0]))
    param("b_ada", by_channel(a["b_ada"].reshape(-1)))
    for l in range(DEPTH):
        param(f"norm1_{l}", by_channel(a["norm1_g"][l]))
        param(f"norm2_{l}", by_channel(a["norm2_g"][l]))
        param(f"conv_{l}", by_channel(a["conv_w"][l].T))
        param(f"mnorm_{l}", by_channel(a["mlstm_norm_g"][l]))
        param(f"bgates_{l}", a["b_gates"][l].reshape(-1))
        param(f"wgates_{l}", by_channel(a["w_in"][l][:, 3 * CONV + 1536:3 * CONV + 1552]))

    nc = _bacc.Bacc("TRN2", target_bir_lowering=False, num_devices=1)
    arrays = {"stream": stream, "tokens": _np.ascontiguousarray(tokens), "params": params}
    args = [nc.dram_tensor(name, x.shape, _mybir.dt.from_np(x.dtype), kind="ExternalInput").ap()
            for name, x in arrays.items()]
    out = nc.dram_tensor("out", (P, KT, SEQ), _mybir.dt.float32, kind="ExternalOutput").ap()
    backbone(nc, *args, out)
    r = _run(nc, [arrays], core_ids=[0])
    got = r.results[0]["out"]
    return _np.ascontiguousarray(got.transpose(2, 1, 0)).reshape(1, SEQ, D)
```
